# Optimizing a Trainium2 kernel written in Bass

```python
import jax, jax.numpy as jnp
from jax import lax
import numpy as np

D_MODEL = 1024
BATCH = 1
SEQ = 256
DEPTH = 2

CHUNK = 64
D_MIX = 1024
M_HEADS = 4
M_HEAD_DIM = 128
M_WIDTH = M_HEADS * M_HEAD_DIM
CONV_W = 4
G_GROUPS = 4
G_GROUP_CH = 128
G_WIDTH = G_GROUPS * G_GROUP_CH
G_BLOCK = 128
D_IN = 2 * M_WIDTH + 2 * G_WIDTH
D_FF = 2752
N_EXPERTS = 8
TOP_K = 2
D_FF_EXPERT = 3584
N_DENSE = (DEPTH + 1) // 2
N_MOE = DEPTH // 2
EPS = 1e-6

kernel_name = "hybrid_mlstm_gmlp_moe_trunk"

def rmsnorm(x, g):
    xf = x.astype(jnp.float32)
    y = xf * lax.rsqrt(jnp.mean(xf * xf, axis=-1, keepdims=True) + EPS)
    return (y * g.astype(jnp.float32)).astype(x.dtype)

def layernorm_f32(xf, g):
    mu = jnp.mean(xf, axis=-1, keepdims=True)
    var = jnp.mean(jnp.square(xf - mu), axis=-1, keepdims=True)
    return (xf - mu) * lax.rsqrt(var + EPS) * g.astype(jnp.float32)

def causal_depthwise_conv(x, w, b):
    y = lax.conv_general_dilated(
        x, w[:, None, :].astype(x.dtype), window_strides=(1,),
        padding=[(w.shape[0] - 1, 0)],
        dimension_numbers=("NWC", "WIO", "NWC"),
        feature_group_count=x.shape[-1])
    return y + b.astype(x.dtype)

def mlstm_chunkwise(q, k, v, ig, lf):
    B, S, H, dh = q.shape
    nc = S // CHUNK

    def to_chunks(a):
        a = a.reshape((B, nc, CHUNK, H) + a.shape[3:])
        return jnp.moveaxis(jnp.moveaxis(a, 1, 0), 3, 2)

    tril = jnp.tril(jnp.ones((CHUNK, CHUNK), dtype=bool))

    def step(carry, xs):
        C, n, m = carry
        qc, kc, vc, igc, lfc = xs
        b = jnp.cumsum(lfc, axis=-1)
        d = b[..., :, None] - b[..., None, :] + igc[..., None, :]
        d = jnp.where(tril, d, -jnp.inf)
        inter = b + m[..., None]
        m_t = jnp.maximum(inter, jnp.max(d, axis=-1))
        w = jnp.exp(d - m_t[..., None])
        a = jnp.exp(inter - m_t)
        s = jnp.einsum("bhtk,bhsk->bhts", qc, kc) * w
        num = (a[..., None] * jnp.einsum("bhvk,bhtk->bhtv", C, qc)
               + jnp.einsum("bhts,bhsv->bhtv", s, vc))
        den = a * jnp.einsum("bhk,bhtk->bht", n, qc) + jnp.sum(s, axis=-1)
        den = jnp.maximum(jnp.abs(den), jnp.exp(-m_t))
        h = num / den[..., None]
        b_end = b[..., -1]
        log_prev = b_end + m
        log_s = b_end[..., None] - b + igc
        m_new = jnp.maximum(log_prev, jnp.max(log_s, axis=-1))
        a_prev = jnp.exp(log_prev - m_new)
        w_s = jnp.exp(log_s - m_new[..., None])
        C_new = a_prev[..., None, None] * C + jnp.einsum("bhs,bhsv,bhsk->bhvk", w_s, vc, kc)
        n_new = a_prev[..., None] * n + jnp.einsum("bhs,bhsk->bhk", w_s, kc)
        return (C_new, n_new, m_new), h

    init = (jnp.zeros((B, H, dh, dh), jnp.float32),
            jnp.zeros((B, H, dh), jnp.float32),
            jnp.zeros((B, H), jnp.float32))
    xs = (to_chunks(q), to_chunks(k), to_chunks(v), to_chunks(ig), to_chunks(lf))
    _, hs = lax.scan(step, init, xs)
    return jnp.transpose(hs, (1, 0, 3, 2, 4)).reshape(B, S, H, dh)

def hybrid_mixer(h, w_in, conv_w, conv_b, w_q, w_k, w_v, w_if, b_if, skip_m,
                 mh_norm_g, gm_v_g, w_sp, b_sp, gm_out_g, w_out):
    B, S, _ = h.shape
    proj = h @ w_in.astype(h.dtype)
    x_m, o_pre, u, v = jnp.split(proj, [M_WIDTH, 2 * M_WIDTH, 2 * M_WIDTH + G_WIDTH], axis=-1)

    x_c = jax.nn.silu(causal_depthwise_conv(x_m, conv_w, conv_b))
    xc_h = x_c.reshape(B, S, M_HEADS, M_HEAD_DIM)
    xm_h = x_m.reshape(B, S, M_HEADS, M_HEAD_DIM)
    q = jnp.einsum("bshd,hde->bshe", xc_h, w_q.astype(h.dtype))
    k = jnp.einsum("bshd,hde->bshe", xc_h, w_k.astype(h.dtype))
    vm = jnp.einsum("bshd,hde->bshe", xm_h, w_v.astype(h.dtype))
    qkv = jnp.concatenate([q.reshape(B, S, -1), k.reshape(B, S, -1), vm.reshape(B, S, -1)], axis=-1)
    gates = (qkv @ w_if.astype(h.dtype) + b_if.astype(h.dtype)).astype(jnp.float32)
    ig = gates[..., :M_HEADS]
    lf = jax.nn.log_sigmoid(gates[..., M_HEADS:])
    hm = mlstm_chunkwise((q * (M_HEAD_DIM ** -0.5)).astype(jnp.float32),
                         k.astype(jnp.float32), vm.astype(jnp.float32), ig, lf)
    o = jax.nn.sigmoid(o_pre.astype(jnp.float32)).reshape(B, S, M_HEADS, M_HEAD_DIM)
    hm = o * hm
    mu = jnp.mean(hm, axis=-1, keepdims=True)
    var = jnp.mean(jnp.square(hm - mu), axis=-1, keepdims=True)
    hm = ((hm - mu) * lax.rsqrt(var + EPS)).reshape(B, S, M_WIDTH)
    y_m = (hm * mh_norm_g.astype(jnp.float32)
           + skip_m.astype(jnp.float32) * x_c.astype(jnp.float32)).astype(h.dtype)

    u = jax.nn.gelu(u)
    vg = layernorm_f32(jax.nn.gelu(v).astype(jnp.float32), gm_v_g)
    vb = vg.reshape(B, S // G_BLOCK, G_BLOCK, G_GROUPS, G_GROUP_CH)
    pos = jnp.arange(G_BLOCK)
    chunk_mask = (pos[:, None] // CHUNK) >= (pos[None, :] // CHUNK)
    ws = jnp.where(chunk_mask[None], w_sp.astype(jnp.float32), 0.0)
    sv = jnp.einsum("gij,bnjgc->bnigc", ws, vb) + b_sp.astype(jnp.float32).T[:, :, None]
    y_g = u.astype(jnp.float32) * sv.reshape(B, S, G_WIDTH)
    y_g = rmsnorm(y_g, gm_out_g).astype(h.dtype)

    y = jnp.concatenate([y_m, y_g], axis=-1)
    return y @ w_out.astype(h.dtype)

def swiglu(t, w1, w3, w2):
    return (jax.nn.silu(t @ w1.astype(t.dtype)) * (t @ w3.astype(t.dtype))) @ w2.astype(t.dtype)

def moe_ffn(h, w_router, w1, w3, w2):
    B, S, D = h.shape
    t = h.reshape(-1, D)
    logits = (t @ w_router.astype(t.dtype)).astype(jnp.float32)
    top_v, top_i = lax.top_k(logits, TOP_K)
    gate = jax.nn.softmax(top_v, axis=-1)
    combine = jnp.sum(jax.nn.one_hot(top_i, N_EXPERTS, dtype=jnp.float32) * gate[..., None], axis=1)
    out = jnp.zeros_like(t)
    for e in range(N_EXPERTS):
        out = out + combine[:, e:e + 1].astype(t.dtype) * swiglu(t, w1[e], w3[e], w2[e])
    return out.reshape(B, S, D)

def setup_inputs(seed: int = 0) -> dict:
    key = jax.random.key(seed)
    ks = jax.random.split(key, 32)
    f32 = jnp.float32

    def nrm(k, shape, scale):
        return jax.random.normal(k, shape, f32) * scale

    def gain(k, shape):
        return 1.0 + 0.02 * jax.random.normal(k, shape, f32)

    b_i = 0.1 * jax.random.normal(ks[9], (DEPTH, M_HEADS), f32)
    b_f = jnp.linspace(3.0, 6.0, M_HEADS, dtype=f32)[None, :] + 0.1 * jax.random.normal(ks[10], (DEPTH, M_HEADS), f32)
    return {
        "x": nrm(ks[0], (BATCH, SEQ, D_MODEL), 1.0),
        "mix_norm_g": gain(ks[1], (DEPTH, D_MODEL)),
        "w_in": nrm(ks[2], (DEPTH, D_MODEL, D_IN), D_MODEL ** -0.5),
        "conv_w": nrm(ks[3], (DEPTH, CONV_W, M_WIDTH), CONV_W ** -0.5),
        "conv_b": nrm(ks[4], (DEPTH, M_WIDTH), 0.02),
        "w_q": nrm(ks[5], (DEPTH, M_HEADS, M_HEAD_DIM, M_HEAD_DIM), M_HEAD_DIM ** -0.5),
        "w_k": nrm(ks[6], (DEPTH, M_HEADS, M_HEAD_DIM, M_HEAD_DIM), M_HEAD_DIM ** -0.5),
        "w_v": nrm(ks[7], (DEPTH, M_HEADS, M_HEAD_DIM, M_HEAD_DIM), M_HEAD_DIM ** -0.5),
        "w_if": nrm(ks[8], (DEPTH, 3 * M_WIDTH, 2 * M_HEADS), 0.5 * (3 * M_WIDTH) ** -0.5),
        "b_if": jnp.concatenate([b_i, b_f], axis=-1),
        "skip_m": gain(ks[11], (DEPTH, M_WIDTH)),
        "mh_norm_g": gain(ks[12], (DEPTH, M_WIDTH)),
        "gm_v_g": gain(ks[13], (DEPTH, G_WIDTH)),
        "w_sp": nrm(ks[14], (DEPTH, G_GROUPS, G_BLOCK, G_BLOCK), 0.5 * G_BLOCK ** -0.5),
        "b_sp": gain(ks[15], (DEPTH, G_GROUPS, G_BLOCK)),
        "gm_out_g": gain(ks[16], (DEPTH, G_WIDTH)),
        "w_out": nrm(ks[17], (DEPTH, D_MIX, D_MODEL), D_MIX ** -0.5),
        "ffn_norm_g": gain(ks[18], (DEPTH, D_MODEL)),
        "dense_w1": nrm(ks[19], (N_DENSE, D_MODEL, D_FF), D_MODEL ** -0.5),
        "dense_w3": nrm(ks[20], (N_DENSE, D_MODEL, D_FF), D_MODEL ** -0.5),
        "dense_w2": nrm(ks[21], (N_DENSE, D_FF, D_MODEL), D_FF ** -0.5),
        "moe_router": nrm(ks[22], (N_MOE, D_MODEL, N_EXPERTS), D_MODEL ** -0.5),
        "moe_w1": nrm(ks[23], (N_MOE, N_EXPERTS, D_MODEL, D_FF_EXPERT), D_MODEL ** -0.5),
        "moe_w3": nrm(ks[24], (N_MOE, N_EXPERTS, D_MODEL, D_FF_EXPERT), D_MODEL ** -0.5),
        "moe_w2": nrm(ks[25], (N_MOE, N_EXPERTS, D_FF_EXPERT, D_MODEL), D_FF_EXPERT ** -0.5),
        "final_norm_g": gain(ks[26], (D_MODEL,)),
    }

def reference(x, mix_norm_g, w_in, conv_w, conv_b, w_q, w_k, w_v, w_if, b_if, skip_m,
              mh_norm_g, gm_v_g, w_sp, b_sp, gm_out_g, w_out, ffn_norm_g,
              dense_w1, dense_w3, dense_w2, moe_router, moe_w1, moe_w3, moe_w2,
              final_norm_g):
    for l in range(DEPTH):
        h = rmsnorm(x, mix_norm_g[l])
        x = x + hybrid_mixer(h, w_in[l], conv_w[l], conv_b[l], w_q[l], w_k[l], w_v[l],
                             w_if[l], b_if[l], skip_m[l], mh_norm_g[l], gm_v_g[l],
                             w_sp[l], b_sp[l], gm_out_g[l], w_out[l])
        h = rmsnorm(x, ffn_norm_g[l])
        if l % 2 == 0:
            i = l // 2
            x = x + swiglu(h, dense_w1[i], dense_w3[i], dense_w2[i])
        else:
            i = l // 2
            x = x + moe_ffn(h, moe_router[i], moe_w1[i], moe_w3[i], moe_w2[i])
    return rmsnorm(x, final_norm_g)


_drawn_inputs = setup_inputs


def setup_inputs(seed=0):
    import zlib

    import numpy as np

    out = dict(_drawn_inputs(seed))
    spreads = {}
    factors = {'mh_norm_g': 3.185,
     'gm_v_g': 17.627,
     'final_norm_g': 22.057,
     'skip_m': 7.679,
     'b_sp': 22.17,
     'gm_out_g': 4.836,
     'ffn_norm_g': 3.366}
    for name, (base, spread) in spreads.items():
        noise = np.random.default_rng([zlib.crc32(name.encode()), seed]).standard_normal(out[name].shape)
        drawn = base * np.exp(spread * noise) if base else spread * noise
        out[name] = __import__('jax').numpy.asarray(drawn.astype(out[name].dtype))
    for name, factor in factors.items():
        out[name] = (out[name] * factor).astype(out[name].dtype)
    return out
```

```python
import concourse.bass as bass
from concourse import mybir
from contextlib import ExitStack

fp32 = mybir.dt.float32
i32 = mybir.dt.int32
u32 = mybir.dt.uint32
ALU = mybir.AluOpType
ACT = mybir.ActivationFunctionType
AX = mybir.AxisListType

P = 128
SEQ, D, L = 256, 1024, 2
NT = SEQ // P
KD = D // P
H, DH = 4, 128
MW = H * DH
CW = 4
CHUNK = 64
DFF, DFE, E = 2752, 3584, 8
EPS = 1e-6
SCALE = DH ** -0.5
UF = 256
ND = -(-DFF // UF)
NE = DFE // UF
SLOT = 64
PASS = 2 * SLOT
NJ = E * (SEQ // PASS)
R13, R2 = 7, 2
MIX = 6
W13_MOE = 2 * MIX + ND
W2_MOE = ND

WIN_ORDER = [0, 3, 2, 1]

ROWS = {}
_at = 0
for _name, _n in (("mix_norm_g", L * KD), ("ffn_norm_g", L * KD), ("conv_w", L * CW * H),
                  ("conv_b", L * H), ("skip_m", L * H), ("mh_norm_g", L * H),
                  ("gm_out_g", L * H), ("b_sp", L * H)):
    ROWS[_name] = (_at, _n)
    _at += _n
NROWS = _at


def dense_width(u):
    return min(UF, DFF - u * UF)


def trunk(nc, x, mix_norm_g, w_in, conv_w, conv_b, w_q, w_k, w_v, w_if, b_if, skip_m,
          mh_norm_g, gm_v_g, w_sp, b_sp, gm_out_g, w_out, ffn_norm_g,
          dense_w1, dense_w3, dense_w2, moe_router, moe_w1, moe_w3, moe_w2,
          final_norm_g, out):
    ctx = ExitStack()
    with ctx:
        def sb(name, shape, dt=fp32):
            return ctx.enter_context(nc.sbuf_tensor(name, shape, dt))

        def sem(name):
            return ctx.enter_context(nc.semaphore(name))

        w13 = [sb(f"w13_{i}", [P, KD, 2, UF]) for i in range(R13)]
        w13_wide = [w[:].rearrange("p k w f -> p k (w f)") for w in w13]
        w2 = [sb(f"w2_{i}", [P, 2, D]) for i in range(R2)]
        x_sb = sb("x_sb", [P, NT, D])
        xs = sb("xs", [P, NT, D])
        o_sb = xs[:, 0, :].rearrange("p (t c) -> p t c", t=NT)
        u_sb = xs[:, 1, :].rearrange("p (t c) -> p t c", t=NT)
        hT = sb("hT", [P, KD, SEQ])
        wS = hT[:].rearrange("p k s -> p (k s)")[:, 0:H * 384].rearrange("p (h s) -> p h s", h=H)
        wqkv = sb("wqkv", [P, 3, H, DH])
        wif = sb("wif", [P, 3 * H, 2 * H])
        bif = sb("bif", [H, L, 2])
        wsp = sb("wsp", [P, H, P])
        wspT = sb("wspT", [P, H, P])
        gvb = sb("gvb", [P, MW])
        fgb = hT[:].rearrange("p k s -> p (k s)")[:, 0:D]
        wr = sb("wr", [P, KD, E])
        prm = sb("prm", [NROWS, P])
        prmT = sb("prmT", [P, NROWS])
        ident = sb("ident", [P, P])
        sel = sb("sel", [H, H, P])
        before = sb("before", [P, P])
        ones_pp = sb("ones_pp", [P, P])
        neg_half = sb("neg_half", [P, NT * H])
        slot_no = sb("slot_no", [P, 2, 2, SLOT])
        expert_no = sb("expert_no", [P, NT, E])

        ss = sb("ss", [P, NT])
        var = sb("var", [P, NT])
        rstd = sb("rstd", [P, NT])

        ARENA = 9408
        arena = sb("arena", [P, ARENA])
        at = [0]

        def carve(n):
            at[0] += n
            assert at[0] <= ARENA, at[0]
            return arena[:, at[0] - n:at[0]]

        XP = SEQ + CW - 1
        yT = carve(KD * SEQ).rearrange("p (k s) -> p k s", k=KD)
        xmT = carve(H * XP).rearrange("p (h s) -> p h s", h=H)
        xcT = carve(H * SEQ).rearrange("p (h s) -> p h s", h=H)
        qT = carve(H * SEQ).rearrange("p (h s) -> p h s", h=H)
        kT = carve(H * SEQ).rearrange("p (h s) -> p h s", h=H)
        v_tok = carve(NT * H * (DH + 1)).rearrange("p (t h c) -> p t h c", t=NT, h=H)
        v_gate = carve(NT * MW).rearrange("p (t c) -> p t c", t=NT)
        vT_hm = carve(H * SEQ)
        vT = vT_hm.rearrange("p (h s) -> p h s", h=H)
        hm = vT_hm.rearrange("p (t c) -> p t c", t=NT)
        g_tok = carve(NT * 2 * H).rearrange("p (t c) -> p t c", t=NT)
        aT = carve(NT * H).rearrange("p (t h) -> p t h", t=NT)
        floorT = carve(H * NT).rearrange("p (h t) -> p h t", t=NT)
        den = carve(H * NT).rearrange("p (h t) -> p h t", t=NT)
        rden = carve(H * NT).rearrange("p (h t) -> p h t", t=NT)
        stats = carve(H * NT * 6).rearrange("p (h t c) -> p h t c", h=H, t=NT)
        mv = carve(H * NT * 2).rearrange("p (h t c) -> p h t c", h=H, t=NT)
        hvar = carve(H * NT)
        hrstd = carve(H * NT)
        gstats = carve(NT * 6).rearrange("p (t c) -> p t c", t=NT)
        gmv = carve(NT * 2).rearrange("p (t c) -> p t c", t=NT)
        gvar, grstd, yss, yvar, yrstd = (carve(NT) for _ in range(5))
        lf_min, gate_e, run_b, a_row, run_m, neg_m = (yT[0:H, i, :] for i in range(6))
        neg_stab = lf_min

        at[0] = 0
        d_sil = carve(2 * SEQ).rearrange("p (q s) -> p q s", q=2)
        d_g = carve(4 * SEQ).rearrange("p (q s) -> p q s", q=4)
        at[0] = 0
        onehot = carve(NT * 2 * 2 * SLOT).rearrange("p (t i c) -> p t i c", t=NT, i=2)
        onehotT = carve(2 * NT * P).rearrange("p (i t c) -> p i t c", t=NT, i=2)
        xselT = carve(KD * PASS).rearrange("p (k s) -> p k s", k=KD)
        m_sil = carve(2 * 2 * P).rearrange("p (q i f) -> p q i f", q=2, i=2)
        m_g = carve(2 * 2 * P).rearrange("p (q i f) -> p q i f", q=2, i=2)
        m_gT = carve(2 * 2 * P).rearrange("p (q i f) -> p q i f", q=2, i=2)
        y_sb = carve(2 * 512).rearrange("p (i c) -> p i c", i=2)
        logits, oh0, oh1, picked, rank, weight = (
            carve(NT * E).rearrange("p (t e) -> p t e", t=NT) for _ in range(6))
        top = carve(NT * 8).rearrange("p (t e) -> p t e", t=NT)
        top_fi = carve(NT * 8).rearrange("p (t e) -> p t e", t=NT)
        p1, p0, pden = (carve(NT) for _ in range(3))
        slot_of = carve(NJ * NT).rearrange("p (j t) -> p j t", t=NT)
        comb = carve(NJ * NT).rearrange("p (j t) -> p j t", t=NT)
        top_i = sb("top_i", [P, NT, 8], u32)
        cnt_f = sb("cnt_f", [1, NJ])
        cnt = sb("cnt", [1, NJ], i32)
        steps_f = sb("steps_f", [1, 2])
        steps = sb("steps", [1, 1], i32)

        def col(name, i):
            return prmT[:, ROWS[name][0] + i:ROWS[name][0] + i + 1]

        pb = ctx.enter_context(nc.psum_tensor("pb", [P, 8, 512], fp32))

        s_x = sem("x_loaded")
        s_prm = sem("params_loaded")
        s_wqkv = sem("wqkv_loaded")
        s_small = sem("small_loaded")
        s_wsp = sem("wsp_loaded")
        w13_rdy = [sem(f"w13_loaded_{i}") for i in range(R13)]
        w2_rdy = [sem(f"w2_loaded_{i}") for i in range(R2)]
        w2_used = sem("w2_used")
        s_const = sem("constants_made")
        s_prm_ps = sem("params_transposed")
        s_prmT = sem("params_in_sbuf")
        s_pad = sem("conv_pad_made")
        s_vone = sem("value_ones_made")
        sq_a = sem("squares_summed_act")
        var_r = sem("variance_ready")
        rstd_r = sem("rstd_ready")
        xs_a = sem("xs_ready_act")
        xs_d = sem("xs_ready_dve")
        hT_ps = sem("hT_in_psum")
        hT_d = sem("hT_ready_dve")
        hT_a = sem("hT_ready_act")
        x_upd = sem("x_updated")
        xm_ps = sem("xm_in_psum")
        xm_sb = sem("xm_ready")
        conv_r = sem("conv_ready")
        xc_r = sem("xc_ready")
        skip_r = sem("skip_ready")
        tok_ps = sem("tokenwise_proj_in_psum")
        gelu_r = sem("gelu_ready")
        o_r = sem("o_ready")
        qkv_ps = sem("qkv_in_psum")
        qk_r = sem("qk_ready")
        vT_r = sem("vT_ready")
        vt_r = sem("v_tok_ready")
        gate_ps = sem("gates_in_psum")
        gate_r = sem("gates_ready")
        gateT_ps = sem("gate_rows_in_psum")
        absf_r = sem("abs_forget_ready")
        ln_r = sem("softplus_ready")
        row_r = sem("gate_rows_ready")
        mb_ps = sem("running_max_broadcast")
        aT_ps = sem("a_columns_in_psum")
        aT_r = sem("a_columns_ready")
        floor_r = sem("floor_ready")
        arg_r = sem("weight_exponent_ready")
        wexp_r = sem("weights_exponentiated")
        wmask_r = sem("weights_masked")
        sc_ps = sem("scores_in_psum")
        sT_r = sem("weighted_scores_ready")
        num_ps = sem("numerators_in_psum")
        hvar_r = sem("head_variance_ready")
        hrstd_r = sem("head_rstd_ready")
        hm_r = sem("head_output_ready")
        hmT_ps = sem("head_output_transposed")
        wspT_ps = sem("wsp_transposed")
        wspT_r = sem("wspT_ready")
        gvar_r = sem("v_variance_ready")
        grstd_r = sem("v_rstd_ready")
        vn_r = sem("v_normalised")
        vg_r = sem("v_scaled")
        sv_ps = sem("gating_in_psum")
        yg_r = sem("gated_ready")
        yss_r = sem("gated_squares_summed")
        yvar_r = sem("gated_variance_ready")
        yrstd_r = sem("gated_rstd_ready")
        ygs_r = sem("gated_normalised")
        ygT_ps = sem("gated_transposed")
        ygT_r = sem("gated_channels_ready")
        ymT_r = sem("head_channels_ready")
        wo_ps = sem("mixer_output_in_psum")
        up_ps = sem("dense_up_in_psum")
        sil_r = sem("dense_silu_ready")
        g_r = sem("dense_product_ready")
        down_ps = sem("dense_down_in_psum")
        lg_ps = sem("logits_in_psum")
        pick_r = sem("picked_ready")
        rank_ps = sem("ranks_in_psum")
        route_r = sem("routing_ready")
        oh_r = sem("onehot_ready")
        gx_ps = sem("gathered_in_psum")
        ohT_ps = sem("onehot_transposed")
        ohT_r = sem("onehotT_ready")
        xsel_r = sem("gathered_ready")
        eup_ps = sem("expert_up_in_psum")
        esil_r = sem("expert_silu_ready")
        eg_r = sem("expert_product_ready")
        egT_ps = sem("expert_product_transposed")
        egT_r = sem("expert_productT_ready")
        y_a = sem("expert_output_ready_act")
        y_d = sem("expert_output_ready_dve")
        sct_ps = sem("scattered_in_psum")
        x_moe = sem("x_updated_by_expert")
        gap_r = sem("logit_gap_ready")
        gexp_r = sem("gate_exponential_ready")
        s_dve_done = sem("experts_done")
        fin_r = sem("final_ready")
        s_fgb = sem("final_gain_loaded")
        s_out = sem("output_stored")
        dve_chain = sem("dve_chain")
        act_chain = sem("act_chain")
        pool_chain = sem("pool_chain")

        block = ctx.enter_context(nc.Block())

        def w13_item(l, i):
            return l * (MIX + ND) + i

        @block.sync
        def _(sp):
            def used(n):
                l, i = n // (MIX + ND), n % (MIX + ND)
                if i == 0:
                    sp.wait_ge(xm_ps, 2 * (l + 1))
                elif i < 4:
                    sp.wait_ge(tok_ps, 6 * l + 2 * i)
                elif i < MIX:
                    sp.wait_ge(wo_ps, 4 * l + 2 * (i - 3))
                else:
                    sp.wait_ge(up_ps, 2 * (i - MIX + 1))

            def ring_slot(n):
                if n >= R13:
                    used(n - R13)
                return n % R13

            def load_w_in(l, i):
                n = ring_slot(w13_item(l, i))
                c = WIN_ORDER[i] * MW
                sp.dma_start(w13_wide[n], w_in[l, :, c:c + MW].rearrange("(k p) f -> p k f", p=P)
                             ).then_inc(w13_rdy[n], 32)

            def load_w_out(l, i):
                n = ring_slot(w13_item(l, 4 + i))
                sp.dma_start(w13_wide[n], w_out[l, :, i * 512:(i + 1) * 512]
                             .rearrange("(k p) f -> p k f", p=P)).then_inc(w13_rdy[n], 32)

            sp.dma_start(x_sb[:], x[0].rearrange("(t p) d -> p t d", p=P)).then_inc(s_x, 16)
            for name, ap, w in (("mix_norm_g", mix_norm_g, KD), ("ffn_norm_g", ffn_norm_g, KD),
                                ("conv_b", conv_b, H), ("skip_m", skip_m, H),
                                ("mh_norm_g", mh_norm_g, H), ("gm_out_g", gm_out_g, H)):
                r, n = ROWS[name]
                sp.dma_start(prm[r:r + n, :], ap.rearrange("l (k p) -> (l k) p", p=P)).then_inc(s_prm, 16)
            r, n = ROWS["conv_w"]
            sp.dma_start(prm[r:r + n, :], conv_w.rearrange("l j (k p) -> (l j k) p", p=P)).then_inc(s_prm, 16)
            r, n = ROWS["b_sp"]
            sp.dma_start(prm[r:r + n, :], b_sp.rearrange("l g i -> (l g) i")).then_inc(s_prm, 16)
            for i in range(4):
                load_w_in(0, i)

            def load_mixer_params(l):
                if l:
                    sp.wait_ge(gate_ps, l)
                    sp.wait_ge(wspT_ps, l)
                    sp.wait_ge(vg_r, 2 * l)
                for i, w in enumerate((w_q, w_k, w_v)):
                    sp.dma_start(wqkv[:, i], w[l].rearrange("h d e -> d h e")).then_inc(s_wqkv, 16)
                sp.dma_start(wif[:], w_if[l].rearrange("(c p) g -> p c g", p=P)).then_inc(s_small, 16)
                sp.dma_start(gvb[:], gm_v_g[l:l + 1, :].to_broadcast((P, MW))).then_inc(s_small, 16)
                sp.dma_start(wsp[:], w_sp[l].rearrange("g i j -> i g j")).then_inc(s_wsp, 16)
                if l == 0:
                    sp.dma_start(bif[:], b_if.rearrange("l (a h) -> h l a", h=H),
                                 allow_slow_non_contiguous=True).then_inc(s_small, 16)
                    sp.dma_start(wr[:], moe_router[0].rearrange("(k p) e -> p k e", p=P)).then_inc(s_small, 16)

            load_mixer_params(0)
            for i in range(2):
                load_w_out(0, i)
            for u in range(ND):
                n = ring_slot(w13_item(0, MIX + u))
                wd = dense_width(u)
                for k, w in enumerate((dense_w1, dense_w3)):
                    sp.dma_start(w13[n][:, :, k, 0:wd], w[0, :, u * UF:u * UF + wd]
                                 .rearrange("(k p) f -> p k f", p=P)).then_inc(w13_rdy[n], 16)
            load_mixer_params(1)
            for i in range(4):
                load_w_in(1, i)
            for i in range(2):
                load_w_out(1, i)

            def load_expert(j, e):
                for u in range(NE):
                    n = (W13_MOE + u) % R13
                    if isinstance(j, int) and j == 0 and u < R13:
                        used(W13_MOE + u - R13)
                    else:
                        sp.wait_ge(eup_ps, j * (2 * NE) + 2 * (u - R13 + 1))
                    for k, w in enumerate((moe_w1, moe_w3)):
                        sp.dma_start(w13[n][:, :, k, :], w[0, bass.ds(e, 1), :, u * UF:(u + 1) * UF]
                                     .rearrange("a (k p) f -> p (a k) f", p=P)).then_inc(w13_rdy[n], 16)

            load_expert(0, 0)
            with sp.Fori(1, E) as e:
                load_expert(e, e)
            sp.wait_ge(lg_ps, 1)
            sp.dma_start(fgb, final_norm_g.rearrange("(a d) -> a d", a=1).to_broadcast((P, D))
                         ).then_inc(s_fgb, 16)
            sp.wait_ge(route_r, 1)
            n_steps = sp.value_load(steps[0:1, 0:1], min_val=E, max_val=NJ)
            with sp.If(n_steps > E):
                with sp.Fori(0, E) as e:
                    load_expert(e + E, e)
            with sp.Else():
                sp.nop()
            sp.wait_ge(fin_r, NT)
            sp.dma_start(out[0].rearrange("(t p) d -> p t d", p=P), x_sb[:]).then_inc(s_out, 16)
            sp.wait_ge(s_out, 16)

        @block.gpsimd
        def _(pool):
            links = [0]

            def link(ins):
                links[0] += 1
                ins.then_inc(pool_chain, 1)
                pool.wait_ge(pool_chain, links[0])

            nc.gpsimd.memset(ident[:], 0.0)
            nc.gpsimd.memset(ones_pp[:], 1.0)
            nc.gpsimd.memset(neg_half[:], -0.5)
            link(nc.gpsimd.memset(sel[:], 0.0))
            nc.gpsimd.affine_select(out=ident[:], in_=ident[:], compare_op=ALU.not_equal, fill=1.0,
                                    base=0, pattern=[[-1, P]], channel_multiplier=1)
            nc.gpsimd.affine_select(out=before[:], in_=ones_pp[:], compare_op=ALU.is_gt, fill=0.0,
                                    base=0, pattern=[[1, P]], channel_multiplier=-1)
            nc.gpsimd.affine_select(out=sel[:], in_=sel[:], compare_op=ALU.not_equal, fill=1.0,
                                    base=0, pattern=[[-1, H], [0, P]], channel_multiplier=1)
            nc.gpsimd.iota(slot_no[:], pattern=[[SLOT, 2], [0, 2], [1, SLOT]], base=0,
                           channel_multiplier=0, allow_small_or_imprecise_dtypes=True)
            nc.gpsimd.iota(expert_no[:], pattern=[[0, NT], [1, E]], base=0,
                           channel_multiplier=0, allow_small_or_imprecise_dtypes=True
                           ).then_inc(s_const, 1)

            def rsqrt(n):
                pool.wait_ge(var_r, n + 1)
                nc.gpsimd.tensor_tensor(rstd[:], var[:], neg_half[:, 0:NT], ALU.pow).then_inc(rstd_r, 1)

            def mixer(l):
                rsqrt(2 * l)
                pool.wait_ge(gvar_r, l + 1)
                nc.gpsimd.tensor_tensor(grstd, gvar, neg_half[:, 0:NT], ALU.pow).then_inc(grstd_r, 1)
                pool.wait_ge(s_small, 64 + 32 * l)
                for t in range(NT):
                    pool.wait_ge(vn_r, NT * l + t + 1)
                    nc.gpsimd.tensor_tensor(v_gate[:, t, :], v_gate[:, t, :], gvb[:], ALU.mult
                                            ).then_inc(vg_r, 1)
                pool.wait_ge(qkv_ps, 8 * l + 4)
                for h in range(H):
                    ins = nc.gpsimd.tensor_scalar(xcT[:, h, :], xcT[:, h, :], col("skip_m", l * H + h),
                                                  None, ALU.mult)
                ins.then_inc(skip_r, 1)
                pool.wait_ge(yvar_r, l + 1)
                nc.gpsimd.tensor_tensor(yrstd, yvar, neg_half[:, 0:NT], ALU.pow).then_inc(yrstd_r, 1)
                pool.wait_ge(wexp_r, 2 * (l + 1))
                for b in range(2):
                    d = wS[:, :, 256 * b:256 * b + P]
                    nc.gpsimd.affine_select(out=d, in_=d, compare_op=ALU.is_ge, fill=0.0, base=0,
                                            pattern=[[0, H], [1, P]], channel_multiplier=-1
                                            ).then_inc(wmask_r, 1)
                pool.wait_ge(hvar_r, l + 1)
                nc.gpsimd.tensor_tensor(hrstd, hvar, neg_half[:, 0:NT * H], ALU.pow).then_inc(hrstd_r, 1)

            mixer(0)
            rsqrt(1)
            for u in range(ND):
                if u >= R2:
                    pool.wait_ge(w2_used, u - R2 + 1)
                for b in range(2):
                    rows_b = min(P, DFF - u * UF - b * P)
                    if rows_b > 0:
                        f = u * UF + b * P
                        pool.dma_start(w2[u % R2][0:rows_b, b, :], dense_w2[0, f:f + rows_b, :]
                                       ).then_inc(w2_rdy[u % R2], 16)
            mixer(1)
            rsqrt(3)

            def load_expert(j, e):
                for u in range(NE):
                    n = (W2_MOE + u) % R2
                    pool.wait_ge(w2_used, j * NE + (W2_MOE - 1 + u - R2 + 1))
                    pool.dma_start(w2[n][:], moe_w2[0, bass.ds(e, 1), u * UF:(u + 1) * UF, :]
                                   .rearrange("a (b p) d -> p (a b) d", p=P)).then_inc(w2_rdy[n], 32)

            pool.wait_ge(down_ps, 4)
            with pool.Fori(0, E) as e:
                load_expert(e, e)
            pool.wait_ge(route_r, 1)
            n_steps = pool.value_load(steps[0:1, 0:1], min_val=E, max_val=NJ)
            with pool.If(n_steps > E):
                with pool.Fori(0, E) as e:
                    load_expert(e + E, e)
            with pool.Else():
                pool.nop()
            pool.wait_ge(var_r, 5)
            nc.gpsimd.tensor_tensor(rstd[:], var[:], neg_half[:, 0:NT], ALU.pow).then_inc(rstd_r, 1)

        @block.scalar
        def _(act):
            links = [0]

            def link(ins):
                links[0] += 1
                ins.then_inc(act_chain, 1)
                act.wait_ge(act_chain, links[0])

            def norm(n):
                if n == 0:
                    act.wait_ge(s_x, 16)
                else:
                    act.wait_ge(x_upd, 4 * n)
                link(nc.scalar.activation(xs[:, 0, :], x_sb[:, 0, :], ACT.Square, accum_out=ss[:, 0:1]))
                nc.scalar.activation(ss[:, 0:1], ss[:, 0:1], ACT.Copy).then_inc(sq_a, 1)
                act.wait_ge(rstd_r, n + 1)
                nc.scalar.activation(xs[:, 0, :], x_sb[:, 0, :], ACT.Copy, scale=rstd[:, 0:1]).then_inc(xs_a, 1)
                if n == 0:
                    act.wait_ge(s_prmT, 1)
                g, l = ("ffn_norm_g", "mix_norm_g")[n % 2 == 0], n // 2
                for i in (1, 3):
                    act.wait_ge(hT_ps, 4 * n + i + 1)
                    for k in (2 * i, 2 * i + 1):
                        nc.scalar.activation(hT[:, k, :], pb[:, i, 256 * (k % 2):256 * (k % 2) + 256], ACT.Copy,
                                             scale=col(g, l * KD + k)).then_inc(hT_a, 1)

            def mixer(l):
                norm(2 * l)
                for i in range(2):
                    act.wait_ge(xm_ps, 2 * l + i + 1)
                    nc.scalar.activation(xmT[:, 2 * i:2 * i + 2, CW - 1:], pb[:, 4 + i, :]
                                         .rearrange("p (h s) -> p h s", h=2), ACT.Copy).then_inc(xm_sb, 1)
                for h in range(H):
                    act.wait_ge(conv_r, H * l + h + 1)
                    nc.scalar.activation(xcT[:, h, :], xcT[:, h, :], ACT.Silu).then_inc(xc_r, 1)
                for i in range(2 * NT):
                    act.wait_ge(tok_ps, 6 * l + i + 1)
                    dst = (v_gate, u_sb)[i // NT]
                    nc.scalar.activation(dst[:, i % NT, :], pb[:, (6, 7, 0, 1)[i], :], ACT.Gelu_apprx_tanh
                                         ).then_inc(gelu_r, 1)
                for t in range(NT):
                    act.wait_ge(tok_ps, 6 * l + 4 + t + 1)
                    nc.scalar.activation(o_sb[:, t, :], pb[:, 2 + t, :], ACT.Sigmoid).then_inc(o_r, 1)
                for i in range(2):
                    act.wait_ge(qkv_ps, 8 * l + 4 + i + 1)
                    nc.scalar.activation(vT[:, 2 * i:2 * i + 2, :], pb[:, i, :]
                                         .rearrange("p (h s) -> p h s", h=2), ACT.Copy).then_inc(vT_r, 1)
                act.wait_ge(absf_r, l + 1)
                link(nc.scalar.activation(gate_e, gate_e, ACT.Exp, scale=-1.0))
                nc.scalar.activation(gate_e, gate_e, ACT.Ln, bias=1.0).then_inc(ln_r, 1)
                for t in range(NT):
                    act.wait_ge(yg_r, NT * l + t + 1)
                    link(nc.scalar.activation(u_sb[:, t, :], v_gate[:, t, :], ACT.Square,
                                              accum_out=yss[:, t:t + 1]))
                nc.scalar.activation(yss, yss, ACT.Copy).then_inc(yss_r, 1)
                act.wait_ge(yrstd_r, l + 1)
                for t in range(NT):
                    nc.scalar.activation(v_gate[:, t, :], v_gate[:, t, :], ACT.Copy,
                                         scale=yrstd[:, t:t + 1]).then_inc(ygs_r, 1)
                act.wait_ge(aT_ps, l + 1)
                nc.scalar.activation(floorT.rearrange("p h t -> p t h"), pb[:, 5, 64:64 + NT * H]
                                     .rearrange("p (t h) -> p t h", t=NT), ACT.Exp).then_inc(floor_r, 1)
                for i in range(2):
                    act.wait_ge(arg_r, 2 * l + i + 1)
                    nc.scalar.activation(wS[:, 2 * i:2 * i + 2, :], wS[:, 2 * i:2 * i + 2, :], ACT.Exp
                                         ).then_inc(wexp_r, 1)
                for i in range(2):
                    act.wait_ge(ygT_ps, 2 * l + i + 1)
                    for g in range(2):
                        nc.scalar.activation(yT[:, H + 2 * i + g, :], pb[:, 2 + i, 256 * g:256 * g + 256],
                                             ACT.Copy, scale=col("gm_out_g", l * H + 2 * i + g)
                                             ).then_inc(ygT_r, 1)

            mixer(0)
            norm(1)
            for q in range(2 * ND):
                act.wait_ge(up_ps, q + 1)
                if q >= 2:
                    act.wait_ge(g_r, q - 1)
                r = min(P, DFF - q * P)
                nc.scalar.activation(d_sil[0:r, q % 2, :], pb[0:r, q % 4, 0:SEQ], ACT.Silu).then_inc(sil_r, 1)
            mixer(1)
            norm(3)

            act.wait_ge(gap_r, 1)
            nc.scalar.activation(p1, p1, ACT.Exp).then_inc(gexp_r, 1)
            act.wait_ge(route_r, 1)
            n_steps = act.value_load(steps[0:1, 0:1], min_val=E, max_val=NJ)
            with act.Fori(0, n_steps) as j:
                n_tok = act.value_load(cnt[0:1, bass.ds(j, 1)], min_val=-SEQ, max_val=SEQ)
                act.wait_ge(ohT_ps, j + 1)
                nc.scalar.activation(onehotT, pb[:, 7, :].rearrange("p (i t c) -> p i t c", i=2, t=NT),
                                     ACT.Copy).then_inc(ohT_r, 1)

                def units(tiles):
                    for u in range(NE):
                        for i in range(tiles):
                            act.wait_ge(eup_ps, j * (2 * NE) + (2 * u + (i + 1 if tiles == 2 else 2)))
                            if u >= 2:
                                act.wait_ge(eg_r, j * (2 * NE) + 2 * (u - 1))
                            nc.scalar.activation(m_sil[:, u % 2, i, :], pb[:, 2 * i + u % 2, 0:P],
                                                 ACT.Silu).then_inc(esil_r, 3 - tiles)
                        if u:
                            transposed(tiles, u - 1)
                    transposed(tiles, NE - 1)
                    act.wait_ge(w2_used, ND - 1 + (j + 1) * NE)
                    nc.scalar.activation(y_sb[:, 0, :], pb[:, 4, :], ACT.Copy).then_inc(y_a, 1)

                def transposed(tiles, u):
                    act.wait_ge(egT_ps, j * NE + (u + 1))
                    nc.scalar.activation(m_gT[:, u % 2, 0:tiles, :], pb[:, 6, 0:tiles * P]
                                         .rearrange("p (i f) -> p i f", i=tiles), ACT.Copy).then_inc(egT_r, 1)

                with act.If(n_tok > SLOT):
                    units(2)
                with act.Else():
                    units(1)
            act.wait_ge(s_dve_done, 1)
            link(nc.scalar.activation(xs[:, 0, :], x_sb[:, 0, :], ACT.Square, accum_out=ss[:, 0:1]))
            nc.scalar.activation(ss[:, 0:1], ss[:, 0:1], ACT.Copy).then_inc(sq_a, 1)

        @block.vector
        def _(dve):
            links = [0]

            def link(ins):
                links[0] += 1
                ins.then_inc(dve_chain, 1)
                dve.wait_ge(dve_chain, links[0])

            V = nc.vector

            def variance(n):
                link(V.tensor_tensor_reduce(out=xs[:, 1, :], in0=x_sb[:, 1, :], in1=x_sb[:, 1, :],
                                            scale=1.0, scalar=0.0, op0=ALU.mult, op1=ALU.add,
                                            accum_out=ss[:, 1:2]))
                dve.wait_ge(sq_a, n + 1)
                V.tensor_scalar(var[:], ss[:], 1.0 / D, EPS, ALU.mult, ALU.add).then_inc(var_r, 1)

            def norm(n):
                if n == 0:
                    dve.wait_ge(s_x, 16)
                variance(n)
                dve.wait_ge(rstd_r, n + 1)
                V.tensor_scalar(xs[:, 1, :], x_sb[:, 1, :], rstd[:, 1:2], None, ALU.mult).then_inc(xs_d, 1)
                if n == 0:
                    dve.wait_ge(s_prm_ps, 1)
                    V.tensor_copy(prmT[:], pb[:, 7, 0:NROWS]).then_inc(s_prmT, 1)
                    dve.wait_ge(s_prmT, 1)
                g, l = ("ffn_norm_g", "mix_norm_g")[n % 2 == 0], n // 2
                for i in (0, 2):
                    dve.wait_ge(hT_ps, 4 * n + i + 1)
                    for k in (2 * i, 2 * i + 1):
                        V.tensor_scalar(hT[:, k, :], pb[:, i, 256 * (k % 2):256 * (k % 2) + 256],
                                        col(g, l * KD + k), None, ALU.mult).then_inc(hT_d, 1)

            def mixer(l):
                norm(2 * l)
                V.memset(xmT[:, :, 0:CW - 1], 0.0).then_inc(s_pad, 1)
                V.memset(v_tok[:, :, :, DH:DH + 1], 1.0).then_inc(s_vone, 1)
                dve.wait_ge(wspT_ps, l + 1)
                link(V.tensor_copy(wspT[:], pb[:, 6, :].rearrange("p (g i) -> p g i", g=H)))
                V.memset(wspT[CHUNK:P, :, 0:CHUNK], 0.0).then_inc(wspT_r, 1)
                dve.wait_ge(s_pad, l + 1)
                for h in range(H):
                    dve.wait_ge(xm_sb, 2 * l + h // 2 + 1)
                    tap = lambda j: col("conv_w", (l * CW + j) * H + h)
                    link(V.tensor_scalar(xcT[:, h, :], xmT[:, h, 0:SEQ], tap(0), col("conv_b", l * H + h),
                                         ALU.mult, ALU.add))
                    for j in range(1, CW):
                        ins = V.scalar_tensor_tensor(out=xcT[:, h, :], in0=xmT[:, h, j:j + SEQ],
                                                     scalar=tap(j), in1=xcT[:, h, :],
                                                     op0=ALU.mult, op1=ALU.add)
                        if j < CW - 1:
                            link(ins)
                    ins.then_inc(conv_r, 1)
                for t in range(NT):
                    dve.wait_ge(gelu_r, 4 * l + t + 1)
                    link(V.bn_stats(gstats[:, t, :], v_gate[:, t, :]))
                    link(V.bn_aggr(gmv[:, t, :], gstats[:, t, :]))
                V.tensor_scalar(gvar, gmv[:, :, 1], EPS, None, ALU.add).then_inc(gvar_r, 1)
                dve.wait_ge(grstd_r, l + 1)
                for t in range(NT):
                    V.tensor_scalar(v_gate[:, t, :], v_gate[:, t, :], gmv[:, t, 0:1], grstd[:, t:t + 1],
                                    ALU.subtract, ALU.mult).then_inc(vn_r, 1)
                for i in range(4):
                    dve.wait_ge(qkv_ps, 8 * l + i + 1)
                    V.tensor_copy((qT, kT)[i // 2][:, 2 * (i % 2):2 * (i % 2) + 2, :], pb[:, 4 + i, :]
                                  .rearrange("p (h s) -> p h s", h=2)).then_inc(qk_r, 1)
                dve.wait_ge(s_vone, l + 1)
                for t in range(NT):
                    dve.wait_ge(qkv_ps, 8 * l + 6 + t + 1)
                    V.tensor_copy(v_tok[:, t, :, 0:DH], pb[:, 2 + t, :].rearrange("p (h c) -> p h c", h=H)
                                  ).then_inc(vt_r, 1)
                dve.wait_ge(gate_ps, l + 1)
                V.tensor_copy(g_tok, pb[:, 4, 0:NT * 2 * H].rearrange("p (t c) -> p t c", t=NT)
                              ).then_inc(gate_r, 1)
                dve.wait_ge(gateT_ps, l + 1)
                bi, bf = bif[:, l, 0:1], bif[:, l, 1:2]
                link(V.tensor_scalar(run_b, pb[0:H, 5, 256:512], bf, None, ALU.add))
                V.scalar_tensor_tensor(out=gate_e, in0=run_b, scalar=-1.0, in1=run_b,
                                       op0=ALU.mult, op1=ALU.max).then_inc(absf_r, 1)
                link(V.tensor_scalar(lf_min, run_b, 0.0, None, ALU.min))
                dve.wait_ge(ln_r, l + 1)
                link(V.tensor_tensor(gate_e, lf_min, gate_e, ALU.subtract))
                link(V.tensor_tensor_scan(run_b, ones_pp[0:H, 0:1].to_broadcast((H, SEQ)), gate_e, 0.0, ALU.mult, ALU.add))
                link(V.scalar_tensor_tensor(out=a_row, in0=pb[0:H, 5, 0:256], scalar=bi, in1=run_b,
                                            op0=ALU.add, op1=ALU.subtract))
                link(V.tensor_tensor_scan(run_m, a_row, a_row, 0.0, ALU.max, ALU.max))
                V.tensor_scalar(neg_m, run_m, -1.0, None, ALU.mult)
                V.scalar_tensor_tensor(out=neg_stab, in0=run_b, scalar=-1.0, in1=run_m,
                                       op0=ALU.mult, op1=ALU.subtract).then_inc(row_r, 1)
                for t in range(NT):
                    dve.wait_ge(sv_ps, NT * l + t + 1)
                    dve.wait_ge(gelu_r, 4 * l + 4)
                    for g in range(H):
                        c = slice(g * P, (g + 1) * P)
                        ins = V.scalar_tensor_tensor(out=v_gate[:, t, c], in0=pb[:, 6 + t, c],
                                                     scalar=col("b_sp", l * H + g), in1=u_sb[:, t, c],
                                                     op0=ALU.add, op1=ALU.mult)
                    ins.then_inc(yg_r, 1)
                dve.wait_ge(aT_ps, l + 1)
                link(V.tensor_copy(aT, pb[:, 4, 32:32 + NT * H].rearrange("p (t h) -> p t h", t=NT)))
                for i in range(2):
                    dve.wait_ge(mb_ps, 2 * l + i + 1)
                    for h in (2 * i, 2 * i + 1):
                        m = pb[:, 6 + i, 256 * (h % 2):256 * (h % 2) + 256]
                        V.tensor_scalar(wS[:, h, 0:256], m, aT[:, 0, h:h + 1], 0.0, ALU.add, ALU.min)
                        ins = V.tensor_scalar(wS[:, h, 256:384], m[:, P:], aT[:, 1, h:h + 1], 0.0,
                                              ALU.add, ALU.min)
                    ins.then_inc(arg_r, 1)
                dve.wait_ge(yss_r, l + 1)
                V.tensor_scalar(yvar, yss, 1.0 / MW, EPS, ALU.mult, ALU.add).then_inc(yvar_r, 1)
                dve.wait_ge(wmask_r, 2 * (l + 1))
                for h in range(H):
                    dve.wait_ge(sc_ps, H * l + h + 1)
                    V.scalar_tensor_tensor(out=wS[:, h, :], in0=pb[:, h, 0:384], scalar=SCALE,
                                           in1=wS[:, h, :], op0=ALU.mult, op1=ALU.mult).then_inc(sT_r, 1)
                dve.wait_ge(num_ps, H * (l + 1))
                dve.wait_ge(floor_r, l + 1)
                nums = pb[:, 4:8, :].rearrange("p h (t c) -> p h t c", t=NT)
                link(V.tensor_copy(rden, nums[:, :, :, DH]))
                link(V.scalar_tensor_tensor(out=den, in0=rden, scalar=-1.0, in1=rden,
                                            op0=ALU.mult, op1=ALU.max))
                link(V.tensor_tensor(den, den, floorT, ALU.max))
                link(V.reciprocal(rden, den))
                dve.wait_ge(o_r, NT * (l + 1))
                for h in range(H):
                    for t in range(NT):
                        link(V.scalar_tensor_tensor(out=hm[:, t, h * DH:(h + 1) * DH],
                                                    in0=nums[:, h, t, 0:DH], scalar=rden[:, h, t:t + 1],
                                                    in1=o_sb[:, t, h * DH:(h + 1) * DH],
                                                    op0=ALU.mult, op1=ALU.mult))
                        link(V.bn_stats(stats[:, h, t, :], hm[:, t, h * DH:(h + 1) * DH]))
                        link(V.bn_aggr(mv[:, h, t, :], stats[:, h, t, :]))
                V.tensor_scalar(hvar, mv.rearrange("p h t c -> p (h t) c")[:, :, 1], EPS, None, ALU.add
                                ).then_inc(hvar_r, 1)
                dve.wait_ge(hrstd_r, l + 1)
                for h in range(H):
                    for t in range(NT):
                        c = slice(h * DH, (h + 1) * DH)
                        ins = V.tensor_scalar(hm[:, t, c], hm[:, t, c], mv[:, h, t, 0:1],
                                              hrstd[:, h * NT + t:h * NT + t + 1], ALU.subtract, ALU.mult)
                    ins.then_inc(hm_r, 1)
                dve.wait_ge(skip_r, l + 1)
                for h in range(H):
                    dve.wait_ge(hmT_ps, 2 * l + h // 2 + 1)
                    V.scalar_tensor_tensor(out=yT[:, h, :], in0=pb[:, h // 2, 256 * (h % 2):256 * (h % 2) + 256],
                                           scalar=col("mh_norm_g", l * H + h), in1=xcT[:, h, :],
                                           op0=ALU.mult, op1=ALU.add).then_inc(ymT_r, 1)
                residual(wo_ps, 4 * l, n=2 * l + 1)

            def residual(ready, base, n):
                for i in range(4):
                    half, t = i // 2, i % 2
                    dve.wait_ge(ready, base + i + 1)
                    c = slice(half * 512, half * 512 + 512)
                    ins = V.tensor_tensor(x_sb[:, t, c], x_sb[:, t, c], pb[:, 4 + i, :], ALU.add)
                    ins.then_inc(x_upd, 1)
                dve.wait_ge(x_upd, 4 * n)

            mixer(0)
            norm(1)
            for q in range(2 * ND):
                dve.wait_ge(sil_r, q + 1)
                r = min(P, DFF - q * P)
                V.tensor_tensor(d_g[0:r, q % 4, :], d_sil[0:r, q % 2, :], pb[0:r, q % 4, SEQ:2 * SEQ],
                                ALU.mult).then_inc(g_r, 1)
            residual(down_ps, 0, 2)
            mixer(1)
            norm(3)

            dve.wait_ge(lg_ps, 1)
            link(V.tensor_copy(logits, pb[:, 4, 0:NT * E].rearrange("p (t e) -> p t e", t=NT)))
            for t in range(NT):
                link(V.max(top[:, t, :], logits[:, t, :]))
                link(V.max_index(top_i[:, t, :], top[:, t, :], logits[:, t, :]))
            link(V.tensor_copy(top_fi, top_i[:]))
            for t in range(NT):
                V.tensor_scalar(oh0[:, t, :], expert_no[:, t, :], top_fi[:, t, 0:1], None, ALU.is_equal)
                link(V.tensor_scalar(oh1[:, t, :], expert_no[:, t, :], top_fi[:, t, 1:2], None, ALU.is_equal))
            V.tensor_tensor(picked, oh0, oh1, ALU.add).then_inc(pick_r, 1)
            link(V.tensor_tensor(p1, top[:, :, 1], top[:, :, 0], ALU.subtract))
            V.tensor_copy(p1, p1).then_inc(gap_r, 1)
            dve.wait_ge(gexp_r, 1)
            link(V.tensor_scalar(pden, p1, 1.0, None, ALU.add))
            link(V.reciprocal(p0, pden))
            link(V.tensor_tensor(p1, p1, p0, ALU.mult))
            for t in range(NT):
                link(V.tensor_scalar(oh0[:, t, :], oh0[:, t, :], p0[:, t:t + 1], None, ALU.mult))
                link(V.scalar_tensor_tensor(out=weight[:, t, :], in0=oh1[:, t, :], scalar=p1[:, t:t + 1],
                                            in1=oh0[:, t, :], op0=ALU.mult, op1=ALU.add))
            dve.wait_ge(rank_ps, 1)
            link(V.scalar_tensor_tensor(out=rank, in0=pb[:, 5, 0:NT * E].rearrange("p (t e) -> p t e", t=NT),
                                        scalar=1.0, in1=picked, op0=ALU.add, op1=ALU.mult))
            for p in range(NJ // E):
                js = slice(p * E, (p + 1) * E)
                V.tensor_scalar(slot_of[:, js, :].rearrange("p e t -> p t e"), rank, -1.0 - p * PASS, None, ALU.add)
                V.tensor_copy(comb[:, js, :].rearrange("p e t -> p t e"), weight)
                V.tensor_scalar(cnt_f[0:1, js], pb[0:1, 5, 32:32 + E], float(-p * PASS), None, ALU.add)
            link(V.reduce_max(steps_f[0:1, 0:1], pb[0:1, 5, 32:32 + E], AX.X))
            link(V.tensor_scalar(steps_f[0:1, 1:2], steps_f[0:1, 0:1], float(PASS), float(E), ALU.is_gt, ALU.mult))
            link(V.tensor_scalar(steps_f[0:1, 1:2], steps_f[0:1, 1:2], float(E), None, ALU.add))
            link(V.tensor_copy(cnt[:], cnt_f[:]))
            V.tensor_copy(steps[:], steps_f[0:1, 1:2]).then_inc(route_r, 1)
            dve.wait_ge(route_r, 1)

            n_steps = dve.value_load(steps[0:1, 0:1], min_val=E, max_val=NJ)
            gain = prmT[:, ROWS["ffn_norm_g"][0] + KD:ROWS["ffn_norm_g"][0] + 2 * KD].unsqueeze(2)\
                .to_broadcast((P, KD, PASS))
            dve.sem_inc(x_moe, 1)
            with dve.Fori(0, n_steps) as j:
                n_tok = dve.value_load(cnt[0:1, bass.ds(j, 1)], min_val=-SEQ, max_val=SEQ)
                for t in range(NT):
                    ins = V.tensor_scalar(onehot[:, t], slot_no[:].rearrange("p i a c -> p i (a c)"),
                                          slot_of[:, bass.ds(j, 1), t], None, ALU.is_equal)
                ins.then_inc(oh_r, 1)
                for i in range(2):
                    dve.wait_ge(gx_ps, j * 2 + (i + 1))
                    ks = slice(4 * i, 4 * i + 4)
                    V.tensor_tensor(xselT[:, ks, :], pb[:, i, :].rearrange("p (k s) -> p k s", k=4),
                                    gain[:, ks, :], ALU.mult).then_inc(xsel_r, 1)

                def units(tiles):
                    for u in range(NE):
                        for i in range(tiles):
                            dve.wait_ge(esil_r, j * (2 * NE) + (2 * u + (i + 1 if tiles == 2 else 2)))
                            if u >= 2:
                                dve.wait_ge(egT_ps, j * NE + (u - 1))
                            V.tensor_tensor(m_g[:, u % 2, i, :], m_sil[:, u % 2, i, :],
                                            pb[:, 2 * i + u % 2, P:2 * P], ALU.mult
                                            ).then_inc(eg_r, 3 - tiles)
                    dve.wait_ge(w2_used, ND - 1 + (j + 1) * NE)
                    if tiles == 2:
                        V.tensor_copy(y_sb[:, 1, :], pb[:, 5, :]).then_inc(y_d, 1)
                    else:
                        dve.sem_inc(y_d, 1)

                with dve.If(n_tok > SLOT):
                    units(2)
                with dve.Else():
                    units(1)
                for t in range(NT):
                    dve.wait_ge(sct_ps, j * NT + (t + 1))
                    for half in range(2):
                        c = slice(half * 512, half * 512 + 512)
                        ins = V.scalar_tensor_tensor(out=x_sb[:, t, c], in0=pb[:, 6 * t + half, :],
                                                     scalar=comb[:, bass.ds(j, 1), t], in1=x_sb[:, t, c],
                                                     op0=ALU.mult, op1=ALU.add)
                    ins.then_inc(x_moe, 1)
            dve.drain().then_inc(s_dve_done, 1)
            dve.wait_ge(s_dve_done, 1)
            variance(4)
            dve.wait_ge(rstd_r, 5)
            dve.wait_ge(s_fgb, 16)
            for t in range(NT):
                V.scalar_tensor_tensor(out=x_sb[:, t, :], in0=x_sb[:, t, :], scalar=rstd[:, t:t + 1],
                                       in1=fgb, op0=ALU.mult, op1=ALU.mult).then_inc(fin_r, 1)

        @block.tensor
        def _(pe):
            mm = nc.tensor.matmul

            def ring_ready(n):
                pe.wait_ge(w13_rdy[n % R13], 32 * (n // R13 + 1))
                return w13_wide[n % R13]

            def norm(n):
                pe.wait_ge(xs_a, n + 1)
                pe.wait_ge(xs_d, n + 1)
                for k in range(KD):
                    for t in range(NT):
                        ins = nc.tensor.transpose(pb[:, k // 2, 256 * (k % 2) + P * t:256 * (k % 2) + P * t + P],
                                                  xs[:, t, k * P:(k + 1) * P], ident[:])
                    if k % 2:
                        ins.then_inc(hT_ps, 1)

            def hT_ready(n, k):
                i = 2 * (k // 4) + k % 2
                pe.wait_ge((hT_d, hT_a)[k // 2 % 2], 4 * n + i + 1)

            def mixer(l):
                norm(2 * l)
                pe.wait_ge(s_wsp, 16 * (l + 1))
                for g in range(H):
                    ins = nc.tensor.transpose(pb[:, 6, g * P:(g + 1) * P], wsp[:, g, :], ident[:])
                ins.then_inc(wspT_ps, 1)
                w = ring_ready(w13_item(l, 0))
                for h in range(H):
                    for k in range(KD):
                        if h == 0:
                            hT_ready(2 * l, k)
                        ins = mm(pb[:, 4 + h // 2, 256 * (h % 2):256 * (h % 2) + 256],
                                 w[:, k, h * P:(h + 1) * P], hT[:, k, :], start=k == 0, stop=k == KD - 1)
                    if h % 2:
                        ins.then_inc(xm_ps, 1)
                for i in range(3):
                    w = ring_ready(w13_item(l, 1 + i))
                    if i == 0:
                        pe.wait_ge(wspT_r, l + 1)
                    for t in range(NT):
                        bank = pb[:, (6, 7, 0, 1, 2, 3)[2 * i + t], :]
                        for k in range(KD):
                            ins = mm(bank, hT[:, k, t * P:(t + 1) * P], w[:, k, :], start=k == 0, stop=k == KD - 1)
                        ins.then_inc(tok_ps, 1)
                pe.wait_ge(s_wqkv, 48 * (l + 1))
                for i in range(3):
                    for h in range(H):
                        if h % 2 == 0:
                            if i == 0:
                                pe.wait_ge(xm_sb, 2 * l + h // 2 + 1)
                            elif i == 1:
                                pe.wait_ge(gelu_r, 4 * l + h // 2 + 1)
                            else:
                                pe.wait_ge(gelu_r, 4 * l + 2 + h // 2 + 1)
                        if i == 0:
                            pe.wait_ge(xc_r, H * l + h + 1)
                        src = xmT[:, h, CW - 1:] if i == 2 else xcT[:, h, :]
                        ins = mm(pb[:, (4, 6, 0)[i] + h // 2, 256 * (h % 2):256 * (h % 2) + 256],
                                 wqkv[:, i, h, :], src, start=True, stop=True)
                        if h % 2:
                            ins.then_inc(qkv_ps, 1)
                for t in range(NT):
                    pe.wait_ge(o_r, NT * l + t + 1)
                    for h in range(H):
                        ins = mm(pb[:, 2 + t, h * DH:(h + 1) * DH],
                                 xmT[:, h, CW - 1 + t * P:CW - 1 + (t + 1) * P], wqkv[:, 2, h, :],
                                 start=True, stop=True)
                    ins.then_inc(qkv_ps, 1)
                pe.wait_ge(qk_r, 4 * (l + 1))
                pe.wait_ge(vT_r, 2 * (l + 1))
                pe.wait_ge(s_small, 64 + 32 * l)
                for t in range(NT):
                    for c in range(3 * H):
                        src = (qT, kT, vT)[c // H][:, c % H, t * P:(t + 1) * P]
                        ins = mm(pb[:, 4, t * 2 * H:(t + 1) * 2 * H], src, wif[:, c, :],
                                 start=c == 0, stop=c == 3 * H - 1)
                ins.then_inc(gate_ps, 1)
                pe.wait_ge(gate_r, l + 1)
                for t in range(NT):
                    for f in range(2):
                        ins = nc.tensor.transpose(pb[0:H, 5, 256 * f + t * P:256 * f + (t + 1) * P],
                                                  g_tok[:, t, f * H:(f + 1) * H], ident[:])
                ins.then_inc(gateT_ps, 1)
                for t in range(NT):
                    pe.wait_ge(vg_r, NT * l + t + 1)
                    for g in range(H):
                        ins = mm(pb[:, 6 + t, g * P:(g + 1) * P], wspT[:, g, :],
                                 v_gate[:, t, g * P:(g + 1) * P], start=True, stop=True)
                    ins.then_inc(sv_ps, 1)
                pe.wait_ge(vt_r, NT * (l + 1))
                for h in range(H):
                    mm(pb[:, h, 0:256], kT[:, h, 0:P], qT[:, h, :], start=True, stop=True)
                    mm(pb[:, h, 256:384], kT[:, h, P:], qT[:, h, P:], start=True, stop=True).then_inc(sc_ps, 1)
                pe.wait_ge(row_r, l + 1)
                pe.wait_ge(yg_r, NT * (l + 1))
                for t in range(NT):
                    for i, r in enumerate((a_row, neg_stab)):
                        ins = nc.tensor.transpose(pb[:, 4 + i, 32 * (i + 1) + t * H:32 * (i + 1) + (t + 1) * H],
                                                  r[:, t * P:(t + 1) * P], ident[0:H, 0:H])
                ins.then_inc(aT_ps, 1)
                for h in range(H):
                    ins = mm(pb[:, 6 + h // 2, 256 * (h % 2):256 * (h % 2) + 256], sel[:, h, :], neg_m,
                             start=True, stop=True)
                    if h % 2:
                        ins.then_inc(mb_ps, 1)
                pe.wait_ge(arg_r, 2 * (l + 1))
                pe.wait_ge(floor_r, l + 1)
                for h in range(H):
                    pe.wait_ge(sT_r, H * l + h + 1)
                    n0, n1 = pb[:, 4 + h, 0:DH + 1], pb[:, 4 + h, 256:256 + DH + 1]
                    mm(n0, wS[:, h, 0:P], v_tok[:, 0, h, :], start=True, stop=True)
                    mm(n1, wS[:, h, P:2 * P], v_tok[:, 0, h, :], start=True, stop=False)
                    mm(n1, wS[:, h, 2 * P:3 * P], v_tok[:, 1, h, :], start=False, stop=True).then_inc(num_ps, 1)
                pe.wait_ge(ygs_r, NT * (l + 1))
                for g in range(H):
                    for t in range(NT):
                        ins = nc.tensor.transpose(pb[:, 2 + g // 2, 256 * (g % 2) + P * t:256 * (g % 2) + P * t + P],
                                                  v_gate[:, t, g * P:(g + 1) * P], ident[:])
                    if g % 2:
                        ins.then_inc(ygT_ps, 1)
                for h in range(H):
                    pe.wait_ge(hm_r, H * l + h + 1)
                    for t in range(NT):
                        ins = nc.tensor.transpose(pb[:, h // 2, 256 * (h % 2) + P * t:256 * (h % 2) + P * t + P],
                                                  hm[:, t, h * DH:(h + 1) * DH], ident[:])
                    if h % 2:
                        ins.then_inc(hmT_ps, 1)
                for half in range(2):
                    w = ring_ready(w13_item(l, 4 + half))
                    for t in range(NT):
                        for i in range(KD):
                            c = (i + H) % KD
                            if half == 0 and t == 0:
                                if c >= H:
                                    pe.wait_ge(ygT_r, H * l + c - H + 1)
                                else:
                                    pe.wait_ge(ymT_r, H * l + c + 1)
                            ins = mm(pb[:, 4 + 2 * half + t, :], yT[:, c, t * P:(t + 1) * P], w[:, c, :],
                                     start=i == 0, stop=i == KD - 1)
                        ins.then_inc(wo_ps, 1)

            pe.wait_ge(s_const, 1)
            pe.wait_ge(s_prm, 16 * 8)
            nc.tensor.transpose(pb[:, 7, 0:NROWS], prm[:], ident[0:NROWS, 0:NROWS]).then_inc(s_prm_ps, 1)

            mixer(0)

            norm(1)
            pe.wait_ge(hT_d, 8)
            pe.wait_ge(hT_a, 8)

            def dense_down(q):
                r = min(P, DFF - q * P)
                u, b = q // 2, q % 2
                if b == 0:
                    blocks = 1 + (DFF > u * UF + P)
                    full = 16 * 2 * (u // R2)
                    pe.wait_ge(w2_rdy[u % R2], full + 16 * blocks)
                pe.wait_ge(g_r, q + 1)
                for half in range(2):
                    for t in range(NT):
                        ins = mm(pb[:, 4 + 2 * half + t, :], d_g[0:r, q % 4, t * P:(t + 1) * P],
                                 w2[u % R2][0:r, b, half * 512:half * 512 + 512],
                                 start=q == 0, stop=q == 2 * ND - 1)
                        if q == 2 * ND - 1:
                            ins.then_inc(down_ps, 1)
                if b == 1 and u < ND - 1:
                    ins.then_inc(w2_used, 1)

            for q in range(2 * ND):
                u, b = q // 2, q % 2
                n = w13_item(0, MIX + u)
                ring_ready(n)
                r = min(P, DFF - q * P)
                if q >= 4:
                    pe.wait_ge(g_r, q - 3)
                for k2 in range(2):
                    for k in range(KD):
                        ins = mm(pb[0:r, q % 4, k2 * SEQ:(k2 + 1) * SEQ], w13[n % R13][:, k, k2, b * P:b * P + r],
                                 hT[:, k, :], start=k == 0, stop=k == KD - 1)
                ins.then_inc(up_ps, 1)
                if q >= 2:
                    dense_down(q - 2)
            dense_down(2 * ND - 2)
            dense_down(2 * ND - 1)

            mixer(1)

            norm(3)
            for t in range(NT):
                for k in range(KD):
                    if t == 0:
                        hT_ready(3, k)
                    ins = mm(pb[:, 4, t * E:(t + 1) * E], hT[:, k, t * P:(t + 1) * P], wr[:, k, :],
                             start=k == 0, stop=k == KD - 1)
            ins.then_inc(lg_ps, 1)
            pe.wait_ge(pick_r, 1)
            mm(pb[:, 5, 0:E], before[:], picked[:, 0, :], start=True, stop=True)
            mm(pb[:, 5, E:2 * E], ones_pp[:], picked[:, 0, :], start=True, stop=False)
            mm(pb[:, 5, E:2 * E], before[:], picked[:, 1, :], start=False, stop=True)
            for t in range(NT):
                ins = mm(pb[0:1, 5, 32:32 + E], ones_pp[:, 0:1], picked[:, t, :], start=t == 0, stop=t == NT - 1)
            ins.then_inc(rank_ps, 1)

            pe.wait_ge(route_r, 1)
            n_steps = pe.value_load(steps[0:1, 0:1], min_val=E, max_val=NJ)
            with pe.Fori(0, n_steps) as j:
                n_tok = pe.value_load(cnt[0:1, bass.ds(j, 1)], min_val=-SEQ, max_val=SEQ)
                pe.wait_ge(oh_r, j + 1)
                pe.wait_ge(x_moe, j * NT + 1)
                for k in range(KD):
                    for t in range(NT):
                        ins = mm(pb[:, k // 4, (k % 4) * PASS:(k % 4 + 1) * PASS],
                                 xs[:, t, k * P:(k + 1) * P], onehot[:, t, :, 0:SLOT],
                                 start=t == 0, stop=t == NT - 1)
                    if k % 4 == 3:
                        ins.then_inc(gx_ps, 1)
                for i in range(2):
                    for t in range(NT):
                        ins = nc.tensor.transpose(pb[:, 7, (i * NT + t) * P:(i * NT + t + 1) * P],
                                                  onehot[:, t, i, :], ident[:])
                ins.then_inc(ohT_ps, 1)
                pe.wait_ge(xsel_r, j * 2 + 2)

                def units(tiles):
                    def up(u):
                        n = (W13_MOE + u) % R13
                        pe.wait_ge(w13_rdy[n], j * (32 * NE // R13) + 32 * ((W13_MOE + u) // R13 + 1))
                        if u >= 2:
                            pe.wait_ge(eg_r, j * (2 * NE) + 2 * (u - 1))
                        for i in range(tiles):
                            for k in range(KD):
                                for half in range(2):
                                    ins = mm(pb[SLOT * half:SLOT * half + SLOT, 2 * i + u % 2, 0:2 * P]
                                             .rearrange("p (w f) -> p w f", w=2),
                                             xselT[:, k, i * SLOT:(i + 1) * SLOT],
                                             w13[n][:, k, :, half * P:(half + 1) * P],
                                             start=k == 0, stop=k == KD - 1)
                            ins.then_inc(eup_ps, 3 - tiles)

                    def turn(u):
                        pe.wait_ge(eg_r, j * (2 * NE) + 2 * (u + 1))
                        for i in range(tiles):
                            ins = nc.tensor.transpose(pb[:, 6, i * P:(i + 1) * P], m_g[:, u % 2, i, :], ident[:])
                        ins.then_inc(egT_ps, 1)

                    def down(u):
                        n = (W2_MOE + u) % R2
                        pe.wait_ge(w2_rdy[n], j * (32 * NE // R2) + 32 * ((W2_MOE + u) // R2 + 1))
                        pe.wait_ge(egT_r, j * NE + (u + 1))
                        for i in range(tiles):
                            for b in range(2):
                                for half in range(2):
                                    ins = mm(pb[SLOT * half:SLOT * half + SLOT, 4 + i, :],
                                             m_gT[:, u % 2, i, b * SLOT:(b + 1) * SLOT],
                                             w2[n][:, b, half * 512:(half + 1) * 512],
                                             start=u == 0 and b == 0, stop=u == NE - 1 and b == 1)
                        ins.then_inc(w2_used, 1)

                    up(0)
                    for u in range(1, NE):
                        turn(u - 1)
                        up(u)
                        down(u - 1)
                    turn(NE - 1)
                    down(NE - 1)
                    pe.wait_ge(y_a, j + 1)
                    pe.wait_ge(y_d, j + 1)
                    pe.wait_ge(ohT_r, j + 1)
                    for t in range(NT):
                        for i in range(tiles):
                            for half in range(2):
                                r = slice(SLOT * half, SLOT * half + SLOT)
                                ins = mm(pb[:, 6 * t + half, :], onehotT[r, i, t, :], y_sb[r, i, :],
                                         start=i == 0, stop=i == tiles - 1)
                        ins.then_inc(sct_ps, 1)

                with pe.If(n_tok > SLOT):
                    units(2)
                with pe.Else():
                    units(1)


_INS = ["x", "mix_norm_g", "w_in", "conv_w", "conv_b", "w_q", "w_k", "w_v", "w_if", "b_if", "skip_m",
        "mh_norm_g", "gm_v_g", "w_sp", "b_sp", "gm_out_g", "w_out", "ffn_norm_g",
        "dense_w1", "dense_w3", "dense_w2", "moe_router", "moe_w1", "moe_w3", "moe_w2", "final_norm_g"]


def kernel(**inputs):
    import numpy as _np
    import concourse.bacc as _bacc
    from concourse.bass_utils import run_bass_kernel_spmd as _run

    nc = _bacc.Bacc("TRN2", target_bir_lowering=False, num_devices=1)
    arrays, args = {}, []
    for name in _INS:
        a = _np.ascontiguousarray(inputs[name])
        arrays[f"in_{name}"] = a
        args.append(nc.dram_tensor(f"in_{name}", a.shape, mybir.dt.from_np(a.dtype), kind="ExternalInput").ap())
    args.append(nc.dram_tensor("out_0", (1, SEQ, D), fp32, kind="ExternalOutput").ap())
    trunk(nc, *args)
    r = _run(nc, [arrays], core_ids=[0])
    return r.results[0]["out_0"]
```

```python
import concourse.bass as bass
from concourse import mybir
from contextlib import ExitStack

fp32 = mybir.dt.float32
fp32r = mybir.dt.float32r
i32 = mybir.dt.int32
u32 = mybir.dt.uint32
ALU = mybir.AluOpType
ACT = mybir.ActivationFunctionType
AX = mybir.AxisListType

P = 128
SEQ, D, L = 256, 1024, 2
NT = SEQ // P
KD = D // P
H, DH = 4, 128
MW = H * DH
CW = 4
CHUNK = 64
DFF, DFE, E = 2752, 3584, 8
EPS = 1e-6
SCALE = DH ** -0.5
UF = 256
ND = -(-DFF // UF)
NE = DFE // UF
PASS = 128
NJ = E * (SEQ // PASS)
KH = KD // 2
R13, R2 = 7, 2
MIX = 6
W13_MOE = 2 * (2 * MIX + ND)
W2_MOE = ND

WIN_ORDER = [0, 3, 2, 1]

ROWS = {}
_at = 0
for _name, _n in (("mix_norm_g", L * KD), ("ffn_norm_g", L * KD), ("conv_w", L * CW * H),
                  ("conv_b", L * H), ("skip_m", L * H), ("mh_norm_g", L * H),
                  ("gm_out_g", L * H), ("b_sp", L * H)):
    ROWS[_name] = (_at, _n)
    _at += _n
NROWS = _at


def dense_width(u):
    return min(UF, DFF - u * UF)


def trunk(nc, x, mix_norm_g, w_in, conv_w, conv_b, w_q, w_k, w_v, w_if, b_if, skip_m,
          mh_norm_g, gm_v_g, w_sp, b_sp, gm_out_g, w_out, ffn_norm_g,
          dense_w1, dense_w3, dense_w2, moe_router, moe_w1, moe_w3, moe_w2,
          final_norm_g, out):
    ctx = ExitStack()
    with ctx:
        def sb(name, shape, dt=fp32):
            return ctx.enter_context(nc.sbuf_tensor(name, shape, dt))

        def sem(name):
            return ctx.enter_context(nc.semaphore(name))

        w13 = [sb(f"w13_{i}", [P, KH, 2, UF]) for i in range(R13)]
        w13_wide = [w[:].rearrange("p k w f -> p k (w f)") for w in w13]
        w2 = [sb(f"w2_{i}", [P, 2, D]) for i in range(R2)]
        s13h = sb("s13h", [P, 2, KH, 2 * UF], fp32r)
        s13l = sb("s13l", [P, 2, KH, 2 * UF], fp32r)
        s2h = sb("s2h", [P, 2, D], fp32r)
        s2l = sb("s2l", [P, 2, D], fp32r)
        x_sb = sb("x_sb", [P, NT, D])
        xs = sb("xs", [P, NT, D])
        o_sb = xs[:, 0, :].rearrange("p (t c) -> p t c", t=NT)
        u_sb = xs[:, 1, :].rearrange("p (t c) -> p t c", t=NT)
        hT = sb("hT", [P, KD, SEQ])
        wS = hT[:].rearrange("p k s -> p (k s)")[:, 0:H * 384].rearrange("p (h s) -> p h s", h=H)
        wqkv = sb("wqkv", [P, 3, H, DH])
        wif = sb("wif", [P, 3 * H, 2 * H])
        bif = sb("bif", [H, L, 2])
        wspT = sb("wspT", [P, H, P])
        gvb = sb("gvb", [P, MW])
        fgb = hT[:].rearrange("p k s -> p (k s)")[:, 0:D]
        wr = sb("wr", [P, KD, E])
        prm = sb("prm", [NROWS, P])
        prmT = sb("prmT", [P, NROWS])
        ident = sb("ident", [P, P])
        sel = sb("sel", [H, H, P])
        before = sb("before", [P, P])
        ones_pp = sb("ones_pp", [P, P])
        neg_half = sb("neg_half", [P, NT * H])
        slot_no = sb("slot_no", [P, PASS])
        expert_no = sb("expert_no", [P, NT, E])

        ss = sb("ss", [P, NT])
        var = sb("var", [P, NT])
        rstd = sb("rstd", [P, NT])

        ARENA = 9408
        arena = sb("arena", [P, ARENA])
        at = [0]

        def carve(n):
            at[0] += n
            assert at[0] <= ARENA, at[0]
            return arena[:, at[0] - n:at[0]]

        XP = SEQ + CW - 1
        yT = carve(KD * SEQ).rearrange("p (k s) -> p k s", k=KD)
        xmT = carve(H * XP).rearrange("p (h s) -> p h s", h=H)
        xcT = carve(H * SEQ).rearrange("p (h s) -> p h s", h=H)
        qT = carve(H * SEQ).rearrange("p (h s) -> p h s", h=H)
        kT = carve(H * SEQ).rearrange("p (h s) -> p h s", h=H)
        v_tok = carve(NT * H * (DH + 1)).rearrange("p (t h c) -> p t h c", t=NT, h=H)
        v_gate = carve(NT * MW).rearrange("p (t c) -> p t c", t=NT)
        wsp = v_gate.rearrange("p t c -> p (t c)")[:, 0:H * P].rearrange("p (g j) -> p g j", g=H)
        vT_hm = carve(H * SEQ)
        vT = vT_hm.rearrange("p (h s) -> p h s", h=H)
        hm = vT_hm.rearrange("p (t c) -> p t c", t=NT)
        g_tok = carve(NT * 2 * H).rearrange("p (t c) -> p t c", t=NT)
        aT = carve(NT * H).rearrange("p (t h) -> p t h", t=NT)
        floorT = carve(H * NT).rearrange("p (h t) -> p h t", t=NT)
        den = carve(H * NT).rearrange("p (h t) -> p h t", t=NT)
        rden = carve(H * NT).rearrange("p (h t) -> p h t", t=NT)
        stats = carve(H * NT * 6).rearrange("p (h t c) -> p h t c", h=H, t=NT)
        mv = carve(H * NT * 2).rearrange("p (h t c) -> p h t c", h=H, t=NT)
        hvar = carve(H * NT)
        hrstd = carve(H * NT)
        gstats = carve(NT * 6).rearrange("p (t c) -> p t c", t=NT)
        gmv = carve(NT * 2).rearrange("p (t c) -> p t c", t=NT)
        gvar, grstd, yss, yvar, yrstd = (carve(NT) for _ in range(5))
        lf_min, gate_e, run_b, a_row, run_m, neg_m = (yT[0:H, i, :] for i in range(6))
        neg_stab = lf_min

        at[0] = 0
        d_sil = carve(2 * SEQ).rearrange("p (q s) -> p q s", q=2)
        d_g = carve(4 * SEQ).rearrange("p (q s) -> p q s", q=4)
        at[0] = 0
        onehot = carve(NT * PASS).rearrange("p (t c) -> p t c", t=NT)
        onehotT = carve(NT * P).rearrange("p (t c) -> p t c", t=NT)
        x_gain = carve(KD * PASS).rearrange("p (k s) -> p k s", k=KD)
        m_sil = carve(2 * UF).rearrange("p (q f) -> p q f", q=2)
        m_g = carve(2 * UF).rearrange("p (q f) -> p q f", q=2)
        y_sb = carve(D)
        xsel_h = sb("xsel_h", [P, KD, PASS], fp32r)
        xsel_l = sb("xsel_l", [P, KD, PASS], fp32r)
        gT_h = sb("gT_h", [P, 2, PASS], fp32r)
        gT_l = sb("gT_l", [P, 2, PASS], fp32r)
        logits, oh0, oh1, picked, rank, weight = (
            carve(NT * E).rearrange("p (t e) -> p t e", t=NT) for _ in range(6))
        top = carve(NT * 8).rearrange("p (t e) -> p t e", t=NT)
        top_fi = carve(NT * 8).rearrange("p (t e) -> p t e", t=NT)
        p1, p0, pden = (carve(NT) for _ in range(3))
        slot_of = carve((NJ + 1) * NT).rearrange("p (j t) -> p j t", t=NT)
        comb = carve(NJ * NT).rearrange("p (j t) -> p j t", t=NT)
        top_i = sb("top_i", [P, NT, 8], u32)
        last_f = sb("last_f", [1, 2])
        last_ij = sb("last_ij", [1, 1], i32)

        def col(name, i):
            return prmT[:, ROWS[name][0] + i:ROWS[name][0] + i + 1]

        pb = ctx.enter_context(nc.psum_tensor("pb", [P, 8, 512], fp32))

        s_x = sem("x_loaded")
        s_prm = sem("params_loaded")
        s_wqkv = sem("wqkv_loaded")
        s_small = sem("small_loaded")
        s_wsp = sem("wsp_loaded")
        w13_rdy = [sem(f"w13_loaded_{i}") for i in range(R13)]
        w2_rdy = [sem(f"w2_loaded_{i}") for i in range(R2)]
        w2_used = sem("w2_used")
        s_const = sem("constants_made")
        s_prm_ps = sem("params_transposed")
        s_prmT = sem("params_in_sbuf")
        s_pad = sem("conv_pad_made")
        s_vone = sem("value_ones_made")
        sq_a = sem("squares_summed_act")
        var_r = sem("variance_ready")
        rstd_r = sem("rstd_ready")
        xs_a = sem("xs_ready_act")
        xs_d = sem("xs_ready_dve")
        hT_ps = sem("hT_in_psum")
        hT_d = sem("hT_ready_dve")
        hT_a = sem("hT_ready_act")
        x_upd = sem("x_updated")
        xm_ps = sem("xm_in_psum")
        xm_sb = sem("xm_ready")
        conv_r = sem("conv_ready")
        xc_r = sem("xc_ready")
        skip_r = sem("skip_ready")
        tok_ps = sem("tokenwise_proj_in_psum")
        gelu_r = sem("gelu_ready")
        o_r = sem("o_ready")
        qkv_ps = sem("qkv_in_psum")
        qk_r = sem("qk_ready")
        vT_r = sem("vT_ready")
        vt_r = sem("v_tok_ready")
        gate_ps = sem("gates_in_psum")
        gate_r = sem("gates_ready")
        gateT_ps = sem("gate_rows_in_psum")
        absf_r = sem("abs_forget_ready")
        ln_r = sem("softplus_ready")
        row_r = sem("gate_rows_ready")
        mb_ps = sem("running_max_broadcast")
        aT_ps = sem("a_columns_in_psum")
        aT_r = sem("a_columns_ready")
        floor_r = sem("floor_ready")
        arg_r = sem("weight_exponent_ready")
        wexp_r = sem("weights_exponentiated")
        wmask_r = sem("weights_masked")
        sc_ps = sem("scores_in_psum")
        sT_r = sem("weighted_scores_ready")
        num_ps = sem("numerators_in_psum")
        hvar_r = sem("head_variance_ready")
        hrstd_r = sem("head_rstd_ready")
        hm_r = sem("head_output_ready")
        hmT_ps = sem("head_output_transposed")
        wspT_ps = sem("wsp_transposed")
        wspT_r = sem("wspT_ready")
        gvar_r = sem("v_variance_ready")
        grstd_r = sem("v_rstd_ready")
        vn_r = sem("v_normalised")
        vg_r = sem("v_scaled")
        sv_ps = sem("gating_in_psum")
        yg_r = sem("gated_ready")
        yss_r = sem("gated_squares_summed")
        yvar_r = sem("gated_variance_ready")
        yrstd_r = sem("gated_rstd_ready")
        ygs_r = sem("gated_normalised")
        ygT_ps = sem("gated_transposed")
        ygT_r = sem("gated_channels_ready")
        ymT_r = sem("head_channels_ready")
        wo_ps = sem("mixer_output_in_psum")
        up_ps = sem("dense_up_in_psum")
        sil_r = sem("dense_silu_ready")
        g_r = sem("dense_product_ready")
        down_ps = sem("dense_down_in_psum")
        lg_ps = sem("logits_in_psum")
        pick_r = sem("picked_ready")
        rank_ps = sem("ranks_in_psum")
        route_r = sem("routing_ready")
        oh_r = sem("onehot_ready")
        gx_ps = sem("gathered_in_psum")
        ohT_ps = sem("onehot_transposed")
        ohT_r = sem("onehotT_ready")
        xg_r = sem("gathered_times_gain")
        xh_r = sem("gathered_high_ready")
        xsel_r = sem("gathered_ready")
        w13_hi = sem("w13_high_ready")
        w13_lo = sem("w13_low_ready")
        s13_used = sem("w13_parts_used")
        w2_hi = sem("w2_high_ready")
        w2_lo = sem("w2_low_ready")
        s2_used = sem("w2_parts_used")
        esil_r = sem("expert_silu_ready")
        eg_r = sem("expert_product_ready")
        egT_ps = sem("expert_product_transposed")
        gTh_r = sem("expert_productT_high_ready")
        egT_r = sem("expert_productT_ready")
        y_a = sem("expert_output_ready_act")
        y_d = sem("expert_output_ready_dve")
        sct_ps = sem("scattered_in_psum")
        x_moe = sem("x_updated_by_expert")
        gap_r = sem("logit_gap_ready")
        gexp_r = sem("gate_exponential_ready")
        s_dve_done = sem("experts_done")
        fin_r = sem("final_ready")
        s_fgb = sem("final_gain_loaded")
        s_out = sem("output_stored")
        dve_chain = sem("dve_chain")
        act_chain = sem("act_chain")
        pool_chain = sem("pool_chain")

        block = ctx.enter_context(nc.Block())

        def w13_item(l, i):
            return l * (MIX + ND) + i

        @block.sync
        def _(sp):
            def used(n):
                l, i = n // 2 // (MIX + ND), n // 2 % (MIX + ND)
                if i == 0:
                    sp.wait_ge(xm_ps, 2 * (l + 1))
                elif i < 4:
                    sp.wait_ge(tok_ps, 6 * l + 2 * i)
                elif i < MIX:
                    sp.wait_ge(wo_ps, 4 * l + 2 * (i - 3))
                else:
                    sp.wait_ge(up_ps, 2 * (i - MIX + 1))

            def ring_slot(n):
                if n >= R13:
                    used(n - R13)
                return n % R13

            def load_columns(g, w):
                for a in range(2):
                    n = 2 * g + a
                    sp.dma_start(w13_wide[ring_slot(n)], w[a * KH * P:(a + 1) * KH * P, :]
                                 .rearrange("(k p) f -> p k f", p=P)).then_inc(w13_rdy[n % R13], 32)

            def load_w_in(l, i):
                c = WIN_ORDER[i] * MW
                load_columns(w13_item(l, i), w_in[l, :, c:c + MW])

            def load_w_out(l, i):
                load_columns(w13_item(l, 4 + i), w_out[l, :, i * 512:(i + 1) * 512])

            sp.dma_start(x_sb[:], x[0].rearrange("(t p) d -> p t d", p=P)).then_inc(s_x, 16)
            for name, ap, w in (("mix_norm_g", mix_norm_g, KD), ("ffn_norm_g", ffn_norm_g, KD),
                                ("conv_b", conv_b, H), ("skip_m", skip_m, H),
                                ("mh_norm_g", mh_norm_g, H), ("gm_out_g", gm_out_g, H)):
                r, n = ROWS[name]
                sp.dma_start(prm[r:r + n, :], ap.rearrange("l (k p) -> (l k) p", p=P)).then_inc(s_prm, 16)
            r, n = ROWS["conv_w"]
            sp.dma_start(prm[r:r + n, :], conv_w.rearrange("l j (k p) -> (l j k) p", p=P)).then_inc(s_prm, 16)
            r, n = ROWS["b_sp"]
            sp.dma_start(prm[r:r + n, :], b_sp.rearrange("l g i -> (l g) i")).then_inc(s_prm, 16)
            load_w_in(0, 0)

            def load_mixer_params(l):
                if l:
                    sp.wait_ge(gate_ps, l)
                    sp.wait_ge(vg_r, 2 * l)
                    sp.wait_ge(wo_ps, 4 * l)
                for i, w in enumerate((w_q, w_k, w_v)):
                    sp.dma_start(wqkv[:, i], w[l].rearrange("h d e -> d h e")).then_inc(s_wqkv, 16)
                sp.dma_start(wif[:], w_if[l].rearrange("(c p) g -> p c g", p=P)).then_inc(s_small, 16)
                sp.dma_start(gvb[:], gm_v_g[l:l + 1, :].to_broadcast((P, MW))).then_inc(s_small, 16)
                sp.dma_start(wsp[:], w_sp[l].rearrange("g i j -> i g j")).then_inc(s_wsp, 16)
                if l == 0:
                    sp.dma_start(bif[:], b_if.rearrange("l (a h) -> h l a", h=H),
                                 allow_slow_non_contiguous=True).then_inc(s_small, 16)
                    sp.dma_start(wr[:], moe_router[0].rearrange("(k p) e -> p k e", p=P)).then_inc(s_small, 16)

            load_mixer_params(0)
            for i in range(1, 4):
                load_w_in(0, i)
            for i in range(2):
                load_w_out(0, i)
            for u in range(ND):
                wd = dense_width(u)
                for a in range(2):
                    n = ring_slot(2 * w13_item(0, MIX + u) + a)
                    for k, w in enumerate((dense_w1, dense_w3)):
                        sp.dma_start(w13[n][:, :, k, 0:wd],
                                     w[0, a * KH * P:(a + 1) * KH * P, u * UF:u * UF + wd]
                                     .rearrange("(k p) f -> p k f", p=P)).then_inc(w13_rdy[n], 16)
            load_mixer_params(1)
            for i in range(4):
                load_w_in(1, i)
            for i in range(2):
                load_w_out(1, i)

            def load_expert(j, e):
                for c in range(2 * NE):
                    u, a = c // 2, c % 2
                    n = (W13_MOE + c) % R13
                    if isinstance(j, int) and j == 0 and c < R13:
                        used(W13_MOE + c - R13)
                    else:
                        sp.wait_ge(w13_lo, j * (2 * NE) + (c - R13 + 1))
                    for k, w in enumerate((moe_w1, moe_w3)):
                        sp.dma_start(w13[n][:, :, k, :],
                                     w[0, bass.ds(e, 1), a * KH * P:(a + 1) * KH * P, u * UF:(u + 1) * UF]
                                     .rearrange("e (k p) f -> p (e k) f", p=P)).then_inc(w13_rdy[n], 16)

            load_expert(0, 0)
            with sp.Fori(1, E) as e:
                load_expert(e, e)
            sp.wait_ge(lg_ps, 1)
            sp.dma_start(fgb, final_norm_g.rearrange("(a d) -> a d", a=1).to_broadcast((P, D))
                         ).then_inc(s_fgb, 16)
            sp.wait_ge(route_r, 1)
            last_step = sp.value_load(last_ij[0:1, 0:1], min_val=E - 1, max_val=NJ - 1)
            with sp.If(last_step >= E):
                with sp.Fori(0, E) as e:
                    load_expert(e + E, e)
            with sp.Else():
                sp.nop()
            sp.wait_ge(fin_r, NT)
            sp.dma_start(out[0].rearrange("(t p) d -> p t d", p=P), x_sb[:]).then_inc(s_out, 16)
            sp.wait_ge(s_out, 16)

        @block.gpsimd
        def _(pool):
            links = [0]

            def link(ins):
                links[0] += 1
                ins.then_inc(pool_chain, 1)
                pool.wait_ge(pool_chain, links[0])

            nc.gpsimd.memset(ident[:], 0.0)
            nc.gpsimd.memset(ones_pp[:], 1.0)
            nc.gpsimd.memset(neg_half[:], -0.5)
            link(nc.gpsimd.memset(sel[:], 0.0))
            nc.gpsimd.affine_select(out=ident[:], in_=ident[:], compare_op=ALU.not_equal, fill=1.0,
                                    base=0, pattern=[[-1, P]], channel_multiplier=1)
            nc.gpsimd.affine_select(out=before[:], in_=ones_pp[:], compare_op=ALU.is_gt, fill=0.0,
                                    base=0, pattern=[[1, P]], channel_multiplier=-1)
            nc.gpsimd.affine_select(out=sel[:], in_=sel[:], compare_op=ALU.not_equal, fill=1.0,
                                    base=0, pattern=[[-1, H], [0, P]], channel_multiplier=1)
            nc.gpsimd.iota(slot_no[:], pattern=[[1, PASS]], base=0,
                           channel_multiplier=0, allow_small_or_imprecise_dtypes=True)
            nc.gpsimd.iota(expert_no[:], pattern=[[0, NT], [1, E]], base=0,
                           channel_multiplier=0, allow_small_or_imprecise_dtypes=True
                           ).then_inc(s_const, 1)

            def rsqrt(n):
                pool.wait_ge(var_r, n + 1)
                nc.gpsimd.tensor_tensor(rstd[:], var[:], neg_half[:, 0:NT], ALU.pow).then_inc(rstd_r, 1)

            def mixer(l):
                rsqrt(2 * l)
                pool.wait_ge(gvar_r, l + 1)
                nc.gpsimd.tensor_tensor(grstd, gvar, neg_half[:, 0:NT], ALU.pow).then_inc(grstd_r, 1)
                pool.wait_ge(s_small, 64 + 32 * l)
                for t in range(NT):
                    pool.wait_ge(vn_r, NT * l + t + 1)
                    nc.gpsimd.tensor_tensor(v_gate[:, t, :], v_gate[:, t, :], gvb[:], ALU.mult
                                            ).then_inc(vg_r, 1)
                pool.wait_ge(qkv_ps, 8 * l + 4)
                for h in range(H):
                    ins = nc.gpsimd.tensor_scalar(xcT[:, h, :], xcT[:, h, :], col("skip_m", l * H + h),
                                                  None, ALU.mult)
                ins.then_inc(skip_r, 1)
                pool.wait_ge(yvar_r, l + 1)
                nc.gpsimd.tensor_tensor(yrstd, yvar, neg_half[:, 0:NT], ALU.pow).then_inc(yrstd_r, 1)
                pool.wait_ge(wexp_r, 2 * (l + 1))
                for b in range(2):
                    d = wS[:, :, 256 * b:256 * b + P]
                    nc.gpsimd.affine_select(out=d, in_=d, compare_op=ALU.is_ge, fill=0.0, base=0,
                                            pattern=[[0, H], [1, P]], channel_multiplier=-1
                                            ).then_inc(wmask_r, 1)
                pool.wait_ge(hvar_r, l + 1)
                nc.gpsimd.tensor_tensor(hrstd, hvar, neg_half[:, 0:NT * H], ALU.pow).then_inc(hrstd_r, 1)

            mixer(0)
            rsqrt(1)
            for u in range(ND):
                if u >= R2:
                    pool.wait_ge(w2_used, u - R2 + 1)
                for b in range(2):
                    rows_b = min(P, DFF - u * UF - b * P)
                    if rows_b > 0:
                        f = u * UF + b * P
                        pool.dma_start(w2[u % R2][0:rows_b, b, :], dense_w2[0, f:f + rows_b, :]
                                       ).then_inc(w2_rdy[u % R2], 16)
            mixer(1)
            rsqrt(3)

            def load_expert(j, e):
                for u in range(NE):
                    n = (W2_MOE + u) % R2
                    if not (isinstance(j, int) and j == 0 and u < R2):
                        pool.wait_ge(w2_lo, j * NE + (u - R2 + 1))
                    pool.dma_start(w2[n][:], moe_w2[0, bass.ds(e, 1), u * UF:(u + 1) * UF, :]
                                   .rearrange("a (b p) d -> p (a b) d", p=P)).then_inc(w2_rdy[n], 32)

            pool.wait_ge(down_ps, 4)
            load_expert(0, 0)
            with pool.Fori(1, E) as e:
                load_expert(e, e)
            pool.wait_ge(route_r, 1)
            last_step = pool.value_load(last_ij[0:1, 0:1], min_val=E - 1, max_val=NJ - 1)
            with pool.If(last_step >= E):
                with pool.Fori(0, E) as e:
                    load_expert(e + E, e)
            with pool.Else():
                pool.nop()
            pool.wait_ge(var_r, 5)
            nc.gpsimd.tensor_tensor(rstd[:], var[:], neg_half[:, 0:NT], ALU.pow).then_inc(rstd_r, 1)

        @block.scalar
        def _(act):
            links = [0]

            def link(ins):
                links[0] += 1
                ins.then_inc(act_chain, 1)
                act.wait_ge(act_chain, links[0])

            def norm(n):
                if n == 0:
                    act.wait_ge(s_x, 16)
                else:
                    act.wait_ge(x_upd, 4 * n)
                link(nc.scalar.activation(xs[:, 0, :], x_sb[:, 0, :], ACT.Square, accum_out=ss[:, 0:1]))
                nc.scalar.activation(ss[:, 0:1], ss[:, 0:1], ACT.Copy).then_inc(sq_a, 1)
                act.wait_ge(rstd_r, n + 1)
                nc.scalar.activation(xs[:, 0, :], x_sb[:, 0, :], ACT.Copy, scale=rstd[:, 0:1]).then_inc(xs_a, 1)
                if n == 0:
                    act.wait_ge(s_prmT, 1)
                g, l = ("ffn_norm_g", "mix_norm_g")[n % 2 == 0], n // 2
                for i in (1, 3):
                    act.wait_ge(hT_ps, 4 * n + i + 1)
                    for k in (2 * i, 2 * i + 1):
                        nc.scalar.activation(hT[:, k, :], pb[:, i, 256 * (k % 2):256 * (k % 2) + 256], ACT.Copy,
                                             scale=col(g, l * KD + k)).then_inc(hT_a, 1)

            def mixer(l):
                norm(2 * l)
                for i in range(2):
                    act.wait_ge(xm_ps, 2 * l + i + 1)
                    nc.scalar.activation(xmT[:, 2 * i:2 * i + 2, CW - 1:], pb[:, 4 + i, :]
                                         .rearrange("p (h s) -> p h s", h=2), ACT.Copy).then_inc(xm_sb, 1)
                for h in range(H):
                    act.wait_ge(conv_r, H * l + h + 1)
                    nc.scalar.activation(xcT[:, h, :], xcT[:, h, :], ACT.Silu).then_inc(xc_r, 1)
                for i in range(2 * NT):
                    act.wait_ge(tok_ps, 6 * l + i + 1)
                    dst = (v_gate, u_sb)[i // NT]
                    nc.scalar.activation(dst[:, i % NT, :], pb[:, (6, 7, 0, 1)[i], :], ACT.Gelu_apprx_tanh
                                         ).then_inc(gelu_r, 1)
                for t in range(NT):
                    act.wait_ge(tok_ps, 6 * l + 4 + t + 1)
                    nc.scalar.activation(o_sb[:, t, :], pb[:, 2 + t, :], ACT.Sigmoid).then_inc(o_r, 1)
                for i in range(2):
                    act.wait_ge(qkv_ps, 8 * l + 4 + i + 1)
                    nc.scalar.activation(vT[:, 2 * i:2 * i + 2, :], pb[:, i, :]
                                         .rearrange("p (h s) -> p h s", h=2), ACT.Copy).then_inc(vT_r, 1)
                act.wait_ge(absf_r, l + 1)
                link(nc.scalar.activation(gate_e, gate_e, ACT.Exp, scale=-1.0))
                nc.scalar.activation(gate_e, gate_e, ACT.Ln, bias=1.0).then_inc(ln_r, 1)
                for t in range(NT):
                    act.wait_ge(yg_r, NT * l + t + 1)
                    link(nc.scalar.activation(u_sb[:, t, :], v_gate[:, t, :], ACT.Square,
                                              accum_out=yss[:, t:t + 1]))
                nc.scalar.activation(yss, yss, ACT.Copy).then_inc(yss_r, 1)
                act.wait_ge(yrstd_r, l + 1)
                for t in range(NT):
                    nc.scalar.activation(v_gate[:, t, :], v_gate[:, t, :], ACT.Copy,
                                         scale=yrstd[:, t:t + 1]).then_inc(ygs_r, 1)
                act.wait_ge(aT_ps, l + 1)
                nc.scalar.activation(floorT.rearrange("p h t -> p t h"), pb[:, 5, 64:64 + NT * H]
                                     .rearrange("p (t h) -> p t h", t=NT), ACT.Exp).then_inc(floor_r, 1)
                for i in range(2):
                    act.wait_ge(arg_r, 2 * l + i + 1)
                    nc.scalar.activation(wS[:, 2 * i:2 * i + 2, :], wS[:, 2 * i:2 * i + 2, :], ACT.Exp
                                         ).then_inc(wexp_r, 1)
                for i in range(2):
                    act.wait_ge(ygT_ps, 2 * l + i + 1)
                    for g in range(2):
                        nc.scalar.activation(yT[:, H + 2 * i + g, :], pb[:, 2 + i, 256 * g:256 * g + 256],
                                             ACT.Copy, scale=col("gm_out_g", l * H + 2 * i + g)
                                             ).then_inc(ygT_r, 1)

            mixer(0)
            norm(1)
            for q in range(2 * ND):
                act.wait_ge(up_ps, q + 1)
                if q >= 2:
                    act.wait_ge(g_r, q - 1)
                r = min(P, DFF - q * P)
                nc.scalar.activation(d_sil[0:r, q % 2, :], pb[0:r, q % 4, 0:SEQ], ACT.Silu).then_inc(sil_r, 1)
            mixer(1)
            norm(3)

            act.wait_ge(gap_r, 1)
            nc.scalar.activation(p1, p1, ACT.Exp).then_inc(gexp_r, 1)
            def high13(j, c):
                n = (W13_MOE + c) % R13
                act.wait_ge(w13_rdy[n], j * (32 * 2 * NE // R13) + 32 * ((W13_MOE + c) // R13 + 1))
                act.wait_ge(s13_used, j * (2 * NE) + (c + 1))
                nc.scalar.activation(s13h[:, c % 2], w13_wide[n], ACT.Copy).then_inc(w13_hi, 1)

            def high2(j, u):
                n = (W2_MOE + u) % R2
                act.wait_ge(w2_rdy[n], j * (32 * NE // R2) + 32 * ((W2_MOE + u) // R2 + 1))
                act.wait_ge(s2_used, j * NE + (u + 1))
                nc.scalar.activation(s2h[:], w2[n][:], ACT.Copy).then_inc(w2_hi, 1)

            def gathered_high(j, i):
                act.wait_ge(xg_r, j * 2 + (i + 1))
                nc.scalar.activation(xsel_h[:, 4 * i:4 * i + 4, :], x_gain[:, 4 * i:4 * i + 4, :], ACT.Copy
                                     ).then_inc(xh_r, 1)

            high13(0, 0)
            high13(0, 1)
            gathered_high(0, 0)
            gathered_high(0, 1)
            act.wait_ge(route_r, 1)
            last_step = act.value_load(last_ij[0:1, 0:1], min_val=E - 1, max_val=NJ - 1)

            def steps_of(j, last):
                for u in range(NE):
                    if u < NE - 1:
                        high13(j, 2 * u + 2)
                    elif not last:
                        high13(j + 1, 0)
                    act.wait_ge(s13_used, j * (2 * NE) + (2 * u + 4))
                    if u >= 2:
                        act.wait_ge(eg_r, j * NE + (u - 1))
                    nc.scalar.activation(m_sil[:, u % 2, :], pb[:, u % 2, 0:UF], ACT.Silu).then_inc(esil_r, 1)
                    if u < NE - 1:
                        high13(j, 2 * u + 3)
                    elif not last:
                        high13(j + 1, 1)
                    high2(j, u)
                    act.wait_ge(egT_ps, j * NE + (u + 1))
                    nc.scalar.activation(gT_h[:], pb[:, 6, 0:2 * PASS].rearrange("p (b s) -> p b s", b=2),
                                         ACT.Copy).then_inc(gTh_r, 1)
                    if u == 0:
                        act.wait_ge(ohT_ps, j + 1)
                        nc.scalar.activation(onehotT, pb[:, 7, 0:NT * P].rearrange("p (t c) -> p t c", t=NT),
                                             ACT.Copy).then_inc(ohT_r, 1)
                gathered_high(j + 1, 0)
                gathered_high(j + 1, 1)
                act.wait_ge(s2_used, (j + 1) * NE + 1)
                nc.scalar.activation(y_sb[:, 0:512], pb[:, 4, :], ACT.Copy).then_inc(y_a, 1)

            with act.Fori(0, last_step) as j:
                steps_of(j, False)
            steps_of(last_step, True)
            act.wait_ge(s_dve_done, 1)
            link(nc.scalar.activation(xs[:, 0, :], x_sb[:, 0, :], ACT.Square, accum_out=ss[:, 0:1]))
            nc.scalar.activation(ss[:, 0:1], ss[:, 0:1], ACT.Copy).then_inc(sq_a, 1)

        @block.vector
        def _(dve):
            links = [0]

            def link(ins):
                links[0] += 1
                ins.then_inc(dve_chain, 1)
                dve.wait_ge(dve_chain, links[0])

            V = nc.vector

            def variance(n):
                link(V.tensor_tensor_reduce(out=xs[:, 1, :], in0=x_sb[:, 1, :], in1=x_sb[:, 1, :],
                                            scale=1.0, scalar=0.0, op0=ALU.mult, op1=ALU.add,
                                            accum_out=ss[:, 1:2]))
                dve.wait_ge(sq_a, n + 1)
                V.tensor_scalar(var[:], ss[:], 1.0 / D, EPS, ALU.mult, ALU.add).then_inc(var_r, 1)

            def norm(n):
                if n == 0:
                    dve.wait_ge(s_x, 16)
                variance(n)
                dve.wait_ge(rstd_r, n + 1)
                V.tensor_scalar(xs[:, 1, :], x_sb[:, 1, :], rstd[:, 1:2], None, ALU.mult).then_inc(xs_d, 1)
                if n == 0:
                    dve.wait_ge(s_prm_ps, 1)
                    V.tensor_copy(prmT[:], pb[:, 7, 0:NROWS]).then_inc(s_prmT, 1)
                    dve.wait_ge(s_prmT, 1)
                g, l = ("ffn_norm_g", "mix_norm_g")[n % 2 == 0], n // 2
                for i in (0, 2):
                    dve.wait_ge(hT_ps, 4 * n + i + 1)
                    for k in (2 * i, 2 * i + 1):
                        V.tensor_scalar(hT[:, k, :], pb[:, i, 256 * (k % 2):256 * (k % 2) + 256],
                                        col(g, l * KD + k), None, ALU.mult).then_inc(hT_d, 1)

            def mixer(l):
                norm(2 * l)
                V.memset(xmT[:, :, 0:CW - 1], 0.0).then_inc(s_pad, 1)
                V.memset(v_tok[:, :, :, DH:DH + 1], 1.0).then_inc(s_vone, 1)
                dve.wait_ge(wspT_ps, l + 1)
                link(V.tensor_copy(wspT[:], pb[:, 6, :].rearrange("p (g i) -> p g i", g=H)))
                V.memset(wspT[CHUNK:P, :, 0:CHUNK], 0.0).then_inc(wspT_r, 1)
                dve.wait_ge(s_pad, l + 1)
                for h in range(H):
                    dve.wait_ge(xm_sb, 2 * l + h // 2 + 1)
                    tap = lambda j: col("conv_w", (l * CW + j) * H + h)
                    link(V.tensor_scalar(xcT[:, h, :], xmT[:, h, 0:SEQ], tap(0), col("conv_b", l * H + h),
                                         ALU.mult, ALU.add))
                    for j in range(1, CW):
                        ins = V.scalar_tensor_tensor(out=xcT[:, h, :], in0=xmT[:, h, j:j + SEQ],
                                                     scalar=tap(j), in1=xcT[:, h, :],
                                                     op0=ALU.mult, op1=ALU.add)
                        if j < CW - 1:
                            link(ins)
                    ins.then_inc(conv_r, 1)
                for t in range(NT):
                    dve.wait_ge(gelu_r, 4 * l + t + 1)
                    link(V.bn_stats(gstats[:, t, :], v_gate[:, t, :]))
                    link(V.bn_aggr(gmv[:, t, :], gstats[:, t, :]))
                V.tensor_scalar(gvar, gmv[:, :, 1], EPS, None, ALU.add).then_inc(gvar_r, 1)
                dve.wait_ge(grstd_r, l + 1)
                for t in range(NT):
                    V.tensor_scalar(v_gate[:, t, :], v_gate[:, t, :], gmv[:, t, 0:1], grstd[:, t:t + 1],
                                    ALU.subtract, ALU.mult).then_inc(vn_r, 1)
                for i in range(4):
                    dve.wait_ge(qkv_ps, 8 * l + i + 1)
                    V.tensor_copy((qT, kT)[i // 2][:, 2 * (i % 2):2 * (i % 2) + 2, :], pb[:, 4 + i, :]
                                  .rearrange("p (h s) -> p h s", h=2)).then_inc(qk_r, 1)
                dve.wait_ge(s_vone, l + 1)
                for t in range(NT):
                    dve.wait_ge(qkv_ps, 8 * l + 6 + t + 1)
                    V.tensor_copy(v_tok[:, t, :, 0:DH], pb[:, 2 + t, :].rearrange("p (h c) -> p h c", h=H)
                                  ).then_inc(vt_r, 1)
                dve.wait_ge(gate_ps, l + 1)
                V.tensor_copy(g_tok, pb[:, 4, 0:NT * 2 * H].rearrange("p (t c) -> p t c", t=NT)
                              ).then_inc(gate_r, 1)
                dve.wait_ge(gateT_ps, l + 1)
                bi, bf = bif[:, l, 0:1], bif[:, l, 1:2]
                link(V.tensor_scalar(run_b, pb[0:H, 5, 256:512], bf, None, ALU.add))
                V.scalar_tensor_tensor(out=gate_e, in0=run_b, scalar=-1.0, in1=run_b,
                                       op0=ALU.mult, op1=ALU.max).then_inc(absf_r, 1)
                link(V.tensor_scalar(lf_min, run_b, 0.0, None, ALU.min))
                dve.wait_ge(ln_r, l + 1)
                link(V.tensor_tensor(gate_e, lf_min, gate_e, ALU.subtract))
                link(V.tensor_tensor_scan(run_b, ones_pp[0:H, 0:1].to_broadcast((H, SEQ)), gate_e, 0.0, ALU.mult, ALU.add))
                link(V.scalar_tensor_tensor(out=a_row, in0=pb[0:H, 5, 0:256], scalar=bi, in1=run_b,
                                            op0=ALU.add, op1=ALU.subtract))
                link(V.tensor_tensor_scan(run_m, a_row, a_row, 0.0, ALU.max, ALU.max))
                V.tensor_scalar(neg_m, run_m, -1.0, None, ALU.mult)
                V.scalar_tensor_tensor(out=neg_stab, in0=run_b, scalar=-1.0, in1=run_m,
                                       op0=ALU.mult, op1=ALU.subtract).then_inc(row_r, 1)
                for t in range(NT):
                    dve.wait_ge(sv_ps, NT * l + t + 1)
                    dve.wait_ge(gelu_r, 4 * l + 4)
                    for g in range(H):
                        c = slice(g * P, (g + 1) * P)
                        ins = V.scalar_tensor_tensor(out=v_gate[:, t, c], in0=pb[:, 6 + t, c],
                                                     scalar=col("b_sp", l * H + g), in1=u_sb[:, t, c],
                                                     op0=ALU.add, op1=ALU.mult)
                    ins.then_inc(yg_r, 1)
                dve.wait_ge(aT_ps, l + 1)
                link(V.tensor_copy(aT, pb[:, 4, 32:32 + NT * H].rearrange("p (t h) -> p t h", t=NT)))
                for i in range(2):
                    dve.wait_ge(mb_ps, 2 * l + i + 1)
                    for h in (2 * i, 2 * i + 1):
                        m = pb[:, 6 + i, 256 * (h % 2):256 * (h % 2) + 256]
                        V.tensor_scalar(wS[:, h, 0:256], m, aT[:, 0, h:h + 1], 0.0, ALU.add, ALU.min)
                        ins = V.tensor_scalar(wS[:, h, 256:384], m[:, P:], aT[:, 1, h:h + 1], 0.0,
                                              ALU.add, ALU.min)
                    ins.then_inc(arg_r, 1)
                dve.wait_ge(yss_r, l + 1)
                V.tensor_scalar(yvar, yss, 1.0 / MW, EPS, ALU.mult, ALU.add).then_inc(yvar_r, 1)
                dve.wait_ge(wmask_r, 2 * (l + 1))
                for h in range(H):
                    dve.wait_ge(sc_ps, H * l + h + 1)
                    V.scalar_tensor_tensor(out=wS[:, h, :], in0=pb[:, h, 0:384], scalar=SCALE,
                                           in1=wS[:, h, :], op0=ALU.mult, op1=ALU.mult).then_inc(sT_r, 1)
                dve.wait_ge(num_ps, H * (l + 1))
                dve.wait_ge(floor_r, l + 1)
                nums = pb[:, 4:8, :].rearrange("p h (t c) -> p h t c", t=NT)
                link(V.tensor_copy(rden, nums[:, :, :, DH]))
                link(V.scalar_tensor_tensor(out=den, in0=rden, scalar=-1.0, in1=rden,
                                            op0=ALU.mult, op1=ALU.max))
                link(V.tensor_tensor(den, den, floorT, ALU.max))
                link(V.reciprocal(rden, den))
                dve.wait_ge(o_r, NT * (l + 1))
                for h in range(H):
                    for t in range(NT):
                        link(V.scalar_tensor_tensor(out=hm[:, t, h * DH:(h + 1) * DH],
                                                    in0=nums[:, h, t, 0:DH], scalar=rden[:, h, t:t + 1],
                                                    in1=o_sb[:, t, h * DH:(h + 1) * DH],
                                                    op0=ALU.mult, op1=ALU.mult))
                        link(V.bn_stats(stats[:, h, t, :], hm[:, t, h * DH:(h + 1) * DH]))
                        link(V.bn_aggr(mv[:, h, t, :], stats[:, h, t, :]))
                V.tensor_scalar(hvar, mv.rearrange("p h t c -> p (h t) c")[:, :, 1], EPS, None, ALU.add
                                ).then_inc(hvar_r, 1)
                dve.wait_ge(hrstd_r, l + 1)
                for h in range(H):
                    for t in range(NT):
                        c = slice(h * DH, (h + 1) * DH)
                        ins = V.tensor_scalar(hm[:, t, c], hm[:, t, c], mv[:, h, t, 0:1],
                                              hrstd[:, h * NT + t:h * NT + t + 1], ALU.subtract, ALU.mult)
                    ins.then_inc(hm_r, 1)
                dve.wait_ge(skip_r, l + 1)
                for h in range(H):
                    dve.wait_ge(hmT_ps, 2 * l + h // 2 + 1)
                    V.scalar_tensor_tensor(out=yT[:, h, :], in0=pb[:, h // 2, 256 * (h % 2):256 * (h % 2) + 256],
                                           scalar=col("mh_norm_g", l * H + h), in1=xcT[:, h, :],
                                           op0=ALU.mult, op1=ALU.add).then_inc(ymT_r, 1)
                residual(wo_ps, 4 * l, n=2 * l + 1)

            def residual(ready, base, n):
                for i in range(4):
                    half, t = i // 2, i % 2
                    dve.wait_ge(ready, base + i + 1)
                    c = slice(half * 512, half * 512 + 512)
                    ins = V.tensor_tensor(x_sb[:, t, c], x_sb[:, t, c], pb[:, 4 + i, :], ALU.add)
                    ins.then_inc(x_upd, 1)
                dve.wait_ge(x_upd, 4 * n)

            mixer(0)
            norm(1)
            for q in range(2 * ND):
                dve.wait_ge(sil_r, q + 1)
                r = min(P, DFF - q * P)
                V.tensor_tensor(d_g[0:r, q % 4, :], d_sil[0:r, q % 2, :], pb[0:r, q % 4, SEQ:2 * SEQ],
                                ALU.mult).then_inc(g_r, 1)
            residual(down_ps, 0, 2)
            mixer(1)
            norm(3)

            dve.wait_ge(lg_ps, 1)
            link(V.tensor_copy(logits, pb[:, 4, 0:NT * E].rearrange("p (t e) -> p t e", t=NT)))
            for t in range(NT):
                link(V.max(top[:, t, :], logits[:, t, :]))
                link(V.max_index(top_i[:, t, :], top[:, t, :], logits[:, t, :]))
            link(V.tensor_copy(top_fi, top_i[:]))
            for t in range(NT):
                V.tensor_scalar(oh0[:, t, :], expert_no[:, t, :], top_fi[:, t, 0:1], None, ALU.is_equal)
                link(V.tensor_scalar(oh1[:, t, :], expert_no[:, t, :], top_fi[:, t, 1:2], None, ALU.is_equal))
            V.tensor_tensor(picked, oh0, oh1, ALU.add).then_inc(pick_r, 1)
            link(V.tensor_tensor(p1, top[:, :, 1], top[:, :, 0], ALU.subtract))
            V.tensor_copy(p1, p1).then_inc(gap_r, 1)
            dve.wait_ge(gexp_r, 1)
            link(V.tensor_scalar(pden, p1, 1.0, None, ALU.add))
            link(V.reciprocal(p0, pden))
            link(V.tensor_tensor(p1, p1, p0, ALU.mult))
            for t in range(NT):
                link(V.tensor_scalar(oh0[:, t, :], oh0[:, t, :], p0[:, t:t + 1], None, ALU.mult))
                link(V.scalar_tensor_tensor(out=weight[:, t, :], in0=oh1[:, t, :], scalar=p1[:, t:t + 1],
                                            in1=oh0[:, t, :], op0=ALU.mult, op1=ALU.add))
            dve.wait_ge(rank_ps, 1)
            link(V.scalar_tensor_tensor(out=rank, in0=pb[:, 5, 0:NT * E].rearrange("p (t e) -> p t e", t=NT),
                                        scalar=1.0, in1=picked, op0=ALU.add, op1=ALU.mult))
            V.memset(slot_of[:, NJ, :], -1.0)
            for p in range(NJ // E):
                js = slice(p * E, (p + 1) * E)
                V.tensor_scalar(slot_of[:, js, :].rearrange("p e t -> p t e"), rank, -1.0 - p * PASS, None, ALU.add)
                V.tensor_copy(comb[:, js, :].rearrange("p e t -> p t e"), weight)
            link(V.reduce_max(last_f[0:1, 0:1], pb[0:1, 5, 32:32 + E], AX.X))
            link(V.tensor_scalar(last_f[0:1, 1:2], last_f[0:1, 0:1], float(PASS), float(E), ALU.is_gt, ALU.mult))
            link(V.tensor_scalar(last_f[0:1, 1:2], last_f[0:1, 1:2], float(E - 1), None, ALU.add))
            V.tensor_copy(last_ij[:], last_f[0:1, 1:2]).then_inc(route_r, 1)
            dve.wait_ge(route_r, 1)

            last_step = dve.value_load(last_ij[0:1, 0:1], min_val=E - 1, max_val=NJ - 1)
            gain = prmT[:, ROWS["ffn_norm_g"][0] + KD:ROWS["ffn_norm_g"][0] + 2 * KD].unsqueeze(2)\
                .to_broadcast((P, KD, PASS))

            def make_onehot(j):
                for t in range(NT):
                    slots = slot_of[:, j, t:t + 1] if isinstance(j, int) else slot_of[:, bass.ds(j, 1), t]
                    ins = V.tensor_scalar(onehot[:, t], slot_no[:], slots, None, ALU.is_equal)
                ins.then_inc(oh_r, 1)

            def gathered(j, i):
                dve.wait_ge(gx_ps, j * 2 + (i + 1))
                ks = slice(4 * i, 4 * i + 4)
                V.tensor_tensor(x_gain[:, ks, :], pb[:, i, :].rearrange("p (k s) -> p k s", k=4),
                                gain[:, ks, :], ALU.mult).then_inc(xg_r, 1)
                dve.wait_ge(xh_r, j * 2 + (i + 1))
                V.tensor_tensor(xsel_l[:, ks, :], x_gain[:, ks, :], xsel_h[:, ks, :].bitcast(fp32),
                                ALU.subtract).then_inc(xsel_r, 1)

            def low13(j, c):
                dve.wait_ge(w13_hi, j * (2 * NE) + (c + 1))
                V.tensor_tensor(s13l[:, c % 2], w13_wide[(W13_MOE + c) % R13], s13h[:, c % 2].bitcast(fp32),
                                ALU.subtract).then_inc(w13_lo, 1)

            def low2(j, u):
                dve.wait_ge(w2_hi, j * NE + (u + 1))
                V.tensor_tensor(s2l[:], w2[(W2_MOE + u) % R2][:], s2h[:].bitcast(fp32),
                                ALU.subtract).then_inc(w2_lo, 1)

            low13(0, 0)
            low13(0, 1)
            make_onehot(0)
            gathered(0, 0)
            gathered(0, 1)
            dve.sem_inc(x_moe, 1)

            def steps_of(j, last):
                for u in range(NE):
                    if u < NE - 1:
                        low13(j, 2 * u + 2)
                    elif not last:
                        low13(j + 1, 0)
                    dve.wait_ge(esil_r, j * NE + (u + 1))
                    if u >= 2:
                        dve.wait_ge(egT_ps, j * NE + (u - 1))
                    V.tensor_tensor(m_g[:, u % 2, :], m_sil[:, u % 2, :], pb[:, u % 2, UF:2 * UF], ALU.mult
                                    ).then_inc(eg_r, 1)
                    if u < NE - 1:
                        low13(j, 2 * u + 3)
                    elif not last:
                        low13(j + 1, 1)
                    low2(j, u)
                    dve.wait_ge(gTh_r, j * NE + (u + 1))
                    V.tensor_tensor(gT_l[:], pb[:, 6, 0:2 * PASS].rearrange("p (b s) -> p b s", b=2),
                                    gT_h[:].bitcast(fp32), ALU.subtract).then_inc(egT_r, 1)
                    if u == NE // 2:
                        dve.wait_ge(ohT_ps, j + 1)
                        make_onehot(j + 1)
                gathered(j + 1, 0)
                gathered(j + 1, 1)
                dve.wait_ge(s2_used, (j + 1) * NE + 1)
                V.tensor_copy(y_sb[:, 512:], pb[:, 5, :]).then_inc(y_d, 1)
                for t in range(NT):
                    dve.wait_ge(sct_ps, j * NT + (t + 1))
                    for half in range(2):
                        c = slice(half * 512, half * 512 + 512)
                        ins = V.scalar_tensor_tensor(out=x_sb[:, t, c], in0=pb[:, (2, 6)[t] + half, :],
                                                     scalar=comb[:, bass.ds(j, 1), t], in1=x_sb[:, t, c],
                                                     op0=ALU.mult, op1=ALU.add)
                    ins.then_inc(x_moe, 1)

            with dve.Fori(0, last_step) as j:
                steps_of(j, False)
            steps_of(last_step, True)
            dve.drain().then_inc(s_dve_done, 1)
            dve.wait_ge(s_dve_done, 1)
            variance(4)
            dve.wait_ge(rstd_r, 5)
            dve.wait_ge(s_fgb, 16)
            for t in range(NT):
                V.scalar_tensor_tensor(out=x_sb[:, t, :], in0=x_sb[:, t, :], scalar=rstd[:, t:t + 1],
                                       in1=fgb, op0=ALU.mult, op1=ALU.mult).then_inc(fin_r, 1)

        @block.tensor
        def _(pe):
            mm = nc.tensor.matmul

            def ring_ready(g):
                for n in (2 * g, 2 * g + 1):
                    pe.wait_ge(w13_rdy[n % R13], 32 * (n // R13 + 1))
                return lambda k: w13_wide[(2 * g + k // KH) % R13][:, k % KH, :]

            def norm(n):
                pe.wait_ge(xs_a, n + 1)
                pe.wait_ge(xs_d, n + 1)
                for k in range(KD):
                    for t in range(NT):
                        ins = nc.tensor.transpose(pb[:, k // 2, 256 * (k % 2) + P * t:256 * (k % 2) + P * t + P],
                                                  xs[:, t, k * P:(k + 1) * P], ident[:])
                    if k % 2:
                        ins.then_inc(hT_ps, 1)

            def hT_ready(n, k):
                i = 2 * (k // 4) + k % 2
                pe.wait_ge((hT_d, hT_a)[k // 2 % 2], 4 * n + i + 1)

            def mixer(l):
                norm(2 * l)
                pe.wait_ge(s_wsp, 16 * (l + 1))
                for g in range(H):
                    ins = nc.tensor.transpose(pb[:, 6, g * P:(g + 1) * P], wsp[:, g, :], ident[:])
                ins.then_inc(wspT_ps, 1)
                w = ring_ready(w13_item(l, 0))
                for h in range(H):
                    for k in range(KD):
                        if h == 0:
                            hT_ready(2 * l, k)
                        ins = mm(pb[:, 4 + h // 2, 256 * (h % 2):256 * (h % 2) + 256],
                                 w(k)[:, h * P:(h + 1) * P], hT[:, k, :], start=k == 0, stop=k == KD - 1)
                    if h % 2:
                        ins.then_inc(xm_ps, 1)
                for i in range(3):
                    w = ring_ready(w13_item(l, 1 + i))
                    if i == 0:
                        pe.wait_ge(wspT_r, l + 1)
                    for t in range(NT):
                        bank = pb[:, (6, 7, 0, 1, 2, 3)[2 * i + t], :]
                        for k in range(KD):
                            ins = mm(bank, hT[:, k, t * P:(t + 1) * P], w(k), start=k == 0, stop=k == KD - 1)
                        ins.then_inc(tok_ps, 1)
                pe.wait_ge(s_wqkv, 48 * (l + 1))
                for i in range(3):
                    for h in range(H):
                        if h % 2 == 0:
                            if i == 0:
                                pe.wait_ge(xm_sb, 2 * l + h // 2 + 1)
                            elif i == 1:
                                pe.wait_ge(gelu_r, 4 * l + h // 2 + 1)
                            else:
                                pe.wait_ge(gelu_r, 4 * l + 2 + h // 2 + 1)
                        if i == 0:
                            pe.wait_ge(xc_r, H * l + h + 1)
                        src = xmT[:, h, CW - 1:] if i == 2 else xcT[:, h, :]
                        ins = mm(pb[:, (4, 6, 0)[i] + h // 2, 256 * (h % 2):256 * (h % 2) + 256],
                                 wqkv[:, i, h, :], src, start=True, stop=True)
                        if h % 2:
                            ins.then_inc(qkv_ps, 1)
                for t in range(NT):
                    pe.wait_ge(o_r, NT * l + t + 1)
                    for h in range(H):
                        ins = mm(pb[:, 2 + t, h * DH:(h + 1) * DH],
                                 xmT[:, h, CW - 1 + t * P:CW - 1 + (t + 1) * P], wqkv[:, 2, h, :],
                                 start=True, stop=True)
                    ins.then_inc(qkv_ps, 1)
                pe.wait_ge(qk_r, 4 * (l + 1))
                pe.wait_ge(vT_r, 2 * (l + 1))
                pe.wait_ge(s_small, 64 + 32 * l)
                for t in range(NT):
                    for c in range(3 * H):
                        src = (qT, kT, vT)[c // H][:, c % H, t * P:(t + 1) * P]
                        ins = mm(pb[:, 4, t * 2 * H:(t + 1) * 2 * H], src, wif[:, c, :],
                                 start=c == 0, stop=c == 3 * H - 1)
                ins.then_inc(gate_ps, 1)
                pe.wait_ge(gate_r, l + 1)
                for t in range(NT):
                    for f in range(2):
                        ins = nc.tensor.transpose(pb[0:H, 5, 256 * f + t * P:256 * f + (t + 1) * P],
                                                  g_tok[:, t, f * H:(f + 1) * H], ident[:])
                ins.then_inc(gateT_ps, 1)
                for t in range(NT):
                    pe.wait_ge(vg_r, NT * l + t + 1)
                    for g in range(H):
                        ins = mm(pb[:, 6 + t, g * P:(g + 1) * P], wspT[:, g, :],
                                 v_gate[:, t, g * P:(g + 1) * P], start=True, stop=True)
                    ins.then_inc(sv_ps, 1)
                pe.wait_ge(vt_r, NT * (l + 1))
                for h in range(H):
                    mm(pb[:, h, 0:256], kT[:, h, 0:P], qT[:, h, :], start=True, stop=True)
                    mm(pb[:, h, 256:384], kT[:, h, P:], qT[:, h, P:], start=True, stop=True).then_inc(sc_ps, 1)
                pe.wait_ge(row_r, l + 1)
                pe.wait_ge(yg_r, NT * (l + 1))
                for t in range(NT):
                    for i, r in enumerate((a_row, neg_stab)):
                        ins = nc.tensor.transpose(pb[:, 4 + i, 32 * (i + 1) + t * H:32 * (i + 1) + (t + 1) * H],
                                                  r[:, t * P:(t + 1) * P], ident[0:H, 0:H])
                ins.then_inc(aT_ps, 1)
                for h in range(H):
                    ins = mm(pb[:, 6 + h // 2, 256 * (h % 2):256 * (h % 2) + 256], sel[:, h, :], neg_m,
                             start=True, stop=True)
                    if h % 2:
                        ins.then_inc(mb_ps, 1)
                pe.wait_ge(arg_r, 2 * (l + 1))
                pe.wait_ge(floor_r, l + 1)
                for h in range(H):
                    pe.wait_ge(sT_r, H * l + h + 1)
                    n0, n1 = pb[:, 4 + h, 0:DH + 1], pb[:, 4 + h, 256:256 + DH + 1]
                    mm(n0, wS[:, h, 0:P], v_tok[:, 0, h, :], start=True, stop=True)
                    mm(n1, wS[:, h, P:2 * P], v_tok[:, 0, h, :], start=True, stop=False)
                    mm(n1, wS[:, h, 2 * P:3 * P], v_tok[:, 1, h, :], start=False, stop=True).then_inc(num_ps, 1)
                pe.wait_ge(ygs_r, NT * (l + 1))
                for g in range(H):
                    for t in range(NT):
                        ins = nc.tensor.transpose(pb[:, 2 + g // 2, 256 * (g % 2) + P * t:256 * (g % 2) + P * t + P],
                                                  v_gate[:, t, g * P:(g + 1) * P], ident[:])
                    if g % 2:
                        ins.then_inc(ygT_ps, 1)
                for h in range(H):
                    pe.wait_ge(hm_r, H * l + h + 1)
                    for t in range(NT):
                        ins = nc.tensor.transpose(pb[:, h // 2, 256 * (h % 2) + P * t:256 * (h % 2) + P * t + P],
                                                  hm[:, t, h * DH:(h + 1) * DH], ident[:])
                    if h % 2:
                        ins.then_inc(hmT_ps, 1)
                for half in range(2):
                    w = ring_ready(w13_item(l, 4 + half))
                    for t in range(NT):
                        for i in range(KD):
                            c = (i + H) % KD
                            if half == 0 and t == 0:
                                if c >= H:
                                    pe.wait_ge(ygT_r, H * l + c - H + 1)
                                else:
                                    pe.wait_ge(ymT_r, H * l + c + 1)
                            ins = mm(pb[:, 4 + 2 * half + t, :], yT[:, c, t * P:(t + 1) * P], w(c),
                                     start=i == 0, stop=i == KD - 1)
                        ins.then_inc(wo_ps, 1)

            pe.wait_ge(s_const, 1)
            pe.wait_ge(s_prm, 16 * 8)
            nc.tensor.transpose(pb[:, 7, 0:NROWS], prm[:], ident[0:NROWS, 0:NROWS]).then_inc(s_prm_ps, 1)

            mixer(0)

            norm(1)
            pe.wait_ge(hT_d, 8)
            pe.wait_ge(hT_a, 8)

            def dense_down(q):
                r = min(P, DFF - q * P)
                u, b = q // 2, q % 2
                if b == 0:
                    blocks = 1 + (DFF > u * UF + P)
                    full = 16 * 2 * (u // R2)
                    pe.wait_ge(w2_rdy[u % R2], full + 16 * blocks)
                pe.wait_ge(g_r, q + 1)
                for half in range(2):
                    for t in range(NT):
                        ins = mm(pb[:, 4 + 2 * half + t, :], d_g[0:r, q % 4, t * P:(t + 1) * P],
                                 w2[u % R2][0:r, b, half * 512:half * 512 + 512],
                                 start=q == 0, stop=q == 2 * ND - 1)
                        if q == 2 * ND - 1:
                            ins.then_inc(down_ps, 1)
                if b == 1 and u < ND - 1:
                    ins.then_inc(w2_used, 1)

            for q in range(2 * ND):
                u, b = q // 2, q % 2
                w = ring_ready(w13_item(0, MIX + u))
                r = min(P, DFF - q * P)
                if q >= 4:
                    pe.wait_ge(g_r, q - 3)
                for k2 in range(2):
                    for k in range(KD):
                        ins = mm(pb[0:r, q % 4, k2 * SEQ:(k2 + 1) * SEQ], w(k)[:, k2 * UF + b * P:k2 * UF + b * P + r],
                                 hT[:, k, :], start=k == 0, stop=k == KD - 1)
                ins.then_inc(up_ps, 1)
                if q >= 2:
                    dense_down(q - 2)
            dense_down(2 * ND - 2)
            dense_down(2 * ND - 1)

            mixer(1)

            norm(3)
            for t in range(NT):
                for k in range(KD):
                    if t == 0:
                        hT_ready(3, k)
                    ins = mm(pb[:, 4, t * E:(t + 1) * E], hT[:, k, t * P:(t + 1) * P], wr[:, k, :],
                             start=k == 0, stop=k == KD - 1)
            ins.then_inc(lg_ps, 1)
            pe.wait_ge(pick_r, 1)
            mm(pb[:, 5, 0:E], before[:], picked[:, 0, :], start=True, stop=True)
            mm(pb[:, 5, E:2 * E], ones_pp[:], picked[:, 0, :], start=True, stop=False)
            mm(pb[:, 5, E:2 * E], before[:], picked[:, 1, :], start=False, stop=True)
            for t in range(NT):
                ins = mm(pb[0:1, 5, 32:32 + E], ones_pp[:, 0:1], picked[:, t, :], start=t == 0, stop=t == NT - 1)
            ins.then_inc(rank_ps, 1)

            pe.wait_ge(route_r, 1)
            last_step = pe.value_load(last_ij[0:1, 0:1], min_val=E - 1, max_val=NJ - 1)

            def gather(j, i):
                if i == 0:
                    pe.wait_ge(oh_r, j + 1)
                for k in range(4 * i, 4 * i + 4):
                    for t in range(NT):
                        ins = mm(pb[:, i, (k % 4) * PASS:(k % 4 + 1) * PASS],
                                 xs[:, t, k * P:(k + 1) * P], onehot[:, t, :],
                                 start=t == 0, stop=t == NT - 1)
                ins.then_inc(gx_ps, 1)

            pe.sem_inc(s13_used, 2)
            pe.sem_inc(s2_used, 1)
            gather(0, 0)
            gather(0, 1)
            with pe.Fori(0, last_step + 1) as j:
                def up(c):
                    pe.wait_ge(w13_lo, j * (2 * NE) + (c + 1))
                    u = c // 2
                    if c == 0:
                        pe.wait_ge(xsel_r, j * 2 + 2)
                    if u >= 2 and c % 2 == 0:
                        pe.wait_ge(eg_r, j * NE + (u - 1))
                    for k in range(KH):
                        x = KH * (c % 2) + k
                        for i, (a, w) in enumerate(((xsel_h, s13h), (xsel_h, s13l), (xsel_l, s13h))):
                            ins = mm(pb[:, u % 2, :], a[:, x, :], w[:, c % 2, k, :],
                                     start=x == 0 and i == 0, stop=x == KD - 1 and i == 2)
                    ins.then_inc(s13_used, 1)

                def turn(u):
                    pe.wait_ge(eg_r, j * NE + (u + 1))
                    for b in range(2):
                        ins = nc.tensor.transpose(pb[:, 6, b * P:(b + 1) * P],
                                                  m_g[:, u % 2, b * P:(b + 1) * P], ident[:])
                    ins.then_inc(egT_ps, 1)

                def down(u):
                    pe.wait_ge(w2_lo, j * NE + (u + 1))
                    pe.wait_ge(egT_r, j * NE + (u + 1))
                    for b in range(2):
                        for i, (a, w) in enumerate(((gT_h, s2h), (gT_h, s2l), (gT_l, s2h))):
                            for half in range(2):
                                ins = mm(pb[:, 4 + half, :], a[:, b, :], w[:, b, half * 512:(half + 1) * 512],
                                         start=u == 0 and b == 0 and i == 0,
                                         stop=u == NE - 1 and b == 1 and i == 2)
                    ins.then_inc(s2_used, 1)

                up(0)
                up(1)
                pe.wait_ge(x_moe, j * NT + 1)
                for t in range(NT):
                    ins = nc.tensor.transpose(pb[:, 7, t * P:(t + 1) * P], onehot[:, t, :], ident[:])
                ins.then_inc(ohT_ps, 1)
                for u in range(1, NE):
                    turn(u - 1)
                    up(2 * u)
                    up(2 * u + 1)
                    down(u - 1)
                turn(NE - 1)
                gather(j + 1, 0)
                gather(j + 1, 1)
                down(NE - 1)
                pe.wait_ge(y_a, j + 1)
                pe.wait_ge(y_d, j + 1)
                pe.wait_ge(ohT_r, j + 1)
                for t in range(NT):
                    for half in range(2):
                        ins = mm(pb[:, (2, 6)[t] + half, :], onehotT[:, t, :], y_sb[:, half * 512:(half + 1) * 512],
                                 start=True, stop=True)
                    ins.then_inc(sct_ps, 1)


_INS = ["x", "mix_norm_g", "w_in", "conv_w", "conv_b", "w_q", "w_k", "w_v", "w_if", "b_if", "skip_m",
        "mh_norm_g", "gm_v_g", "w_sp", "b_sp", "gm_out_g", "w_out", "ffn_norm_g",
        "dense_w1", "dense_w3", "dense_w2", "moe_router", "moe_w1", "moe_w3", "moe_w2", "final_norm_g"]


def kernel(**inputs):
    import numpy as _np
    import concourse.bacc as _bacc
    from concourse.bass_utils import run_bass_kernel_spmd as _run

    nc = _bacc.Bacc("TRN2", target_bir_lowering=False, num_devices=1)
    arrays, args = {}, []
    for name in _INS:
        a = _np.ascontiguousarray(inputs[name])
        arrays[f"in_{name}"] = a
        args.append(nc.dram_tensor(f"in_{name}", a.shape, mybir.dt.from_np(a.dtype), kind="ExternalInput").ap())
    args.append(nc.dram_tensor("out_0", (1, SEQ, D), fp32, kind="ExternalOutput").ap())
    trunk(nc, *args)
    r = _run(nc, [arrays], core_ids=[0])
    return r.results[0]["out_0"]
```

```python
import concourse.bass as bass
from concourse import mybir
from contextlib import ExitStack

fp32 = mybir.dt.float32
fp32r = mybir.dt.float32r
i32 = mybir.dt.int32
u32 = mybir.dt.uint32
ALU = mybir.AluOpType
ACT = mybir.ActivationFunctionType
AX = mybir.AxisListType

P = 128
SEQ, D, L = 256, 1024, 2
NT = SEQ // P
KD = D // P
H, DH = 4, 128
MW = H * DH
CW = 4
CHUNK = 64
DFF, DFE, E = 2752, 3584, 8
EPS = 1e-6
SCALE = DH ** -0.5
UF = 256
ND = -(-DFF // UF)
NE = DFE // UF
PASS = 128
NJ = E * (SEQ // PASS)
KH = KD // 2
R13, R2 = 7, 4
MIX = 6
W13_MOE = 2 * (2 * MIX + ND)
W2_MOE = 2 * ND
ONEHOT_AT = 5

WIN_ORDER = [0, 3, 2, 1]

ROWS = {}
_at = 0
for _name, _n in (("mix_norm_g", L * KD), ("ffn_norm_g", L * KD), ("conv_w", L * CW * H),
                  ("conv_b", L * H), ("skip_m", L * H), ("mh_norm_g", L * H),
                  ("gm_out_g", L * H), ("b_sp", L * H)):
    ROWS[_name] = (_at, _n)
    _at += _n
NROWS = _at


def dense_width(u):
    return min(UF, DFF - u * UF)


def trunk(nc, x, mix_norm_g, w_in, conv_w, conv_b, w_q, w_k, w_v, w_if, b_if, skip_m,
          mh_norm_g, gm_v_g, w_sp, b_sp, gm_out_g, w_out, ffn_norm_g,
          dense_w1, dense_w3, dense_w2, moe_router, moe_w1, moe_w3, moe_w2,
          final_norm_g, out):
    ctx = ExitStack()
    with ctx:
        def sb(name, shape, dt=fp32):
            return ctx.enter_context(nc.sbuf_tensor(name, shape, dt))

        def sem(name):
            return ctx.enter_context(nc.semaphore(name))

        w13 = [sb(f"w13_{i}", [P, KH, 2, UF]) for i in range(R13)]
        w13_wide = [w[:].rearrange("p k w f -> p k (w f)") for w in w13]
        w2 = [sb(f"w2_{i}", [P, D]) for i in range(R2)]
        s13h = sb("s13h", [P, 2, KH, 2 * UF], fp32r)
        s13l = sb("s13l", [P, 2, KH, 2 * UF], fp32r)
        s2h = sb("s2h", [P, 2, D], fp32r)
        s2l = sb("s2l", [P, 2, D], fp32r)
        x_sb = sb("x_sb", [P, NT, D])
        xs = sb("xs", [P, NT, D])
        o_sb = xs[:, 0, :].rearrange("p (t c) -> p t c", t=NT)
        u_sb = xs[:, 1, :].rearrange("p (t c) -> p t c", t=NT)
        hT_h = sb("hT_h", [P, KD, SEQ], fp32r)
        hT_l = sb("hT_l", [P, KD, SEQ], fp32r)
        yT_h, yT_l = hT_h, hT_l
        xsel_h, xsel_l = hT_h[:, :, 0:PASS], hT_l[:, :, 0:PASS]
        wqkv = sb("wqkv", [P, 3, H, DH])
        wif = sb("wif", [P, 3 * H, 2 * H])
        bif = sb("bif", [H, L, 2])
        wspT = sb("wspT", [P, H, P])
        gvb = sb("gvb", [P, MW])
        wr = sb("wr", [P, KD, E])
        prm = sb("prm", [NROWS, P])
        prmT = sb("prmT", [P, NROWS])
        ident = sb("ident", [P, P])
        sel = sb("sel", [H, H, P])
        before = sb("before", [P, P])
        ones_pp = sb("ones_pp", [P, P])
        neg_half = sb("neg_half", [P, NT * H])
        slot_no = sb("slot_no", [P, PASS])
        expert_no = sb("expert_no", [P, NT, E])

        ss = sb("ss", [P, NT])
        var = sb("var", [P, NT])
        rstd = sb("rstd", [P, NT])

        ARENA = 9152
        arena = sb("arena", [P, ARENA])
        at = [0]

        def carve(n):
            at[0] += n
            assert at[0] <= ARENA, at[0]
            return arena[:, at[0] - n:at[0]]

        XP = SEQ + CW - 1
        wS_flat = carve(H * 384)
        wS = wS_flat.rearrange("p (h s) -> p h s", h=H)
        neg_m = carve(SEQ)[0:H, :]
        xmT = carve(H * XP).rearrange("p (h s) -> p h s", h=H)
        xcT = carve(H * SEQ).rearrange("p (h s) -> p h s", h=H)
        qT = carve(H * SEQ).rearrange("p (h s) -> p h s", h=H)
        kT = carve(H * SEQ).rearrange("p (h s) -> p h s", h=H)
        v_tok = carve(NT * H * (DH + 1)).rearrange("p (t h c) -> p t h c", t=NT, h=H)
        v_gate = carve(NT * MW).rearrange("p (t c) -> p t c", t=NT)
        wsp = v_gate.rearrange("p t c -> p (t c)")[:, 0:H * P].rearrange("p (g j) -> p g j", g=H)
        vT_hm = carve(H * SEQ)
        vT = vT_hm.rearrange("p (h s) -> p h s", h=H)
        hm = vT_hm.rearrange("p (t c) -> p t c", t=NT)
        diag = vT_hm[:, 0:NT * P].rearrange("p (t s) -> p t s", t=NT)
        g_tok = carve(NT * 2 * H).rearrange("p (t c) -> p t c", t=NT)
        aT = carve(NT * H).rearrange("p (t h) -> p t h", t=NT)
        floorT = carve(H * NT).rearrange("p (h t) -> p h t", t=NT)
        den = carve(H * NT).rearrange("p (h t) -> p h t", t=NT)
        rden = carve(H * NT).rearrange("p (h t) -> p h t", t=NT)
        stats = carve(H * NT * 6).rearrange("p (h t c) -> p h t c", h=H, t=NT)
        mv = carve(H * NT * 2).rearrange("p (h t c) -> p h t c", h=H, t=NT)
        hvar = carve(H * NT)
        hrstd = carve(H * NT)
        gstats = carve(NT * 6).rearrange("p (t c) -> p t c", t=NT)
        gmv = carve(NT * 2).rearrange("p (t c) -> p t c", t=NT)
        gvar, grstd, yss, yvar, yrstd = (carve(NT) for _ in range(5))
        lf_min, gate_e, run_b, a_row, run_m = (wS_flat[0:H, i * SEQ:(i + 1) * SEQ] for i in range(5))
        neg_stab = lf_min

        at[0] = 0
        d_sil = carve(2 * SEQ).rearrange("p (b s) -> p b s", b=2)
        d_g = carve(2 * SEQ).rearrange("p (b s) -> p b s", b=2)
        at[0] = 0
        onehot = carve(NT * PASS).rearrange("p (t c) -> p t c", t=NT)
        gainb = carve(D)
        m_sil = carve(2 * UF).rearrange("p (q f) -> p q f", q=2)
        m_g = carve(2 * UF).rearrange("p (q f) -> p q f", q=2)
        gT_h = sb("gT_h", [P, 2, SEQ], fp32r)
        gT_l = sb("gT_l", [P, 2, SEQ], fp32r)
        y_h, y_l = hT_h[:, :, PASS:SEQ], hT_l[:, :, PASS:SEQ]
        onehotT = gT_h[:, :, PASS:SEQ]
        wr_h, wr_l = (gT_l[:, i, PASS:PASS + KD * E].rearrange("p (k e) -> p k e", k=KD) for i in range(2))
        logitsT = carve(SEQ)[0:E, :]
        spare = sb("spare", [1, 1])
        fgb = carve(D)
        logits, oh0, oh1, picked, rank, weight = (
            carve(NT * E).rearrange("p (t e) -> p t e", t=NT) for _ in range(6))
        top = carve(NT * 8).rearrange("p (t e) -> p t e", t=NT)
        top_fi = carve(NT * 8).rearrange("p (t e) -> p t e", t=NT)
        p1, p0, pden = (carve(NT) for _ in range(3))
        slot_of = carve(NJ * NT).rearrange("p (j t) -> p j t", t=NT)
        comb = carve((NJ + 1) * NT).rearrange("p (j t) -> p j t", t=NT)
        top_i = sb("top_i", [P, NT, 8], u32)
        last_f = sb("last_f", [1, 2])
        last_ij = sb("last_ij", [1, 1], i32)

        def col(name, i):
            return prmT[:, ROWS[name][0] + i:ROWS[name][0] + i + 1]

        pb = ctx.enter_context(nc.psum_tensor("pb", [P, 8, 512], fp32))

        s_x = sem("x_loaded")
        s_prm = sem("params_loaded")
        s_wqkv = sem("wqkv_loaded")
        s_small = sem("small_loaded")
        s_wsp = sem("wsp_loaded")
        w13_rdy = [sem(f"w13_loaded_{i}") for i in range(R13)]
        w2_rdy = [sem(f"w2_loaded_{i}") for i in range(R2)]
        s_const = sem("constants_made")
        s_prm_ps = sem("params_transposed")
        s_prmT = sem("params_in_sbuf")
        s_pad = sem("conv_pad_made")
        s_vone = sem("value_ones_made")
        sq_a = sem("squares_summed_act")
        var_r = sem("variance_ready")
        rstd_r = sem("rstd_ready")
        diag_r = sem("diagonal_ready")
        xs_a = sem("xs_ready_act")
        xs_d = sem("xs_ready_dve")
        xs_p = sem("xs_ready_pool")
        s_gain = sem("gain_loaded")
        hT_ps = sem("hT_in_psum")
        hTh_r = sem("hT_high_ready")
        hTl_r = sem("hT_low_ready")
        x_upd = sem("x_updated")
        xm_ps = sem("xm_in_psum")
        xm_sb = sem("xm_ready")
        conv_r = sem("conv_ready")
        xc_r = sem("xc_ready")
        skip_r = sem("skip_ready")
        tok_ps = sem("tokenwise_proj_in_psum")
        gelu_r = sem("gelu_ready")
        o_r = sem("o_ready")
        qkv_ps = sem("qkv_in_psum")
        qk_r = sem("qk_ready")
        vT_r = sem("vT_ready")
        vt_r = sem("v_tok_ready")
        gate_ps = sem("gates_in_psum")
        gate_r = sem("gates_ready")
        gateT_ps = sem("gate_rows_in_psum")
        absf_r = sem("abs_forget_ready")
        ln_r = sem("softplus_ready")
        row_r = sem("gate_rows_ready")
        mb_ps = sem("running_max_broadcast")
        aT_ps = sem("a_columns_in_psum")
        floor_r = sem("floor_ready")
        arg_r = sem("weight_exponent_ready")
        wexp_r = sem("weights_exponentiated")
        wmask_r = sem("weights_masked")
        sc_ps = sem("scores_in_psum")
        sT_r = sem("weighted_scores_ready")
        num_ps = sem("numerators_in_psum")
        hvar_r = sem("head_variance_ready")
        hrstd_r = sem("head_rstd_ready")
        hm_r = sem("head_output_ready")
        hmT_ps = sem("head_output_transposed")
        wspT_ps = sem("wsp_transposed")
        wspT_r = sem("wspT_ready")
        gvar_r = sem("v_variance_ready")
        grstd_r = sem("v_rstd_ready")
        vn_r = sem("v_normalised")
        vg_r = sem("v_scaled")
        sv_ps = sem("gating_in_psum")
        yg_r = sem("gated_ready")
        yss_r = sem("gated_squares_summed")
        yvar_r = sem("gated_variance_ready")
        yrstd_r = sem("gated_rstd_ready")
        ygs_r = sem("gated_normalised")
        ygT_ps = sem("gated_transposed")
        ygTh_r = sem("gated_channels_high_ready")
        ygTl_r = sem("gated_channels_low_ready")
        ymT_r = sem("head_channels_ready")
        ymTh_r = sem("head_channels_high_ready")
        ymTl_r = sem("head_channels_low_ready")
        wo_ps = sem("mixer_output_in_psum")
        sil_r = sem("dense_silu_ready")
        g_r = sem("dense_product_ready")
        gh_r = sem("dense_product_high_ready")
        gl_r = sem("dense_product_low_ready")
        down_ps = sem("dense_down_in_psum")
        wrh_r = sem("router_high_ready")
        wrl_r = sem("router_low_ready")
        lgT_ps = sem("logit_rows_in_psum")
        lgT_r = sem("logit_rows_ready")
        lg_ps = sem("logits_in_psum")
        pick_r = sem("picked_ready")
        rank_ps = sem("ranks_in_psum")
        route_r = sem("routing_ready")
        oh_r = sem("onehot_ready")
        gx_ps = sem("gathered_in_psum")
        ohT_ps = sem("onehot_transposed")
        ohT_r = sem("onehotT_ready")
        xh_r = sem("gathered_high_ready")
        xsel_r = sem("gathered_ready")
        w13_hi = sem("w13_high_ready")
        w13_lo = sem("w13_low_ready")
        s13_used = sem("w13_parts_used")
        w2_hi = sem("w2_high_ready")
        w2_lo = sem("w2_low_ready")
        s2_used = sem("w2_parts_used")
        esil_r = sem("expert_silu_ready")
        eg_r = sem("expert_product_ready")
        egT_ps = sem("expert_product_transposed")
        gTh_r = sem("expert_productT_high_ready")
        egT_r = sem("expert_productT_ready")
        yh_r = sem("expert_output_high_ready")
        yl_r = sem("expert_output_low_ready")
        sct_ps = sem("scattered_in_psum")
        x_moe = sem("x_updated_by_expert")
        gap_r = sem("logit_gap_ready")
        gexp_r = sem("gate_exponential_ready")
        fin_r = sem("final_ready")
        s_fgb = sem("final_gain_loaded")
        s_out = sem("output_stored")
        dve_chain = sem("dve_chain")
        act_chain = sem("act_chain")
        pool_chain = sem("pool_chain")

        block = ctx.enter_context(nc.Block())

        def norm_bank(n):
            return 4 if n == 1 else 0

        def done2(m):
            return m + 3

        def done13(n):
            return n + 3

        def w13_item(l, i):
            return l * (MIX + ND) + i

        @block.sync
        def _(sp):
            def ring_slot(n):
                if n >= R13:
                    sp.wait_ge(w13_lo, n - R13 + 1)
                return n % R13

            def load_columns(g, w):
                for a in range(2):
                    n = 2 * g + a
                    sp.dma_start(w13_wide[ring_slot(n)], w[a * KH * P:(a + 1) * KH * P, :]
                                 .rearrange("(k p) f -> p k f", p=P)).then_inc(w13_rdy[n % R13], 32)

            def load_w_in(l, i):
                c = WIN_ORDER[i] * MW
                load_columns(w13_item(l, i), w_in[l, :, c:c + MW])

            def load_w_out(l):
                for i in range(4):
                    a, half = 1 - i // 2, i % 2
                    n = 2 * w13_item(l, 4) + i
                    sp.dma_start(w13_wide[ring_slot(n)],
                                 w_out[l, a * KH * P:(a + 1) * KH * P, half * 512:(half + 1) * 512]
                                 .rearrange("(k p) f -> p k f", p=P)).then_inc(w13_rdy[n % R13], 32)

            sp.dma_start(x_sb[:], x[0].rearrange("(t p) d -> p t d", p=P)).then_inc(s_x, 16)
            for name, ap in (("mix_norm_g", mix_norm_g), ("ffn_norm_g", ffn_norm_g),
                             ("conv_b", conv_b), ("skip_m", skip_m),
                             ("mh_norm_g", mh_norm_g), ("gm_out_g", gm_out_g)):
                r, n = ROWS[name]
                sp.dma_start(prm[r:r + n, :], ap.rearrange("l (k p) -> (l k) p", p=P)).then_inc(s_prm, 16)
            r, n = ROWS["conv_w"]
            sp.dma_start(prm[r:r + n, :], conv_w.rearrange("l j (k p) -> (l j k) p", p=P)).then_inc(s_prm, 16)
            r, n = ROWS["b_sp"]
            sp.dma_start(prm[r:r + n, :], b_sp.rearrange("l g i -> (l g) i")).then_inc(s_prm, 16)
            load_w_in(0, 0)

            def load_mixer_params(l):
                if l:
                    sp.wait_ge(gate_ps, l)
                    sp.wait_ge(vg_r, NT * l)
                    sp.wait_ge(ygT_ps, 2 * l)
                for i, w in enumerate((w_q, w_k, w_v)):
                    sp.dma_start(wqkv[:, i], w[l].rearrange("h d e -> d h e")).then_inc(s_wqkv, 16)
                sp.dma_start(wif[:], w_if[l].rearrange("(c p) g -> p c g", p=P)).then_inc(s_small, 16)
                sp.dma_start(gvb[:], gm_v_g[l:l + 1, :].to_broadcast((P, MW))).then_inc(s_small, 16)
                sp.dma_start(wsp[:], w_sp[l].rearrange("g i j -> i g j")).then_inc(s_wsp, 16)
                if l == 0:
                    sp.dma_start(bif[:], b_if.rearrange("l (a h) -> h l a", h=H),
                                 allow_slow_non_contiguous=True).then_inc(s_small, 16)
                    sp.dma_start(wr[:], moe_router[0].rearrange("(k p) e -> p k e", p=P)).then_inc(s_small, 16)

            load_mixer_params(0)
            for i in range(1, 4):
                load_w_in(0, i)
            load_w_out(0)
            for u in range(ND):
                wd = dense_width(u)
                for a in range(2):
                    n = ring_slot(2 * w13_item(0, MIX + u) + a)
                    for k, w in enumerate((dense_w1, dense_w3)):
                        sp.dma_start(w13[n][:, :, k, 0:wd],
                                     w[0, a * KH * P:(a + 1) * KH * P, u * UF:u * UF + wd]
                                     .rearrange("(k p) f -> p k f", p=P)).then_inc(w13_rdy[n], 16)
            load_mixer_params(1)
            for i in range(4):
                load_w_in(1, i)
            load_w_out(1)

            def load_expert(j, e):
                for c in range(2 * NE):
                    u, a = c // 2, c % 2
                    n = (W13_MOE + c) % R13
                    sp.wait_ge(w13_lo, j * (2 * NE) + (W13_MOE + c - R13 + 1))
                    for k, w in enumerate((moe_w1, moe_w3)):
                        sp.dma_start(w13[n][:, :, k, :],
                                     w[0, bass.ds(e, 1), a * KH * P:(a + 1) * KH * P, u * UF:(u + 1) * UF]
                                     .rearrange("e (k p) f -> p (e k) f", p=P)).then_inc(w13_rdy[n], 16)

            load_expert(0, 0)
            with sp.Fori(1, E) as e:
                load_expert(e, e)
            sp.wait_ge(lg_ps, 1)
            sp.dma_start(fgb, final_norm_g.rearrange("(a d) -> a d", a=1).to_broadcast((P, D))
                         ).then_inc(s_fgb, 16)
            sp.wait_ge(route_r, 1)
            last_step = sp.value_load(last_ij[0:1, 0:1], min_val=E - 1, max_val=NJ - 1)
            with sp.If(last_step >= E):
                with sp.Fori(0, E) as e:
                    load_expert(e + E, e)
            with sp.Else():
                sp.nop()
            for t in range(NT):
                sp.wait_ge(fin_r, t + 1)
                sp.dma_start(out[0, t * P:(t + 1) * P, :], x_sb[:, t, :]).then_inc(s_out, 16)
            sp.wait_ge(s_out, 16 * NT)

        @block.gpsimd
        def _(pool):
            links = [0]

            def link(ins):
                links[0] += 1
                ins.then_inc(pool_chain, 1)
                pool.wait_ge(pool_chain, links[0])

            nc.gpsimd.memset(ident[:], 0.0)
            nc.gpsimd.memset(ones_pp[:], 1.0)
            nc.gpsimd.memset(neg_half[:], -0.5)
            link(nc.gpsimd.memset(sel[:], 0.0))
            nc.gpsimd.affine_select(out=ident[:], in_=ident[:], compare_op=ALU.not_equal, fill=1.0,
                                    base=0, pattern=[[-1, P]], channel_multiplier=1)
            nc.gpsimd.affine_select(out=before[:], in_=ones_pp[:], compare_op=ALU.is_gt, fill=0.0,
                                    base=0, pattern=[[1, P]], channel_multiplier=-1)
            nc.gpsimd.affine_select(out=sel[:], in_=sel[:], compare_op=ALU.not_equal, fill=1.0,
                                    base=0, pattern=[[-1, H], [0, P]], channel_multiplier=1)
            nc.gpsimd.iota(slot_no[:], pattern=[[1, PASS]], base=0,
                           channel_multiplier=0, allow_small_or_imprecise_dtypes=True)
            nc.gpsimd.iota(expert_no[:], pattern=[[0, NT], [1, E]], base=0,
                           channel_multiplier=0, allow_small_or_imprecise_dtypes=True
                           ).then_inc(s_const, 1)

            def rsqrt(n):
                pool.wait_ge(var_r, n + 1)
                nc.gpsimd.tensor_tensor(rstd[:], var[:], neg_half[:, 0:NT], ALU.pow).then_inc(rstd_r, 1)

            def mixer(l):
                rsqrt(2 * l)
                pool.wait_ge(gvar_r, l + 1)
                nc.gpsimd.tensor_tensor(grstd, gvar, neg_half[:, 0:NT], ALU.pow).then_inc(grstd_r, 1)
                pool.wait_ge(s_small, 64 + 32 * l)
                for t in range(NT):
                    pool.wait_ge(vn_r, NT * l + t + 1)
                    nc.gpsimd.tensor_tensor(v_gate[:, t, :], v_gate[:, t, :], gvb[:], ALU.mult
                                            ).then_inc(vg_r, 1)
                pool.wait_ge(qkv_ps, 8 * l + 4)
                for h in range(H):
                    ins = nc.gpsimd.tensor_scalar(xcT[:, h, :], xcT[:, h, :], col("skip_m", l * H + h),
                                                  None, ALU.mult)
                ins.then_inc(skip_r, 1)
                pool.wait_ge(yvar_r, l + 1)
                nc.gpsimd.tensor_tensor(yrstd, yvar, neg_half[:, 0:NT], ALU.pow).then_inc(yrstd_r, 1)
                pool.wait_ge(wexp_r, 2 * (l + 1))
                for b in range(2):
                    d = wS[:, :, 256 * b:256 * b + P]
                    nc.gpsimd.affine_select(out=d, in_=d, compare_op=ALU.is_ge, fill=0.0, base=0,
                                            pattern=[[0, H], [1, P]], channel_multiplier=-1
                                            ).then_inc(wmask_r, 1)
                pool.wait_ge(hvar_r, l + 1)
                nc.gpsimd.tensor_tensor(hrstd, hvar, neg_half[:, 0:NT * H], ALU.pow).then_inc(hrstd_r, 1)

            mixer(0)
            rsqrt(1)

            def w2_slot(m, j=0):
                if m >= R2:
                    pool.wait_ge(w2_lo, j * (2 * NE) + (m - R2 + 1))
                return m % R2

            for m in range(2 * ND):
                n = min(P, DFF - m * P)
                i = w2_slot(m)
                pool.dma_start(w2[i][0:n, :], dense_w2[0, m * P:m * P + n, :]).then_inc(w2_rdy[i], 16)

            def load_w2(j, e, i):
                n = w2_slot(W2_MOE + i, j)
                pool.dma_start(w2[n][:], moe_w2[0, bass.ds(e, 1), i * P:(i + 1) * P, :]
                               .rearrange("a p d -> p (a d)")).then_inc(w2_rdy[n], 16)

            for i in range(R2):
                load_w2(0, 0, i)
            mixer(1)
            pool.wait_ge(num_ps, L * H)
            pool.dma_start(gainb, ffn_norm_g[1:2, :].to_broadcast((P, D))).then_inc(s_gain, 16)
            rsqrt(3)
            pool.wait_ge(s_gain, 16)
            pool.wait_ge(xs_a, 1)
            nc.gpsimd.tensor_tensor(xs[:, 0, :], xs[:, 0, :], gainb, ALU.mult).then_inc(xs_p, 1)
            for i in range(R2, 2 * NE):
                load_w2(0, 0, i)
            with pool.Fori(1, E) as e:
                for i in range(2 * NE):
                    load_w2(e, e, i)
            pool.wait_ge(route_r, 1)
            last_step = pool.value_load(last_ij[0:1, 0:1], min_val=E - 1, max_val=NJ - 1)
            with pool.If(last_step >= E):
                with pool.Fori(0, E) as e:
                    for i in range(2 * NE):
                        load_w2(e + E, e, i)
            with pool.Else():
                pool.nop()
            pool.wait_ge(var_r, 5)
            nc.gpsimd.tensor_tensor(rstd[:], var[:], neg_half[:, 0:NT], ALU.pow).then_inc(rstd_r, 1)

        @block.scalar
        def _(act):
            links = [0]

            def link(ins):
                links[0] += 1
                ins.then_inc(act_chain, 1)
                act.wait_ge(act_chain, links[0])

            def high13(j, n):
                act.wait_ge(w13_rdy[n % R13], j * (32 * 2 * NE // R13) + 32 * (n // R13 + 1))
                act.wait_ge(s13_used, j * (2 * NE) + (n + 1))
                nc.scalar.activation(s13h[:, n % 2], w13_wide[n % R13], ACT.Copy).then_inc(w13_hi, 1)

            def high2(j, m):
                act.wait_ge(w2_rdy[m % R2], j * (16 * 2 * NE // R2) + 16 * (m // R2 + 1))
                act.wait_ge(s2_used, j * (2 * NE) + (m + 1))
                nc.scalar.activation(s2h[:, m % 2], w2[m % R2][:], ACT.Copy).then_inc(w2_hi, 1)

            def norm(n, item):
                if n == 0:
                    act.wait_ge(s_x, 16)
                else:
                    act.wait_ge(x_upd, 4 * n)
                link(nc.scalar.activation(xs[:, 0, :], x_sb[:, 0, :], ACT.Square, accum_out=ss[:, 0:1]))
                nc.scalar.activation(ss[:, 0:1], ss[:, 0:1], ACT.Copy).then_inc(sq_a, 1)
                if n == 0:
                    high13(0, 0)
                    act.wait_ge(s_prmT, 1)
                g, l = ("ffn_norm_g", "mix_norm_g")[n % 2 == 0], n // 2
                for i in range(4):
                    act.wait_ge(hT_ps, 4 * n + i + 1)
                    for k in (2 * i, 2 * i + 1):
                        ins = nc.scalar.activation(hT_h[:, k, :], pb[:, norm_bank(n) + i, 256 * (k % 2):256 * (k % 2) + 256],
                                                   ACT.Copy, scale=col(g, l * KD + k))
                    ins.then_inc(hTh_r, 1)
                if n == 3:
                    nc.scalar.activation(xs[:, 0, :], x_sb[:, 0, :], ACT.Copy, scale=rstd[:, 0:1]).then_inc(xs_a, 1)
                high13(0, item)

            def mixer(l):
                b = 2 * w13_item(l, 0)
                norm(2 * l, b + 1)
                high13(0, b + 2)
                for i in range(2):
                    if i == 0:
                        act.wait_ge(xm_ps, l + 1)
                    else:
                        act.wait_ge(s13_used, done13(b + 1))
                    nc.scalar.activation(xmT[:, 2 * i:2 * i + 2, CW - 1:], pb[:, 4 + i, :]
                                         .rearrange("p (h s) -> p h s", h=2), ACT.Copy).then_inc(xm_sb, 1)
                high13(0, b + 3)
                for h in range(H):
                    if h == 2:
                        high13(0, b + 4)
                    act.wait_ge(conv_r, H * l + h + 1)
                    nc.scalar.activation(xcT[:, h, :], xcT[:, h, :], ACT.Silu).then_inc(xc_r, 1)

                def tokenwise(i, t):
                    if t == 0:
                        act.wait_ge(tok_ps, 3 * l + i)
                    else:
                        act.wait_ge(s13_used, done13(b + 2 * i + 1))

                for t in range(NT):
                    tokenwise(1, t)
                    nc.scalar.activation(v_gate[:, t, :], pb[:, 6 + t, :], ACT.Gelu_apprx_tanh
                                         ).then_inc(gelu_r, 1)
                high13(0, b + 5)
                for i in range(2):
                    act.wait_ge(qkv_ps, 8 * l + 4 + i + 1)
                    nc.scalar.activation(vT[:, 2 * i:2 * i + 2, :], pb[:, 4 + i, :]
                                         .rearrange("p (h s) -> p h s", h=2), ACT.Copy).then_inc(vT_r, 1)
                act.wait_ge(absf_r, l + 1)
                link(nc.scalar.activation(gate_e, gate_e, ACT.Exp, scale=-1.0))
                nc.scalar.activation(gate_e, gate_e, ACT.Ln, bias=1.0).then_inc(ln_r, 1)
                high13(0, b + 6)
                for t in range(NT):
                    tokenwise(2, t)
                    nc.scalar.activation(u_sb[:, t, :], pb[:, t, :], ACT.Gelu_apprx_tanh).then_inc(gelu_r, 1)
                high13(0, b + 7)
                for t in range(NT):
                    act.wait_ge(yg_r, NT * l + t + 1)
                    link(nc.scalar.activation(u_sb[:, t, :], v_gate[:, t, :], ACT.Square,
                                              accum_out=yss[:, t:t + 1]))
                nc.scalar.activation(yss, yss, ACT.Copy).then_inc(yss_r, 1)
                act.wait_ge(aT_ps, l + 1)
                nc.scalar.activation(floorT.rearrange("p h t -> p t h"), pb[:, 5, 400:400 + NT * H]
                                     .rearrange("p (t h) -> p t h", t=NT), ACT.Exp).then_inc(floor_r, 1)
                for i in range(2):
                    act.wait_ge(arg_r, 2 * l + i + 1)
                    nc.scalar.activation(wS[:, 2 * i:2 * i + 2, :], wS[:, 2 * i:2 * i + 2, :], ACT.Exp
                                         ).then_inc(wexp_r, 1)
                act.wait_ge(yrstd_r, l + 1)
                for t in range(NT):
                    nc.scalar.activation(v_gate[:, t, :], v_gate[:, t, :], ACT.Copy,
                                         scale=yrstd[:, t:t + 1]).then_inc(ygs_r, 1)
                high13(0, b + 8)
                for t in range(NT):
                    tokenwise(3, t)
                    nc.scalar.activation(o_sb[:, t, :], pb[:, t, :], ACT.Sigmoid).then_inc(o_r, 1)
                high13(0, b + 9)
                for i in range(2):
                    act.wait_ge(ygT_ps, 2 * l + i + 1)
                    for g in range(2):
                        ins = nc.scalar.activation(yT_h[:, H + 2 * i + g, :], pb[:, i, 256 * g:256 * g + 256],
                                                   ACT.Copy, scale=col("gm_out_g", l * H + 2 * i + g))
                    ins.then_inc(ygTh_r, 1)
                high13(0, b + 10)
                for h in range(H):
                    act.wait_ge(ymT_r, H * l + h + 1)
                    nc.scalar.activation(yT_h[:, h, :], xcT[:, h, :], ACT.Copy).then_inc(ymTh_r, 1)
                high13(0, b + 11)
                high13(0, b + 12)

            mixer(0)
            norm(1, 2 * w13_item(0, MIX) + 1)
            for u in range(ND):
                n = 2 * w13_item(0, MIX + u)
                if u < ND - 1:
                    high13(0, n + 2)
                act.wait_ge(s13_used, done13(n + 1))
                if u >= 1:
                    act.wait_ge(g_r, u)
                p = 2 * (u % 2)
                nc.scalar.activation(d_sil, pb[:, p:p + 2, 0:SEQ], ACT.Silu).then_inc(sil_r, 1)
                if u < ND - 1:
                    high13(0, n + 3)
                act.wait_ge(g_r, u + 1)
                for b in range(2):
                    act.wait_ge(s2_used, 2 * u + b + 1)
                    nc.scalar.activation(gT_h[:, b], d_g[:, b], ACT.Copy).then_inc(gh_r, 1)
                    high2(0, 2 * u + b)
            high13(0, 2 * w13_item(1, 0))
            mixer(1)
            act.wait_ge(s_small, 64)
            nc.scalar.activation(wr_h, wr[:], ACT.Copy).then_inc(wrh_r, 1)
            norm(3, W13_MOE + 1)

            act.wait_ge(gap_r, 1)
            nc.scalar.activation(p1, p1, ACT.Exp).then_inc(gexp_r, 1)

            def gathered_high(j, i):
                act.wait_ge(gx_ps, j * 2 + (i + 1))
                nc.scalar.activation(xsel_h[:, 4 * i:4 * i + 4, :], pb[:, 2 + i, :]
                                     .rearrange("p (k s) -> p k s", k=4), ACT.Copy).then_inc(xh_r, 1)

            gathered_high(0, 0)
            gathered_high(0, 1)
            for t in range(NT):
                ins = nc.scalar.activation(onehotT[:, t], ones_pp[:], ACT.Copy, scale=0.0)
            ins.then_inc(ohT_r, 1)
            for half in range(2):
                nc.scalar.activation(y_h[:, 4 * half:4 * half + 4], ones_pp[:].unsqueeze(1).to_broadcast((P, 4, P)),
                                     ACT.Copy, scale=0.0).then_inc(yh_r, 1)
            act.wait_ge(route_r, 1)
            last_step = act.value_load(last_ij[0:1, 0:1], min_val=E - 1, max_val=NJ - 1)

            def step(j, last):
                nc.scalar.activation(spare[:], ident[0:1, 0:1], ACT.Silu)
                for u in range(NE):
                    if u < NE - 1 or not last:
                        high13(j, W13_MOE + 2 * u + 2)
                    act.wait_ge(s13_used, j * (2 * NE) + done13(W13_MOE + 2 * u + 1))
                    if u >= 2:
                        act.wait_ge(eg_r, j * NE + (u - 1))
                    nc.scalar.activation(m_sil[:, u % 2, :], pb[:, u % 2, 0:UF], ACT.Silu).then_inc(esil_r, 1)
                    if u < NE - 1 or not last:
                        high13(j, W13_MOE + 2 * u + 3)
                    high2(j, W2_MOE + 2 * u)
                    if u < NE - 1:
                        high2(j, W2_MOE + 2 * u + 1)
                    act.wait_ge(egT_ps, j * NE + (u + 1))
                    nc.scalar.activation(gT_h[:, :, 0:PASS], pb[:, 6, 0:2 * PASS].rearrange("p (b s) -> p b s", b=2),
                                         ACT.Copy).then_inc(gTh_r, 1)
                    if u == NE - 1:
                        high2(j, W2_MOE + 2 * u + 1)
                    if u == ONEHOT_AT:
                        act.wait_ge(ohT_ps, j + 1)
                        nc.scalar.activation(onehotT, pb[:, 7, 0:NT * P].rearrange("p (t c) -> p t c", t=NT),
                                             ACT.Copy).then_inc(ohT_r, 1)
                if not last:
                    gathered_high(j + 1, 0)
                    gathered_high(j + 1, 1)
                act.wait_ge(s2_used, j * (2 * NE) + done2(W2_MOE + 2 * NE - 1))
                for half in range(2):
                    nc.scalar.activation(y_h[:, 4 * half:4 * half + 4], pb[:, 4 + half, :]
                                         .rearrange("p (k c) -> p k c", k=4), ACT.Copy).then_inc(yh_r, 1)

            with act.Fori(0, last_step) as j:
                step(j, False)
            step(last_step, True)
            act.wait_ge(x_moe, last_step * NT + (NT + 1))
            link(nc.scalar.activation(xs[:, 0, :], x_sb[:, 0, :], ACT.Square, accum_out=ss[:, 0:1]))
            nc.scalar.activation(ss[:, 0:1], ss[:, 0:1], ACT.Copy).then_inc(sq_a, 1)

        @block.vector
        def _(dve):
            links = [0]

            def link(ins):
                links[0] += 1
                ins.then_inc(dve_chain, 1)
                dve.wait_ge(dve_chain, links[0])

            V = nc.vector

            def variance(n):
                link(V.tensor_tensor_reduce(out=xs[:, 1, :], in0=x_sb[:, 1, :], in1=x_sb[:, 1, :],
                                            scale=1.0, scalar=0.0, op0=ALU.mult, op1=ALU.add,
                                            accum_out=ss[:, 1:2]))
                dve.wait_ge(sq_a, n + 1)
                V.tensor_scalar(var[:], ss[:], 1.0 / D, EPS, ALU.mult, ALU.add).then_inc(var_r, 1)

            def low13(j, n):
                dve.wait_ge(w13_hi, j * (2 * NE) + (n + 1))
                V.tensor_tensor(s13l[:, n % 2], w13_wide[n % R13], s13h[:, n % 2].bitcast(fp32),
                                ALU.subtract).then_inc(w13_lo, 1)

            def low2(j, m):
                dve.wait_ge(w2_hi, j * (2 * NE) + (m + 1))
                V.tensor_tensor(s2l[:, m % 2], w2[m % R2][:], s2h[:, m % 2].bitcast(fp32),
                                ALU.subtract).then_inc(w2_lo, 1)

            def norm(n, item):
                if n == 0:
                    dve.wait_ge(s_x, 16)
                variance(n)
                dve.wait_ge(rstd_r, n + 1)
                for t in range(NT):
                    ins = V.tensor_scalar(diag[:, t, :], ident[:], rstd[:, t:t + 1], None, ALU.mult)
                ins.then_inc(diag_r, 1)
                if n == 0:
                    dve.wait_ge(s_prm_ps, 1)
                    V.tensor_copy(prmT[:], pb[:, 7, 0:NROWS]).then_inc(s_prmT, 1)
                    dve.wait_ge(s_prmT, 1)
                g, l = ("ffn_norm_g", "mix_norm_g")[n % 2 == 0], n // 2
                if n % 2 == 0:
                    low13(0, item - 1)
                for i in range(4):
                    dve.wait_ge(hTh_r, 4 * n + i + 1)
                    for k in (2 * i, 2 * i + 1):
                        V.scalar_tensor_tensor(out=hT_l[:, k, :], in0=pb[:, norm_bank(n) + i, 256 * (k % 2):256 * (k % 2) + 256],
                                               scalar=col(g, l * KD + k), in1=hT_h[:, k, :].bitcast(fp32),
                                               op0=ALU.mult, op1=ALU.subtract).then_inc(hTl_r, 1)
                if item is not None:
                    low13(0, item)

            def mixer(l):
                b = 2 * w13_item(l, 0)
                norm(2 * l, b + 1)
                V.memset(xmT[:, :, 0:CW - 1], 0.0).then_inc(s_pad, 1)
                V.memset(v_tok[:, :, :, DH:DH + 1], 1.0).then_inc(s_vone, 1)
                low13(0, b + 2)
                dve.wait_ge(s_pad, l + 1)
                for h in range(H):
                    dve.wait_ge(xm_sb, 2 * l + h // 2 + 1)
                    tap = lambda j: col("conv_w", (l * CW + j) * H + h)
                    link(V.tensor_scalar(xcT[:, h, :], xmT[:, h, 0:SEQ], tap(0), col("conv_b", l * H + h),
                                         ALU.mult, ALU.add))
                    for j in range(1, CW):
                        ins = V.scalar_tensor_tensor(out=xcT[:, h, :], in0=xmT[:, h, j:j + SEQ],
                                                     scalar=tap(j), in1=xcT[:, h, :],
                                                     op0=ALU.mult, op1=ALU.add)
                        if j < CW - 1:
                            link(ins)
                    ins.then_inc(conv_r, 1)
                    if h == 1:
                        low13(0, b + 3)
                        dve.wait_ge(wspT_ps, l + 1)
                        link(V.tensor_copy(wspT[:], pb[:, 0, :].rearrange("p (g i) -> p g i", g=H)))
                        V.memset(wspT[CHUNK:P, :, 0:CHUNK], 0.0).then_inc(wspT_r, 1)
                low13(0, b + 4)
                for t in range(NT):
                    dve.wait_ge(gelu_r, 4 * l + t + 1)
                    link(V.bn_stats(gstats[:, t, :], v_gate[:, t, :]))
                    link(V.bn_aggr(gmv[:, t, :], gstats[:, t, :]))
                V.tensor_scalar(gvar, gmv[:, :, 1], EPS, None, ALU.add).then_inc(gvar_r, 1)

                def copy_qk(i):
                    dve.wait_ge(qkv_ps, 8 * l + i + 1)
                    V.tensor_copy((qT, kT)[i // 2][:, 2 * (i % 2):2 * (i % 2) + 2, :], pb[:, i, :]
                                  .rearrange("p (h s) -> p h s", h=2)).then_inc(qk_r, 1)

                copy_qk(0)
                copy_qk(1)
                dve.wait_ge(grstd_r, l + 1)
                for t in range(NT):
                    V.tensor_scalar(v_gate[:, t, :], v_gate[:, t, :], gmv[:, t, 0:1], grstd[:, t:t + 1],
                                    ALU.subtract, ALU.mult).then_inc(vn_r, 1)
                copy_qk(2)
                copy_qk(3)
                dve.wait_ge(s_vone, l + 1)
                for t in range(NT):
                    dve.wait_ge(qkv_ps, 8 * l + 6 + t + 1)
                    V.tensor_copy(v_tok[:, t, :, 0:DH], pb[:, 6 + t, :].rearrange("p (h c) -> p h c", h=H)
                                  ).then_inc(vt_r, 1)
                low13(0, b + 5)
                dve.wait_ge(gate_ps, l + 1)
                V.tensor_copy(g_tok, pb[:, 2, 0:NT * 2 * H].rearrange("p (t c) -> p t c", t=NT)
                              ).then_inc(gate_r, 1)
                dve.wait_ge(gateT_ps, l + 1)
                bi, bf = bif[:, l, 0:1], bif[:, l, 1:2]
                link(V.tensor_scalar(run_b, pb[0:H, 3, 256:512], bf, None, ALU.add))
                V.scalar_tensor_tensor(out=gate_e, in0=run_b, scalar=-1.0, in1=run_b,
                                       op0=ALU.mult, op1=ALU.max).then_inc(absf_r, 1)
                link(V.tensor_scalar(lf_min, run_b, 0.0, None, ALU.min))
                dve.wait_ge(ln_r, l + 1)
                link(V.tensor_tensor(gate_e, lf_min, gate_e, ALU.subtract))
                link(V.tensor_tensor_scan(run_b, ones_pp[0:H, 0:1].to_broadcast((H, SEQ)), gate_e, 0.0, ALU.mult, ALU.add))
                link(V.scalar_tensor_tensor(out=a_row, in0=pb[0:H, 3, 0:256], scalar=bi, in1=run_b,
                                            op0=ALU.add, op1=ALU.subtract))
                link(V.tensor_tensor_scan(run_m, a_row, a_row, 0.0, ALU.max, ALU.max))
                V.tensor_scalar(neg_m, run_m, -1.0, None, ALU.mult)
                V.scalar_tensor_tensor(out=neg_stab, in0=run_b, scalar=-1.0, in1=run_m,
                                       op0=ALU.mult, op1=ALU.subtract).then_inc(row_r, 1)
                low13(0, b + 6)
                for t in range(NT):
                    dve.wait_ge(sv_ps, NT * l + t + 1)
                    dve.wait_ge(gelu_r, 4 * l + 4)
                    for g in range(H):
                        c = slice(g * P, (g + 1) * P)
                        ins = V.scalar_tensor_tensor(out=v_gate[:, t, c], in0=pb[:, 6 + t, c],
                                                     scalar=col("b_sp", l * H + g), in1=u_sb[:, t, c],
                                                     op0=ALU.add, op1=ALU.mult)
                    ins.then_inc(yg_r, 1)
                dve.wait_ge(aT_ps, l + 1)
                link(V.tensor_copy(aT, pb[:, 4, 400:400 + NT * H].rearrange("p (t h) -> p t h", t=NT)))
                for i in range(2):
                    dve.wait_ge(mb_ps, 2 * l + i + 1)
                    for h in (2 * i, 2 * i + 1):
                        m = pb[:, 2 + i, 256 * (h % 2):256 * (h % 2) + 256]
                        V.tensor_scalar(wS[:, h, 0:256], m, aT[:, 0, h:h + 1], 0.0, ALU.add, ALU.min)
                        ins = V.tensor_scalar(wS[:, h, 256:384], m[:, P:], aT[:, 1, h:h + 1], 0.0,
                                              ALU.add, ALU.min)
                    ins.then_inc(arg_r, 1)
                low13(0, b + 7)
                dve.wait_ge(yss_r, l + 1)
                V.tensor_scalar(yvar, yss, 1.0 / MW, EPS, ALU.mult, ALU.add).then_inc(yvar_r, 1)
                low13(0, b + 8)
                dve.wait_ge(wmask_r, 2 * (l + 1))
                for h in range(H):
                    dve.wait_ge(sc_ps, H * l + h + 1)
                    V.scalar_tensor_tensor(out=wS[:, h, :], in0=pb[:, 4 + h, 0:384], scalar=SCALE,
                                           in1=wS[:, h, :], op0=ALU.mult, op1=ALU.mult).then_inc(sT_r, 1)
                for g in range(H):
                    dve.wait_ge(ygTh_r, 2 * l + g // 2 + 1)
                    V.scalar_tensor_tensor(out=yT_l[:, H + g, :], in0=pb[:, g // 2, 256 * (g % 2):256 * (g % 2) + 256],
                                           scalar=col("gm_out_g", l * H + g), in1=yT_h[:, H + g, :].bitcast(fp32),
                                           op0=ALU.mult, op1=ALU.subtract).then_inc(ygTl_r, 1)
                low13(0, b + 9)
                dve.wait_ge(num_ps, H * (l + 1))
                dve.wait_ge(floor_r, l + 1)
                nums = pb[:, 4:8, :].rearrange("p h (t c) -> p h t c", t=NT)
                link(V.tensor_copy(rden, nums[:, :, :, DH]))
                link(V.scalar_tensor_tensor(out=den, in0=rden, scalar=-1.0, in1=rden,
                                            op0=ALU.mult, op1=ALU.max))
                link(V.tensor_tensor(den, den, floorT, ALU.max))
                link(V.reciprocal(rden, den))
                dve.wait_ge(o_r, NT * (l + 1))
                for h in range(H):
                    for t in range(NT):
                        ins = V.scalar_tensor_tensor(out=hm[:, t, h * DH:(h + 1) * DH],
                                                     in0=nums[:, h, t, 0:DH], scalar=rden[:, h, t:t + 1],
                                                     in1=o_sb[:, t, h * DH:(h + 1) * DH],
                                                     op0=ALU.mult, op1=ALU.mult)
                link(ins)
                for h in range(H):
                    for t in range(NT):
                        ins = V.bn_stats(stats[:, h, t, :], hm[:, t, h * DH:(h + 1) * DH])
                link(ins)
                for h in range(H):
                    for t in range(NT):
                        ins = V.bn_aggr(mv[:, h, t, :], stats[:, h, t, :])
                link(ins)
                V.tensor_scalar(hvar, mv.rearrange("p h t c -> p (h t) c")[:, :, 1], EPS, None, ALU.add
                                ).then_inc(hvar_r, 1)
                low13(0, b + 10)
                dve.wait_ge(hrstd_r, l + 1)
                for h in range(H):
                    for t in range(NT):
                        c = slice(h * DH, (h + 1) * DH)
                        ins = V.tensor_scalar(hm[:, t, c], hm[:, t, c], mv[:, h, t, 0:1],
                                              hrstd[:, h * NT + t:h * NT + t + 1], ALU.subtract, ALU.mult)
                    ins.then_inc(hm_r, 1)
                dve.wait_ge(skip_r, l + 1)
                def head_low(h):
                    dve.wait_ge(ymTh_r, H * l + h + 1)
                    V.tensor_tensor(yT_l[:, h, :], xcT[:, h, :], yT_h[:, h, :].bitcast(fp32), ALU.subtract
                                    ).then_inc(ymTl_r, 1)

                for h in range(H):
                    dve.wait_ge(hmT_ps, 2 * l + h // 2 + 1)
                    V.scalar_tensor_tensor(out=xcT[:, h, :], in0=pb[:, 4 + h // 2, 256 * (h % 2):256 * (h % 2) + 256],
                                           scalar=col("mh_norm_g", l * H + h), in1=xcT[:, h, :],
                                           op0=ALU.mult, op1=ALU.add).then_inc(ymT_r, 1)
                    if h >= 1:
                        head_low(h - 1)
                head_low(H - 1)
                low13(0, b + 11)
                for half in range(2):
                    for t in range(NT):
                        if t == 0:
                            dve.wait_ge(wo_ps, 2 * l + half + 1)
                        else:
                            dve.wait_ge(s13_used, done13(b + 10 + half))
                        add_to_x(half, t, half * 2 + t)
                    if half == 0:
                        low13(0, b + 12)
                dve.wait_ge(x_upd, 4 * (2 * l + 1))

            def add_to_x(half, t, bank):
                c = slice(half * 512, half * 512 + 512)
                V.tensor_tensor(x_sb[:, t, c], x_sb[:, t, c], pb[:, bank, :], ALU.add).then_inc(x_upd, 1)

            mixer(0)
            norm(1, 2 * w13_item(0, MIX) + 1)
            for u in range(ND):
                n = 2 * w13_item(0, MIX + u)
                if u < ND - 1:
                    low13(0, n + 2)
                dve.wait_ge(sil_r, u + 1)
                if u >= 1:
                    dve.wait_ge(gl_r, 2 * u)
                p = 2 * (u % 2)
                V.tensor_tensor(d_g, d_sil, pb[:, p:p + 2, SEQ:2 * SEQ], ALU.mult).then_inc(g_r, 1)
                if u < ND - 1:
                    low13(0, n + 3)
                for b in range(2):
                    dve.wait_ge(gh_r, 2 * u + b + 1)
                    V.tensor_tensor(gT_l[:, b], d_g[:, b], gT_h[:, b].bitcast(fp32), ALU.subtract).then_inc(gl_r, 1)
                    low2(0, 2 * u + b)
            for i in range(4):
                if i < 3:
                    dve.wait_ge(down_ps, i + 1)
                else:
                    dve.wait_ge(s2_used, done2(2 * ND - 1))
                add_to_x(i // 2, i % 2, 4 + i)
            dve.wait_ge(x_upd, 8)
            mixer(1)
            dve.wait_ge(wrh_r, 1)
            V.tensor_tensor(wr_l, wr[:], wr_h.bitcast(fp32), ALU.subtract).then_inc(wrl_r, 1)
            norm(3, None)
            dve.wait_ge(s_gain, 16)
            V.scalar_tensor_tensor(out=xs[:, 1, :], in0=x_sb[:, 1, :], scalar=rstd[:, 1:2], in1=gainb,
                                   op0=ALU.mult, op1=ALU.mult).then_inc(xs_d, 1)

            dve.wait_ge(lgT_ps, 1)
            V.tensor_copy(logitsT, pb[0:E, 4, 0:SEQ]).then_inc(lgT_r, 1)
            dve.wait_ge(lg_ps, 1)
            link(V.tensor_copy(logits, pb[:, 6, 0:NT * E].rearrange("p (t e) -> p t e", t=NT)))
            for t in range(NT):
                ins = V.max(top[:, t, :], logits[:, t, :])
            link(ins)
            for t in range(NT):
                ins = V.max_index(top_i[:, t, :], top[:, t, :], logits[:, t, :])
            link(ins)
            link(V.tensor_copy(top_fi, top_i[:]))
            for t in range(NT):
                V.tensor_scalar(oh0[:, t, :], expert_no[:, t, :], top_fi[:, t, 0:1], None, ALU.is_equal)
                ins = V.tensor_scalar(oh1[:, t, :], expert_no[:, t, :], top_fi[:, t, 1:2], None, ALU.is_equal)
            link(ins)
            V.tensor_tensor(picked, oh0, oh1, ALU.add).then_inc(pick_r, 1)
            V.tensor_tensor(p1, top[:, :, 1], top[:, :, 0], ALU.subtract).then_inc(gap_r, 1)
            dve.wait_ge(rank_ps, 1)
            link(V.scalar_tensor_tensor(out=rank, in0=pb[:, 5, 0:NT * E].rearrange("p (t e) -> p t e", t=NT),
                                        scalar=1.0, in1=picked, op0=ALU.add, op1=ALU.mult))
            for p in range(NJ // E):
                js = slice(p * E, (p + 1) * E)
                ins = V.tensor_scalar(slot_of[:, js, :].rearrange("p e t -> p t e"), rank, -1.0 - p * PASS,
                                      None, ALU.add)
            link(ins)

            def make_onehot(j):
                for t in range(NT):
                    slots = slot_of[:, j, t:t + 1] if isinstance(j, int) else slot_of[:, bass.ds(j, 1), t]
                    ins = V.tensor_scalar(onehot[:, t], slot_no[:], slots, None, ALU.is_equal)
                ins.then_inc(oh_r, 1)

            make_onehot(0)
            link(V.reduce_max(last_f[0:1, 0:1], pb[0:1, 5, 32:32 + E], AX.X))
            link(V.tensor_scalar(last_f[0:1, 1:2], last_f[0:1, 0:1], float(PASS), float(E), ALU.is_gt, ALU.mult))
            link(V.tensor_scalar(last_f[0:1, 1:2], last_f[0:1, 1:2], float(E - 1), None, ALU.add))
            V.tensor_copy(last_ij[:], last_f[0:1, 1:2]).then_inc(route_r, 1)
            dve.wait_ge(gexp_r, 1)
            link(V.tensor_scalar(pden, p1, 1.0, None, ALU.add))
            link(V.reciprocal(p0, pden))
            link(V.tensor_tensor(p1, p1, p0, ALU.mult))
            for t in range(NT):
                link(V.tensor_scalar(oh0[:, t, :], oh0[:, t, :], p0[:, t:t + 1], None, ALU.mult))
                link(V.scalar_tensor_tensor(out=weight[:, t, :], in0=oh1[:, t, :], scalar=p1[:, t:t + 1],
                                            in1=oh0[:, t, :], op0=ALU.mult, op1=ALU.add))
            V.memset(comb[:, 0, :], 0.0)
            for p in range(NJ // E):
                js = slice(1 + p * E, 1 + (p + 1) * E)
                ins = V.tensor_copy(comb[:, js, :].rearrange("p e t -> p t e"), weight)
            link(ins)
            low13(0, W13_MOE + 1)
            dve.wait_ge(route_r, 1)

            last_step = dve.value_load(last_ij[0:1, 0:1], min_val=E - 1, max_val=NJ - 1)

            def gathered(j):
                for i in range(2):
                    dve.wait_ge(xh_r, j * 2 + (i + 1))
                    ks = slice(4 * i, 4 * i + 4)
                    V.tensor_tensor(xsel_l[:, ks, :], pb[:, 2 + i, :].rearrange("p (k s) -> p k s", k=4),
                                    xsel_h[:, ks, :].bitcast(fp32), ALU.subtract).then_inc(xsel_r, 1)

            def add_scattered(j, t, bank=2):
                dve.wait_ge(sct_ps, j * NT + (t + 1))
                for half in range(2):
                    c = slice(half * 512, half * 512 + 512)
                    ins = V.scalar_tensor_tensor(out=x_sb[:, t, c], in0=pb[:, bank + half, :],
                                                 scalar=comb[:, bass.ds(j, 1), t], in1=x_sb[:, t, c],
                                                 op0=ALU.mult, op1=ALU.add)
                ins.then_inc(x_moe, 1)

            gathered(0)
            dve.wait_ge(yh_r, 2)
            V.tensor_tensor(y_l, y_h.bitcast(fp32), y_h.bitcast(fp32), ALU.subtract).then_inc(yl_r, 1)

            def step(j, last):
                for u in range(NE):
                    if u < NE - 1 or not last:
                        low13(j, W13_MOE + 2 * u + 2)
                    dve.wait_ge(esil_r, j * NE + (u + 1))
                    if u >= 2:
                        dve.wait_ge(egT_ps, j * NE + (u - 1))
                    V.tensor_tensor(m_g[:, u % 2, :], m_sil[:, u % 2, :], pb[:, u % 2, UF:2 * UF], ALU.mult
                                    ).then_inc(eg_r, 1)
                    if u < NE - 1 or not last:
                        low13(j, W13_MOE + 2 * u + 3)
                    low2(j, W2_MOE + 2 * u)
                    if u < NE - 1:
                        low2(j, W2_MOE + 2 * u + 1)
                    dve.wait_ge(gTh_r, j * NE + (u + 1))
                    V.tensor_tensor(gT_l[:, :, 0:PASS], pb[:, 6, 0:2 * PASS].rearrange("p (b s) -> p b s", b=2),
                                    gT_h[:, :, 0:PASS].bitcast(fp32), ALU.subtract).then_inc(egT_r, 1)
                    if u == NE - 1:
                        low2(j, W2_MOE + 2 * u + 1)
                    if u < NT:
                        add_scattered(j, u)
                    if u == NE // 2 and not last:
                        dve.wait_ge(ohT_ps, j + 1)
                        make_onehot(j + 1)
                if not last:
                    gathered(j + 1)
                for half in range(2):
                    dve.wait_ge(yh_r, j * 2 + (half + 3))
                    ks = slice(4 * half, 4 * half + 4)
                    ins = V.tensor_tensor(y_l[:, ks], pb[:, 4 + half, :].rearrange("p (k c) -> p k c", k=4),
                                          y_h[:, ks].bitcast(fp32), ALU.subtract)
                ins.then_inc(yl_r, 1)

            with dve.Fori(0, last_step) as j:
                step(j, False)
            step(last_step, True)
            for t in range(NT):
                add_scattered(last_step + 1, t, bank=(2, 6)[t])
            dve.wait_ge(x_moe, last_step * NT + 2 * NT)
            variance(4)
            dve.wait_ge(rstd_r, 5)
            dve.wait_ge(s_fgb, 16)
            for t in range(NT):
                V.scalar_tensor_tensor(out=x_sb[:, t, :], in0=x_sb[:, t, :], scalar=rstd[:, t:t + 1],
                                       in1=fgb, op0=ALU.mult, op1=ALU.mult).then_inc(fin_r, 1)

        @block.tensor
        def _(pe):
            mm = nc.tensor.matmul

            pe.sem_inc(s13_used, 2)
            pe.sem_inc(s2_used, 2)

            def parts13(n):
                pe.wait_ge(w13_lo, n + 1)
                return s13h[:, n % 2], s13l[:, n % 2]

            def mm3(out, x, w, start, stop):
                for i, (a, b) in enumerate(((0, 0), (0, 1), (1, 0))):
                    ins = mm(out, x[a], w[b], start=start and i == 0, stop=stop and i == 2)
                return ins

            def norm(n):
                pe.wait_ge(diag_r, n + 1)
                for k in range(KD):
                    for t in range(NT):
                        ins = mm(pb[:, norm_bank(n) + k // 2, 256 * (k % 2) + P * t:256 * (k % 2) + P * t + P],
                                 x_sb[:, t, k * P:(k + 1) * P], diag[:, t, :], start=True, stop=True)
                    if k % 2:
                        ins.then_inc(hT_ps, 1)

            def hT_parts(k, t=None):
                c = slice(0, SEQ) if t is None else slice(t * P, (t + 1) * P)
                return hT_h[:, k, c], hT_l[:, k, c]

            def mixer(l):
                b = 2 * w13_item(l, 0)
                norm(2 * l)
                for a in range(2):
                    w = parts13(b + a)
                    for h in range(H):
                        for k in range(KH * a, KH * a + KH):
                            if h == 0:
                                pe.wait_ge(hTl_r, KD * 2 * l + k + 1)
                            ins = mm3(pb[:, 4 + h // 2, 256 * (h % 2):256 * (h % 2) + 256],
                                      [p[:, k % KH, h * P:(h + 1) * P] for p in w], hT_parts(k),
                                      start=k == 0 and h % 2 == 0, stop=k == KD - 1 and h % 2 == 1)
                        if a == 1 and h == 1:
                            ins.then_inc(xm_ps, 1)
                    ins.then_inc(s13_used, 1)

                def tokenwise(i, a, t, bank):
                    w = parts13(b + 2 * i + a)
                    for k in range(KH * a, KH * a + KH):
                        ins = mm3(bank, hT_parts(k, t), [p[:, k % KH, :] for p in w],
                                  start=k == 0, stop=k == KD - 1)
                    if t == NT - 1:
                        ins.then_inc(s13_used, 1)
                    elif a == 1:
                        ins.then_inc(tok_ps, 1)

                pe.wait_ge(s_wsp, 16 * (l + 1))
                for g in range(H):
                    ins = nc.tensor.transpose(pb[:, 0, g * P:(g + 1) * P], wsp[:, g, :], ident[:])
                ins.then_inc(wspT_ps, 1)
                for a in range(2):
                    for t in range(NT):
                        tokenwise(1, a, t, pb[:, 6 + t, :])
                pe.wait_ge(s_wqkv, 48 * (l + 1))
                pe.wait_ge(xm_sb, 2 * (l + 1))
                pe.wait_ge(wspT_r, l + 1)
                for i in range(3):
                    for h in range(H):
                        if i == 0:
                            pe.wait_ge(xc_r, H * l + h + 1)
                        src = xmT[:, h, CW - 1:] if i == 2 else xcT[:, h, :]
                        ins = mm(pb[:, 2 * i + h // 2, 256 * (h % 2):256 * (h % 2) + 256],
                                 wqkv[:, i, h, :], src, start=True, stop=True)
                        if h % 2:
                            ins.then_inc(qkv_ps, 1)
                for t in range(NT):
                    pe.wait_ge(gelu_r, 4 * l + t + 1)
                    for h in range(H):
                        ins = mm(pb[:, 6 + t, h * DH:(h + 1) * DH],
                                 xmT[:, h, CW - 1 + t * P:CW - 1 + (t + 1) * P], wqkv[:, 2, h, :],
                                 start=True, stop=True)
                    ins.then_inc(qkv_ps, 1)
                pe.wait_ge(qk_r, 4 * (l + 1))
                pe.wait_ge(vT_r, 2 * (l + 1))
                pe.wait_ge(s_small, 64 + 32 * l)
                for t in range(NT):
                    for c in range(3 * H):
                        src = (qT, kT, vT)[c // H][:, c % H, t * P:(t + 1) * P]
                        ins = mm(pb[:, 2, t * 2 * H:(t + 1) * 2 * H], src, wif[:, c, :],
                                 start=c == 0, stop=c == 3 * H - 1)
                ins.then_inc(gate_ps, 1)
                tokenwise(2, 0, 0, pb[:, 0, :])
                pe.wait_ge(gate_r, l + 1)
                for t in range(NT):
                    for f in range(2):
                        ins = nc.tensor.transpose(pb[0:H, 3, 256 * f + t * P:256 * f + (t + 1) * P],
                                                  g_tok[:, t, f * H:(f + 1) * H], ident[:])
                ins.then_inc(gateT_ps, 1)
                tokenwise(2, 0, 1, pb[:, 1, :])
                tokenwise(2, 1, 0, pb[:, 0, :])
                tokenwise(2, 1, 1, pb[:, 1, :])
                for t in range(NT):
                    pe.wait_ge(vt_r, NT * l + t + 1)
                    pe.wait_ge(vg_r, NT * l + t + 1)
                    for g in range(H):
                        ins = mm(pb[:, 6 + t, g * P:(g + 1) * P], wspT[:, g, :],
                                 v_gate[:, t, g * P:(g + 1) * P], start=True, stop=True)
                    ins.then_inc(sv_ps, 1)
                pe.wait_ge(row_r, l + 1)
                for i, r in enumerate((a_row, neg_stab)):
                    for t in range(NT):
                        ins = nc.tensor.transpose(pb[:, 4 + i, 400 + t * H:400 + (t + 1) * H],
                                                  r[:, t * P:(t + 1) * P], ident[0:H, 0:H])
                ins.then_inc(aT_ps, 1)
                for h in range(H):
                    ins = mm(pb[:, 2 + h // 2, 256 * (h % 2):256 * (h % 2) + 256], sel[:, h, :], neg_m,
                             start=True, stop=True)
                    if h % 2:
                        ins.then_inc(mb_ps, 1)
                for a in range(2):
                    for t in range(NT):
                        if a == 0:
                            pe.wait_ge(gelu_r, 4 * l + 2 + t + 1)
                        tokenwise(3, a, t, pb[:, t, :])
                pe.wait_ge(arg_r, 2 * (l + 1))
                pe.wait_ge(floor_r, l + 1)
                pe.wait_ge(yg_r, NT * (l + 1))
                for h in range(H):
                    mm(pb[:, 4 + h, 0:256], kT[:, h, 0:P], qT[:, h, :], start=True, stop=True)
                    mm(pb[:, 4 + h, 256:384], kT[:, h, P:], qT[:, h, P:], start=True, stop=True).then_inc(sc_ps, 1)
                pe.wait_ge(ygs_r, NT * (l + 1))
                pe.wait_ge(o_r, NT * (l + 1))
                for g in range(H):
                    for t in range(NT):
                        ins = nc.tensor.transpose(pb[:, g // 2, 256 * (g % 2) + P * t:256 * (g % 2) + P * t + P],
                                                  v_gate[:, t, g * P:(g + 1) * P], ident[:])
                    if g % 2:
                        ins.then_inc(ygT_ps, 1)
                for h in range(H):
                    pe.wait_ge(sT_r, H * l + h + 1)
                    n0, n1 = pb[:, 4 + h, 0:DH + 1], pb[:, 4 + h, 256:256 + DH + 1]
                    mm(n0, wS[:, h, 0:P], v_tok[:, 0, h, :], start=True, stop=True)
                    mm(n1, wS[:, h, P:2 * P], v_tok[:, 0, h, :], start=True, stop=False)
                    mm(n1, wS[:, h, 2 * P:3 * P], v_tok[:, 1, h, :], start=False, stop=True).then_inc(num_ps, 1)

                def output_product(i, half, t):
                    w = parts13(b + 8 + 2 * i + half)
                    for k in range(KH):
                        c = (1 - i) * KH + k
                        if i == 1 and half == 0 and t == 0:
                            pe.wait_ge(ymTl_r, H * l + k + 1)
                        y = yT_h[:, c, t * P:(t + 1) * P], yT_l[:, c, t * P:(t + 1) * P]
                        ins = mm3(pb[:, 2 * half + t, :], y, [p[:, k, :] for p in w],
                                  start=i == 0 and k == 0, stop=i == 1 and k == KH - 1)
                    if t == NT - 1:
                        ins.then_inc(s13_used, 1)
                    elif i == 1:
                        ins.then_inc(wo_ps, 1)

                pe.wait_ge(ygTl_r, H * (l + 1))
                for half in range(2):
                    for t in range(NT):
                        output_product(0, half, t)
                for h in range(H):
                    pe.wait_ge(hm_r, H * l + h + 1)
                    for t in range(NT):
                        ins = nc.tensor.transpose(pb[:, 4 + h // 2, 256 * (h % 2) + P * t:256 * (h % 2) + P * t + P],
                                                  hm[:, t, h * DH:(h + 1) * DH], ident[:])
                    if h % 2:
                        ins.then_inc(hmT_ps, 1)
                for half in range(2):
                    for t in range(NT):
                        output_product(1, half, t)

            pe.wait_ge(s_const, 1)
            pe.wait_ge(s_prm, 16 * 8)
            nc.tensor.transpose(pb[:, 7, 0:NROWS], prm[:], ident[0:NROWS, 0:NROWS]).then_inc(s_prm_ps, 1)

            mixer(0)

            norm(1)

            def dense_blocks(u):
                return [(b, min(P, dense_width(u) - b * P)) for b in range(2)]

            def dense_down(u):
                for b, r in dense_blocks(u):
                    pe.wait_ge(w2_lo, 2 * u + b + 1)
                    pe.wait_ge(gl_r, 2 * u + b + 1)
                    last = u == ND - 1 and b == 1
                    for half in range(2):
                        c = slice(half * 512, half * 512 + 512)
                        for t in range(NT):
                            ts = slice(t * P, (t + 1) * P)
                            ins = mm3(pb[:, 4 + 2 * half + t, :], (gT_h[0:r, b, ts], gT_l[0:r, b, ts]),
                                      (s2h[0:r, b, c], s2l[0:r, b, c]), start=u == 0 and b == 0, stop=last)
                            if last and not (half and t):
                                ins.then_inc(down_ps, 1)
                    ins.then_inc(s2_used, 1)

            for u in range(ND):
                if u >= 2:
                    pe.wait_ge(g_r, u - 1)
                for a in range(2):
                    w = parts13(2 * w13_item(0, MIX + u) + a)
                    for b, r in dense_blocks(u):
                        for k2 in range(2):
                            for k in range(KH * a, KH * a + KH):
                                if u == 0 and b == 0 and k2 == 0:
                                    pe.wait_ge(hTl_r, KD + k + 1)
                                c = k2 * UF + b * P
                                ins = mm3(pb[0:r, 2 * (u % 2) + b, k2 * SEQ:(k2 + 1) * SEQ],
                                          [p[:, k % KH, c:c + r] for p in w], hT_parts(k),
                                          start=k == 0 and k2 == 0, stop=k == KD - 1 and k2 == 1)
                    ins.then_inc(s13_used, 1)
                if u >= 1:
                    dense_down(u - 1)
            dense_down(ND - 1)

            mixer(1)

            norm(3)
            pe.wait_ge(wrl_r, 1)
            for k in range(KD):
                pe.wait_ge(hTl_r, KD * 3 + k + 1)
                ins = mm3(pb[0:E, 4, 0:SEQ], (wr_h[:, k, :], wr_l[:, k, :]), hT_parts(k),
                          start=k == 0, stop=k == KD - 1)
            ins.then_inc(lgT_ps, 1)
            pe.wait_ge(lgT_r, 1)
            for t in range(NT):
                ins = nc.tensor.transpose(pb[:, 6, t * E:(t + 1) * E], logitsT[:, t * P:(t + 1) * P],
                                          ident[0:E, 0:E])
            ins.then_inc(lg_ps, 1)
            pe.wait_ge(pick_r, 1)
            mm(pb[:, 5, 0:E], before[:], picked[:, 0, :], start=True, stop=True)
            mm(pb[:, 5, E:2 * E], ones_pp[:], picked[:, 0, :], start=True, stop=False)
            mm(pb[:, 5, E:2 * E], before[:], picked[:, 1, :], start=False, stop=True)
            for t in range(NT):
                ins = mm(pb[0:1, 5, 32:32 + E], ones_pp[:, 0:1], picked[:, t, :], start=t == 0, stop=t == NT - 1)
            ins.then_inc(rank_ps, 1)

            def gather(j):
                pe.wait_ge(oh_r, j + 1)
                for i in range(2):
                    for k in range(4 * i, 4 * i + 4):
                        for t in range(NT):
                            ins = mm(pb[:, 2 + i, (k % 4) * PASS:(k % 4 + 1) * PASS],
                                     xs[:, t, k * P:(k + 1) * P], onehot[:, t, :],
                                     start=t == 0, stop=t == NT - 1)
                    ins.then_inc(gx_ps, 1)

            def scatter(j, t, bank=2):
                if t == 0:
                    pe.wait_ge(yl_r, j + 1)
                    pe.wait_ge(ohT_r, j + 1)
                elif bank == 2:
                    pe.wait_ge(x_moe, j * NT + t)
                for half in range(2):
                    for i, y in enumerate((y_h, y_l)):
                        ins = mm(pb[:, bank + half, :], onehotT[:, t, :], y[:, 4 * half:4 * half + 4],
                                 start=i == 0, stop=i == 1)
                ins.then_inc(sct_ps, 1)

            pe.wait_ge(xs_p, 1)
            pe.wait_ge(xs_d, 1)
            gather(0)
            pe.wait_ge(route_r, 1)
            last_step = pe.value_load(last_ij[0:1, 0:1], min_val=E - 1, max_val=NJ - 1)

            def step(j, last):
                def up(c):
                    pe.wait_ge(w13_lo, j * (2 * NE) + (W13_MOE + c + 1))
                    u = c // 2
                    if c < 2:
                        pe.wait_ge(xsel_r, j * 2 + (c + 1))
                    if u >= 2 and c % 2 == 0:
                        pe.wait_ge(eg_r, j * NE + (u - 1))
                    for k in range(KH):
                        x = KH * (c % 2) + k
                        for i, (a, w) in enumerate(((xsel_h, s13h), (xsel_h, s13l), (xsel_l, s13h))):
                            ins = mm(pb[:, u % 2, :], a[:, x, :], w[:, c % 2, k, :],
                                     start=x == 0 and i == 0, stop=x == KD - 1 and i == 2)
                    ins.then_inc(s13_used, 1)

                def turn(u):
                    pe.wait_ge(eg_r, j * NE + (u + 1))
                    for b in range(2):
                        ins = nc.tensor.transpose(pb[:, 6, b * P:(b + 1) * P],
                                                  m_g[:, u % 2, b * P:(b + 1) * P], ident[:])
                    ins.then_inc(egT_ps, 1)

                def down(u):
                    pe.wait_ge(egT_r, j * NE + (u + 1))
                    for b in range(2):
                        pe.wait_ge(w2_lo, j * (2 * NE) + (W2_MOE + 2 * u + b + 1))
                        for i, (a, w) in enumerate(((gT_h, s2h), (gT_h, s2l), (gT_l, s2h))):
                            for half in range(2):
                                ins = mm(pb[:, 4 + half, :], a[:, b, 0:PASS], w[:, b, half * 512:(half + 1) * 512],
                                         start=u == 0 and b == 0 and i == 0,
                                         stop=u == NE - 1 and b == 1 and i == 2)
                        ins.then_inc(s2_used, 1)

                up(0)
                up(1)
                scatter(j, 0)
                for u in range(1, NE):
                    turn(u - 1)
                    up(2 * u)
                    up(2 * u + 1)
                    if u == 1:
                        scatter(j, 1)
                    if u == ONEHOT_AT:
                        for t in range(NT):
                            ins = nc.tensor.transpose(pb[:, 7, t * P:(t + 1) * P], onehot[:, t, :], ident[:])
                        ins.then_inc(ohT_ps, 1)
                    down(u - 1)
                turn(NE - 1)
                if not last:
                    pe.wait_ge(x_moe, j * NT + NT)
                    gather(j + 1)
                down(NE - 1)

            with pe.Fori(0, last_step) as j:
                step(j, False)
            step(last_step, True)
            scatter(last_step + 1, 0)
            scatter(last_step + 1, 1, bank=6)


_INS = ["x", "mix_norm_g", "w_in", "conv_w", "conv_b", "w_q", "w_k", "w_v", "w_if", "b_if", "skip_m",
        "mh_norm_g", "gm_v_g", "w_sp", "b_sp", "gm_out_g", "w_out", "ffn_norm_g",
        "dense_w1", "dense_w3", "dense_w2", "moe_router", "moe_w1", "moe_w3", "moe_w2", "final_norm_g"]


def kernel(**inputs):
    import numpy as _np
    import concourse.bacc as _bacc
    from concourse.bass_utils import run_bass_kernel_spmd as _run

    nc = _bacc.Bacc("TRN2", target_bir_lowering=False, num_devices=1)
    arrays, args = {}, []
    for name in _INS:
        a = _np.ascontiguousarray(inputs[name])
        arrays[f"in_{name}"] = a
        args.append(nc.dram_tensor(f"in_{name}", a.shape, mybir.dt.from_np(a.dtype), kind="ExternalInput").ap())
    args.append(nc.dram_tensor("out_0", (1, SEQ, D), fp32, kind="ExternalOutput").ap())
    trunk(nc, *args)
    r = _run(nc, [arrays], core_ids=[0])
    return r.results[0]["out_0"]
```
